# Optimizing a Trainium2 kernel written in Bass

```python
import jax, jax.numpy as jnp
from jax import lax
import numpy as np

D_MODEL = 1024
BATCH = 1
SEQ = 512
DEPTH = 2

GRID_W = 64
CTX_LEN = 256
N_MIXERS = 2
N_RET = (DEPTH + 1) // 2
N_MLA = DEPTH // 2
EPS = 1e-6
ROPE_BASE = 10000.0
RET_HEADS = 4
RET_DK = D_MODEL // RET_HEADS
RET_DV = 2 * RET_DK
RET_VW = RET_HEADS * RET_DV
RET_CHUNK = 128
RET_IN = 2 * D_MODEL + 3 * RET_VW
MLA_HEADS = 8
MLA_NOPE = 128
MLA_ROPE = 64
MLA_QK = MLA_NOPE + MLA_ROPE
MLA_V = 128
MLA_Q_RANK = 384
MLA_KV_RANK = 256
MLA_IN = MLA_Q_RANK + MLA_KV_RANK + MLA_ROPE
ATTN_BLOCK = 128
N_EXPERTS = 64
TOP_K = 8
N_GROUPS = 8
TOPK_GROUPS = 4
EXPERT_FF = 256
SHARED_FF = 256
ROUTED_SCALE = 2.5

kernel_name = 'hybrid_retention_mla_moe_dit'

def rms_scale(x):
    xf = x.astype(jnp.float32)
    return (xf * lax.rsqrt(jnp.mean(xf * xf, axis=-1, keepdims=True) + EPS)).astype(x.dtype)

def rmsnorm(x, g):
    return rms_scale(x) * g

def modulate(h, shift, scale):
    return h * (1 + scale) + shift

def axial_angles(rows_n, rot_dim):
    axis_dim = rot_dim // 2
    inv = ROPE_BASE ** (-jnp.arange(0, axis_dim, 2, dtype=jnp.float32) / axis_dim)
    row = jnp.repeat(jnp.arange(rows_n, dtype=jnp.float32), GRID_W)
    col = jnp.tile(jnp.arange(GRID_W, dtype=jnp.float32), rows_n)
    return row[:, None] * inv, col[:, None] * inv

def rotate_half(x, ang):
    x1, x2 = jnp.split(x, 2, axis=-1)
    cos = jnp.cos(ang)[None, :, None, :].astype(x.dtype)
    sin = jnp.sin(ang)[None, :, None, :].astype(x.dtype)
    return jnp.concatenate([x1 * cos - x2 * sin, x2 * cos + x1 * sin], axis=-1)

def axial_rope(x, ang_r, ang_c):
    xr, xc = jnp.split(x, 2, axis=-1)
    return jnp.concatenate([rotate_half(xr, ang_r), rotate_half(xc, ang_c)], axis=-1)

def retention_scan(q, k, v, log_gamma, s0):
    b, L, H, _ = q.shape
    dv = v.shape[-1]
    nc = L // RET_CHUNK

    def chunks(t):
        return t.reshape(b, nc, RET_CHUNK, H, t.shape[-1]).transpose(1, 0, 2, 3, 4)

    idx = jnp.arange(RET_CHUNK, dtype=jnp.float32)
    rel = idx[:, None] - idx[None, :]
    lg = log_gamma.astype(jnp.float32)
    intra = jnp.where(rel[None] >= 0, jnp.exp(lg[:, None, None] * jnp.maximum(rel, 0.0)[None]), 0.0).astype(q.dtype)
    dec_q = jnp.exp(lg[:, None] * (idx + 1)[None]).T[None, :, :, None].astype(q.dtype)
    dec_k = jnp.exp(lg[:, None] * (RET_CHUNK - 1 - idx)[None]).T[None, :, :, None].astype(q.dtype)
    dec_chunk = jnp.exp(lg * RET_CHUNK)[None, :, None, None].astype(q.dtype)

    def step(S, qkv):
        qc, kc, vc = qkv
        scores = jnp.einsum('bihd,bjhd->bhij', qc, kc) * intra
        y = jnp.einsum('bhij,bjhv->bihv', scores, vc) + jnp.einsum('bihd,bhdv->bihv', qc, S) * dec_q
        S = S * dec_chunk + jnp.einsum('bjhd,bjhv->bhdv', kc * dec_k, vc)
        return S, y

    S, ys = lax.scan(step, s0, (chunks(q), chunks(k), chunks(v)))
    return ys.transpose(1, 0, 2, 3, 4).reshape(b, L, H, dv), S

def bidir_retention(q, k, v, lg_f, lg_b, s0_f, s0_b):
    y_f, s_f = retention_scan(q, k, v, lg_f, s0_f)
    y_b, s_b = retention_scan(q[:, ::-1], k[:, ::-1], v[:, ::-1], lg_b, s0_b)
    return y_f, y_b[:, ::-1], s_f, s_b

def retention_mixer(h_lat, h_ctx, w_in, decay_f, decay_b, w_o, ang_r, ang_c, need_ctx_out):
    lg_f = -jnp.exp(decay_f.astype(jnp.float32))
    lg_b = -jnp.exp(decay_b.astype(jnp.float32))

    def project(h, rotate):
        b, L, _ = h.shape
        q, k, v, g_f, g_b = jnp.split(h @ w_in, [D_MODEL, 2 * D_MODEL, 2 * D_MODEL + RET_VW, 2 * D_MODEL + 2 * RET_VW], axis=-1)
        q = q.reshape(b, L, RET_HEADS, RET_DK)
        k = k.reshape(b, L, RET_HEADS, RET_DK)
        v = v.reshape(b, L, RET_HEADS, RET_DV)
        if rotate:
            q = axial_rope(q, ang_r, ang_c)
            k = axial_rope(k, ang_r, ang_c)
        return q, k * RET_DK ** -0.5, v, g_f, g_b

    def readout(y_f, y_b, g_f, g_b):
        b, L = g_f.shape[:2]
        o = jax.nn.silu(g_f) * rms_scale(y_f).reshape(b, L, RET_VW) + jax.nn.silu(g_b) * rms_scale(y_b).reshape(b, L, RET_VW)
        return o @ w_o

    qc, kc, vc, gfc, gbc = project(h_ctx, False)
    s0 = jnp.zeros((h_ctx.shape[0], RET_HEADS, RET_DK, RET_DV), h_ctx.dtype)
    yc_f, yc_b, sc_f, sc_b = bidir_retention(qc, kc, vc, lg_f, lg_b, s0, s0)
    ql, kl, vl, gfl, gbl = project(h_lat, True)
    yl_f, yl_b, _, _ = bidir_retention(ql, kl, vl, lg_f, lg_b, sc_f, sc_b)
    out_lat = readout(yl_f, yl_b, gfl, gbl)
    out_ctx = readout(yc_f, yc_b, gfc, gbc) if need_ctx_out else None
    return out_lat, out_ctx

def attend(q, k, v):
    s = jnp.einsum('bqhd,bkhd->bhqk', q, k).astype(jnp.float32)
    p = jax.nn.softmax(s, axis=-1).astype(v.dtype)
    return jnp.einsum('bhqk,bkhd->bqhd', p, v)

def mla_mixer(h_lat, h_ctx, w_in, q_a_norm, w_q_b, kv_a_norm, w_kv_b, q_norm, k_norm, w_o, ang_r, ang_c, need_ctx_out):
    def queries(a, rotate):
        b, L, _ = a.shape
        q = (rmsnorm(a[..., :MLA_Q_RANK], q_a_norm) @ w_q_b).reshape(b, L, MLA_HEADS, MLA_QK)
        q_nope = rmsnorm(q[..., :MLA_NOPE], q_norm[:MLA_NOPE])
        q_rope = rmsnorm(q[..., MLA_NOPE:], q_norm[MLA_NOPE:])
        if rotate:
            q_rope = axial_rope(q_rope, ang_r, ang_c)
        return jnp.concatenate([q_nope, q_rope], axis=-1) * MLA_QK ** -0.5

    def keys_values(a, rotate):
        b, L, _ = a.shape
        kv_lat = a[..., MLA_Q_RANK:MLA_Q_RANK + MLA_KV_RANK]
        k_rope = a[..., MLA_Q_RANK + MLA_KV_RANK:][:, :, None, :]
        kv = (rmsnorm(kv_lat, kv_a_norm) @ w_kv_b).reshape(b, L, MLA_HEADS, MLA_NOPE + MLA_V)
        k_nope = rmsnorm(kv[..., :MLA_NOPE], k_norm[:MLA_NOPE])
        k_rope = rmsnorm(k_rope, k_norm[MLA_NOPE:])
        if rotate:
            k_rope = axial_rope(k_rope, ang_r, ang_c)
        k = jnp.concatenate([k_nope, jnp.broadcast_to(k_rope, (b, L, MLA_HEADS, MLA_ROPE))], axis=-1)
        return k, kv[..., MLA_NOPE:]

    a_c = h_ctx @ w_in
    a_l = h_lat @ w_in
    kc, vc = keys_values(a_c, False)
    kl, vl = keys_values(a_l, True)
    ql = queries(a_l, True)
    k_all = jnp.concatenate([kl, kc], axis=1)
    v_all = jnp.concatenate([vl, vc], axis=1)
    b, S = h_lat.shape[:2]
    nb = S // ATTN_BLOCK
    q_blocks = ql.reshape(b, nb, ATTN_BLOCK, MLA_HEADS, MLA_QK).transpose(1, 0, 2, 3, 4)
    o = lax.map(lambda qb: attend(qb, k_all, v_all), q_blocks)
    o = o.transpose(1, 0, 2, 3, 4).reshape(b, S, MLA_HEADS * MLA_V)
    out_lat = o @ w_o
    if need_ctx_out:
        qc = queries(a_c, False)
        out_ctx = attend(qc, kc, vc).reshape(h_ctx.shape[0], h_ctx.shape[1], MLA_HEADS * MLA_V) @ w_o
    else:
        out_ctx = None
    return out_lat, out_ctx

def moe_ffn(h, router_w, router_bias, w_gu, w_down, sh_gu, sh_down):
    n = h.shape[0]
    s = jax.nn.sigmoid((h @ router_w).astype(jnp.float32))
    sel = s + router_bias.astype(jnp.float32)
    grp = sel.reshape(n, N_GROUPS, N_EXPERTS // N_GROUPS)
    gscore = lax.top_k(grp, 2)[0].sum(-1)
    _, gidx = lax.top_k(gscore, TOPK_GROUPS)
    gmask = jax.nn.one_hot(gidx, N_GROUPS, dtype=jnp.float32).sum(1) > 0
    emask = jnp.repeat(gmask, N_EXPERTS // N_GROUPS, axis=1)
    _, eidx = lax.top_k(jnp.where(emask, sel, -jnp.inf), TOP_K)
    w = jnp.take_along_axis(s, eidx, axis=1)
    w = w / jnp.sum(w, axis=-1, keepdims=True) * ROUTED_SCALE
    flat = eidx.reshape(-1)
    order = jnp.argsort(flat)
    tok = order // TOP_K
    sizes = jnp.bincount(flat, length=N_EXPERTS).astype(jnp.int32)
    gu = lax.ragged_dot(h[tok], w_gu, sizes)
    g, u = jnp.split(gu, 2, axis=-1)
    y = lax.ragged_dot(jax.nn.silu(g) * u, w_down, sizes)
    y = y[jnp.argsort(order)].reshape(n, TOP_K, h.shape[-1])
    routed = jnp.einsum('nkd,nk->nd', y, w.astype(y.dtype))
    gs, us = jnp.split(h @ sh_gu, 2, axis=-1)
    return routed + (jax.nn.silu(gs) * us) @ sh_down

def setup_inputs(seed: int = 0) -> dict:
    key = jax.random.key(seed)
    ks = jax.random.split(key, 32)
    f32 = jnp.float32

    def nrm(k, shape, scale):
        return jax.random.normal(k, shape, f32) * scale

    def gain(k, shape):
        return 1.0 + 0.05 * jax.random.normal(k, shape, f32)

    hh = jnp.arange(RET_HEADS, dtype=f32)
    base_decay = jnp.log(-jnp.log1p(-(2.0 ** (-5.0 - hh))))
    return {
        'x': nrm(ks[0], (BATCH, SEQ, D_MODEL), 1.0),
        'c': nrm(ks[1], (BATCH, D_MODEL), 1.0),
        'ctx': nrm(ks[2], (BATCH, CTX_LEN, D_MODEL), 1.0),
        'c_ctx': nrm(ks[3], (D_MODEL,), 1.0),
        'ada_w': nrm(ks[4], (DEPTH, D_MODEL, 6 * D_MODEL), 0.5 * D_MODEL ** -0.5),
        'ada_b': nrm(ks[5], (DEPTH, 6 * D_MODEL), 0.02),
        'norm_mix': gain(ks[6], (DEPTH, D_MODEL)),
        'norm_ffn': gain(ks[7], (DEPTH, D_MODEL)),
        'ret_w_in': nrm(ks[8], (N_RET, D_MODEL, RET_IN), D_MODEL ** -0.5),
        'ret_decay_f': base_decay[None] + 0.05 * jax.random.normal(ks[9], (N_RET, RET_HEADS), f32),
        'ret_decay_b': base_decay[None] + 0.05 * jax.random.normal(ks[10], (N_RET, RET_HEADS), f32),
        'ret_w_o': nrm(ks[11], (N_RET, RET_VW, D_MODEL), RET_VW ** -0.5),
        'mla_w_in': nrm(ks[12], (N_MLA, D_MODEL, MLA_IN), D_MODEL ** -0.5),
        'mla_q_a_norm': gain(ks[13], (N_MLA, MLA_Q_RANK)),
        'mla_w_q_b': nrm(ks[14], (N_MLA, MLA_Q_RANK, MLA_HEADS * MLA_QK), MLA_Q_RANK ** -0.5),
        'mla_kv_a_norm': gain(ks[15], (N_MLA, MLA_KV_RANK)),
        'mla_w_kv_b': nrm(ks[16], (N_MLA, MLA_KV_RANK, MLA_HEADS * (MLA_NOPE + MLA_V)), MLA_KV_RANK ** -0.5),
        'mla_q_norm': gain(ks[17], (N_MLA, MLA_QK)),
        'mla_k_norm': gain(ks[18], (N_MLA, MLA_QK)),
        'mla_w_o': nrm(ks[19], (N_MLA, MLA_HEADS * MLA_V, D_MODEL), (MLA_HEADS * MLA_V) ** -0.5),
        'router_w': nrm(ks[20], (DEPTH, D_MODEL, N_EXPERTS), D_MODEL ** -0.5),
        'router_bias': nrm(ks[21], (DEPTH, N_EXPERTS), 0.01),
        'exp_w_gu': nrm(ks[22], (DEPTH, N_EXPERTS, D_MODEL, 2 * EXPERT_FF), D_MODEL ** -0.5),
        'exp_w_down': nrm(ks[23], (DEPTH, N_EXPERTS, EXPERT_FF, D_MODEL), EXPERT_FF ** -0.5),
        'sh_w_gu': nrm(ks[24], (DEPTH, D_MODEL, 2 * SHARED_FF), D_MODEL ** -0.5),
        'sh_w_down': nrm(ks[25], (DEPTH, SHARED_FF, D_MODEL), SHARED_FF ** -0.5),
    }

def reference(x, c, ctx, c_ctx, ada_w, ada_b, norm_mix, norm_ffn, ret_w_in, ret_decay_f, ret_decay_b, ret_w_o,
              mla_w_in, mla_q_a_norm, mla_w_q_b, mla_kv_a_norm, mla_w_kv_b, mla_q_norm, mla_k_norm, mla_w_o,
              router_w, router_bias, exp_w_gu, exp_w_down, sh_w_gu, sh_w_down):
    ROWS = x.shape[1] // GRID_W
    ret_r, ret_c = axial_angles(ROWS, RET_DK)
    mla_r, mla_c = axial_angles(ROWS, MLA_ROPE)
    b = x.shape[0]
    n_ctx = ctx.shape[1]
    for i in range(DEPTH):
        need_ctx = i < DEPTH - 1
        j = i // N_MIXERS
        mod_l = (jax.nn.silu(c) @ ada_w[i] + ada_b[i])[:, None, :]
        mod_c = (jax.nn.silu(c_ctx) @ ada_w[i] + ada_b[i])[None, None, :]
        sh_ml, sc_ml, g_ml, sh_fl, sc_fl, g_fl = jnp.split(mod_l, 6, axis=-1)
        sh_mc, sc_mc, g_mc, sh_fc, sc_fc, g_fc = jnp.split(mod_c, 6, axis=-1)
        h_l = modulate(rmsnorm(x, norm_mix[i]), sh_ml, sc_ml)
        h_c = modulate(rmsnorm(ctx, norm_mix[i]), sh_mc, sc_mc)
        if i % N_MIXERS == 0:
            out_l, out_c = retention_mixer(h_l, h_c, ret_w_in[j], ret_decay_f[j], ret_decay_b[j], ret_w_o[j],
                                           ret_r, ret_c, need_ctx)
        else:
            out_l, out_c = mla_mixer(h_l, h_c, mla_w_in[j], mla_q_a_norm[j], mla_w_q_b[j], mla_kv_a_norm[j],
                                     mla_w_kv_b[j], mla_q_norm[j], mla_k_norm[j], mla_w_o[j], mla_r, mla_c, need_ctx)
        x = x + g_ml * out_l
        moe = lambda t: moe_ffn(t, router_w[i], router_bias[i], exp_w_gu[i], exp_w_down[i], sh_w_gu[i], sh_w_down[i])
        f_l_in = modulate(rmsnorm(x, norm_ffn[i]), sh_fl, sc_fl)
        if need_ctx:
            ctx = ctx + g_mc * out_c
            f_c_in = modulate(rmsnorm(ctx, norm_ffn[i]), sh_fc, sc_fc)
            f = lax.map(moe, jnp.concatenate([f_c_in, f_l_in], axis=1))
            ctx = ctx + g_fc * f[:, :n_ctx]
            x = x + g_fl * f[:, n_ctx:]
        else:
            x = x + g_fl * lax.map(moe, f_l_in)
    return x


_drawn_inputs = setup_inputs


def setup_inputs(seed=0):
    import zlib

    import numpy as np

    out = dict(_drawn_inputs(seed))
    spreads = {}
    factors = {'mla_q_a_norm': 7.21, 'mla_kv_a_norm': 3.974, 'mla_q_norm': 8.0, 'mla_k_norm': 8.0}
    for name, (base, spread) in spreads.items():
        noise = np.random.default_rng([zlib.crc32(name.encode()), seed]).standard_normal(out[name].shape)
        drawn = base * np.exp(spread * noise) if base else spread * noise
        out[name] = __import__('jax').numpy.asarray(drawn.astype(out[name].dtype))
    for name, factor in factors.items():
        out[name] = (out[name] * factor).astype(out[name].dtype)
    return out
```

```python
from contextlib import ExitStack

import numpy as np

import concourse.bass as bass
from concourse import mybir

ALU = mybir.AluOpType
ACT = mybir.ActivationFunctionType
AX_X = mybir.AxisListType.X
F32 = mybir.dt.float32
BF16 = mybir.dt.bfloat16
U32 = mybir.dt.uint32
I32 = mybir.dt.int32

P = 128
D = 1024
KD = D // P
SEQ, CTX = 512, 256
TC, TL = CTX // P, SEQ // P
T = TC + TL
GRID_W = 64
EPS = 1e-6
H, DK, DV = 4, 256, 512
VW = H * DV
MH, NOPE, ROPE, MV = 8, 128, 64, 128
QK = NOPE + ROPE
QR, KVR = 384, 256
E, TOPK, NG, TOPG = 64, 8, 8, 4
EG = E // NG
FF = 256
ROUTED_SCALE = 2.5
NC = 512


def bc(ap, shape, axes):
    for a in axes:
        ap = ap.unsqueeze(a)
    return ap.broadcast_to(shape)


class Kit:

    def __init__(self, nc, a, consts):
        self.nc, self.a, self.c = nc, a, consts
        self.n = 0
        self.sems = []

    def sem(self, name):
        self.n += 1
        self.sems.append(self.nc.alloc_semaphore(f"{name}_{self.n}"))
        return self.sems[-1]

    def recycle_semaphores(self):
        self.nc.clear_and_free_semaphores(self.sems)
        self.nc.all_engine_barrier()
        self.sems = []

    def sb(self, ctx, name, shape, dt=F32):
        self.n += 1
        return ctx.enter_context(self.nc.sbuf_tensor(f"{name}_{self.n}", shape, dt))

    def ps(self, ctx, name, shape, dt=F32):
        self.n += 1
        return ctx.enter_context(self.nc.psum_tensor(f"{name}_{self.n}", shape, dt))


def conditioning(k, mod_dram):
    nc, a = k.nc, k.a
    depth = a["ada_w"].shape[0]
    W = 6 * D
    RING = 4
    groups = W // NC // RING
    with ExitStack() as ctx:
        cond = k.sb(ctx, "cond", [P, 2, KD])
        silu = k.sb(ctx, "silu", [P, KD, 2])
        ring = k.sb(ctx, "ring", [P, RING, KD, NC])
        bias = k.sb(ctx, "bias", [2, depth * W])
        rows = k.sb(ctx, "rows", [2, depth * W])
        acc = k.ps(ctx, "acc", [P, RING, NC])
        cond_in, bias_in, silu_ready = k.sem("cond_in"), k.sem("bias_in"), k.sem("silu_ready")
        w_in = [k.sem(f"ada_w_in{j}") for j in range(RING)]
        slot_free, bank_free = k.sem("slot_free"), k.sem("bank_free")
        product, rows_ready, rows_out = k.sem("product"), k.sem("rows_ready"), k.sem("rows_out")
        block = ctx.enter_context(nc.Block())

        @block.sync
        def _(sp):
            sp.dma_start(cond[:, 0, :], a["c_ctx"].rearrange("(p k) -> p k", k=KD)).then_inc(cond_in, 16)
            sp.dma_start(cond[:, 1, :], a["c"].rearrange("b (p k) -> p (b k)", k=KD)).then_inc(cond_in, 16)
            sp.dma_start(bias[:], a["ada_b"].rearrange("l n -> (l n)").partition_broadcast(2)).then_inc(bias_in, 16)
            sp.sem_inc(slot_free, RING)
            for l in range(depth):
                w = a["ada_w"][l].rearrange("(p k) (g j n) -> p g j k n", k=KD, j=RING, n=NC)
                with sp.Fori(0, groups) as g:
                    for j in range(RING):
                        sp.wait_ge(slot_free, RING * (l * groups + g) + j + 1)
                        sp.dma_start(ring[:, j], w[:, g, j]).then_inc(w_in[j], 16)
            sp.wait_ge(rows_ready, depth * groups * RING)
            sp.dma_start(mod_dram.rearrange("s l n -> s (l n)"), rows[:]).then_inc(rows_out, 16)
            sp.wait_ge(rows_out, 16)

        @block.scalar
        def _(act):
            act.wait_ge(cond_in, 32)
            act.activation(silu[:].rearrange("p k s -> p s k"), cond[:], ACT.Silu).then_inc(silu_ready, 1)

        @block.tensor
        def _(pe):
            pe.wait_ge(silu_ready, 1)
            with pe.Fori(0, depth * groups) as g:
                for j in range(RING):
                    pe.wait_ge(w_in[j], 16 * (g + 1))
                    pe.wait_ge(bank_free, RING * g + j + 1)
                    for kk in range(KD):
                        mm = pe.matmul(acc[0:2, j, :], silu[:, kk, :], ring[:, j, kk, :],
                                       start=(kk == 0), stop=(kk == KD - 1))
                        if kk == KD - 1:
                            mm.then_inc(product, 1)

        @block.vector
        def _(dve):
            dve.sem_inc(bank_free, RING)
            dve.wait_ge(bias_in, 16)
            with dve.Fori(0, depth * groups) as g:
                for j in range(RING):
                    dve.wait_ge(product, RING * g + j + 1)
                    at = bass.ds((g * RING + j) * NC, NC)
                    dve.tensor_tensor(rows[:, at], acc[0:2, j, :], bias[:, at], ALU.add).then_inc(rows_ready, 1)
                    dve.wait_ge(rows_ready, RING * g + j + 1)
                    dve.sem_inc(bank_free, 1)
                    dve.sem_inc(slot_free, 1)


def norm_modulate(k, ident, layer, which, norm_w, mod_dram, tiles, x_sb, hT, x_dram=None, h_dram=None):
    nc, a = k.nc, k.a
    n = len(tiles)
    t0 = tiles[0]
    streams = sorted({int(t >= TC) for t in tiles})
    with ExitStack() as ctx:
        gain = k.sb(ctx, "gain", [P, D])
        scale = k.sb(ctx, "scale", [P, 2, D])
        shift = k.sb(ctx, "shift", [P, 2, D])
        square = k.sb(ctx, "square", [P, D])
        ms = k.sb(ctx, "ms", [P, T])
        mse = k.sb(ctx, "mse", [P, T])
        root = k.sb(ctx, "root", [P, T])
        rinv = k.sb(ctx, "rinv", [P, T])
        h = k.sb(ctx, "h", [P, 2, D])
        turned = k.ps(ctx, "turned", [P, 2, D])
        x_in, rows_in = k.sem("x_in"), k.sem("rows_in")
        squares, ms_ready, root_ready, rinv_ready = k.sem("squares"), k.sem("ms_ready"), k.sem("root_ready"), k.sem("rinv_ready")
        scale_ready, scaled, h_ready = k.sem("scale_ready"), k.sem("scaled"), k.sem("h_ready")
        h_turned, hT_ready = k.sem("h_turned"), k.sem("hT_ready")
        h_out = [k.sem("h_out0"), k.sem("h_out1")]
        block = ctx.enter_context(nc.Block())

        @block.sync
        def _(sp):
            if x_dram is not None:
                sp.dma_start(x_sb[:, 0:TC], x_dram[0].rearrange("b (t p) d -> p (b t) d", p=P)).then_inc(x_in, 16)
                sp.dma_start(x_sb[:, TC:T], x_dram[1].rearrange("b (t p) d -> p (b t) d", p=P)).then_inc(x_in, 16)
            sp.dma_start(gain[:], norm_w.partition_broadcast(P)).then_inc(rows_in, 16)
            for s in streams:
                row = mod_dram[s, layer]
                sp.dma_start(shift[:, s], row[which * D:(which + 1) * D].partition_broadcast(P)).then_inc(rows_in, 16)
                sp.dma_start(scale[:, s], row[(which + 1) * D:(which + 2) * D].partition_broadcast(P)).then_inc(rows_in, 16)
            if h_dram is not None:
                for i, t in enumerate(tiles):
                    sp.wait_ge(h_ready, i + 1)
                    sp.dma_start(h_dram[i * P:(i + 1) * P, :], h[:, i % 2]).then_inc(h_out[i % 2], 16)
                for j in range(2):
                    sp.wait_ge(h_out[j], 16 * (n // 2))
        @block.scalar
        def _(act):
            if x_dram is not None:
                act.wait_ge(x_in, 32)
            for i, t in enumerate(tiles):
                if i:
                    act.wait_ge(squares, i)
                act.activation(square[:], x_sb[:, t], ACT.Square, accum_out=ms[:, t:t + 1]).then_inc(squares, 1)
            act.wait_ge(ms_ready, 1)
            act.activation(root[:, t0:T], mse[:, t0:T], ACT.Sqrt).then_inc(root_ready, 1)
            for i, t in enumerate(tiles):
                act.wait_ge(h_turned, i + 1)
                act.activation(hT[:, :, i * P:(i + 1) * P], turned[:, i % 2].rearrange("p (k m) -> p k m", k=KD),
                               ACT.Copy).then_inc(hT_ready, 1)

        @block.vector
        def _(dve):
            dve.wait_ge(rows_in, 16 * (1 + 2 * len(streams)))
            for s in streams:
                dve.scalar_tensor_tensor(scale[:, s], scale[:, s], 1.0, gain[:], ALU.add, ALU.mult).then_inc(scale_ready, 1)
            dve.wait_ge(squares, n)
            dve.tensor_scalar(mse[:, t0:T], ms[:, t0:T], 1.0 / D, EPS, ALU.mult, ALU.add).then_inc(ms_ready, 1)
            dve.wait_ge(root_ready, 1)
            dve.reciprocal(rinv[:, t0:T], root[:, t0:T]).then_inc(rinv_ready, 1)
            dve.wait_ge(rinv_ready, 1)
            dve.wait_ge(scale_ready, len(streams))
            for i, t in enumerate(tiles):
                s = int(t >= TC)
                if i >= 2:
                    dve.wait_ge(h_turned, i - 1)
                    if h_dram is not None:
                        dve.wait_ge(h_out[i % 2], 16 * (i // 2))
                dve.scalar_tensor_tensor(h[:, i % 2], x_sb[:, t], rinv[:, t:t + 1], scale[:, s], ALU.mult, ALU.mult).then_inc(scaled, 1)
                dve.wait_ge(scaled, i + 1)
                dve.tensor_tensor(h[:, i % 2], h[:, i % 2], shift[:, s], ALU.add).then_inc(h_ready, 1)

        @block.tensor
        def _(pe):
            for i in range(n):
                pe.wait_ge(h_ready, i + 1)
                if i >= 2:
                    pe.wait_ge(hT_ready, i - 1)
                for kk in range(KD):
                    mm = pe.transpose(turned[:, i % 2, kk * P:(kk + 1) * P], h[:, i % 2, kk * P:(kk + 1) * P], ident[:])
                mm.then_inc(h_turned, 1)


def reached(s, i):
    if s == 0:
        return list(range(i + 1))
    return list(range(i, TC)) if i < TC else list(range(TC)) + list(range(i, T))


def retention(k, ident, hT, oT, x_sb, y_dram):
    nc, a, c = k.nc, k.a, k.c
    w_in = a["ret_w_in"][0].rearrange("(k p) n -> p k n", p=P)
    with ExitStack() as ctx:
        ring = k.sb(ctx, "w", [P, 2, KD, NC])
        zeros = k.sb(ctx, "zeros", [P, NC])
        cos = k.sb(ctx, "cos", [P, TL, 2, 2, 64])
        sin = k.sb(ctx, "sin", [P, TL, 2, 2, 64])
        rel = k.sb(ctx, "rel", [P, 2, T * P])
        tri = k.sb(ctx, "tri", [P, 2, P])
        dec = k.sb(ctx, "dec", [P, 2, H])
        lgp = k.sb(ctx, "lgp", [P, 2, H])
        lg = k.sb(ctx, "lg", [P, 2, H])
        decay = k.sb(ctx, "decay", [P, 2, T * P])
        qk = k.sb(ctx, "qk", [P, 2, NC])
        rot = k.sb(ctx, "rot", [P, 2, 2, 2, 64])
        qT = k.sb(ctx, "qT", [P, 2, T * P])
        kT = k.sb(ctx, "kT", [P, 2, T * P])
        v = k.sb(ctx, "v", [P, T, DV])
        gate = x_sb[:].rearrange("p t (s n) -> p s t n", s=2)
        probs = k.sb(ctx, "probs", [P, 2, 2, T * P])
        square = k.sb(ctx, "square", [P, DV])
        ss = k.sb(ctx, "ss", [P, 2])
        mse = k.sb(ctx, "mse", [P, 2])
        root = k.sb(ctx, "root", [P, 2])
        rinv = k.sb(ctx, "rinv", [P, 2])
        read = k.sb(ctx, "read", [P, 2, DV])
        o = k.sb(ctx, "o", [P, 2, DV])
        bank = k.ps(ctx, "bank", [P, 8, NC])
        qk_ps = [bank[:, 0], bank[:, 1]]
        vg_ps = [bank[:, 2], bank[:, 3]]
        turn_ps = [bank[:, 4], bank[:, 5]]
        score_ps = [bank[:, 0:2].rearrange("p b n -> p (b n)"), bank[:, 2:4].rearrange("p b n -> p (b n)")]
        y_ps = [bank[:, 6], bank[:, 7]]

        const_in, dec_in = k.sem("const_in"), k.sem("dec_in")
        w_qk, w_v, w_gf, w_gb = (k.sem(x) for x in ("w_qk", "w_v", "w_gf", "w_gb"))
        weighed = k.sem("weighed")
        qk_done, qk_read, vg_done, vg_read = k.sem("qk_done"), k.sem("qk_read"), k.sem("vg_done"), k.sem("vg_read")
        rope_step, qk_ready, qk_turned, qkT_ready = k.sem("rope_step"), k.sem("qk_ready"), k.sem("qk_turned"), k.sem("qkT_ready")
        lg_step, tri_done, table_ready = k.sem("lg_step"), k.sem("tri_done"), k.sem("table_ready")
        scored, probs_ready = k.sem("scored"), k.sem("probs_ready")
        y_done, squares, ms_ready, root_ready, rinv_ready = (k.sem(x) for x in ("y_done", "squares", "ms_ready", "root_ready", "rinv_ready"))
        read_ready, o_ready, o_turned, oT_ready = k.sem("read_ready"), k.sem("o_ready"), k.sem("o_turned"), k.sem("oT_ready")
        block = ctx.enter_context(nc.Block())
        zeroed, y_zeroed = k.sem("zeroed"), k.sem("y_zeroed")
        pairs_of_blocks = y_dram.rearrange("(i b p) (c n) -> i p b c n", b=2, p=P, n=NC)

        @block.gpsimd
        def _(pool):
            pool.memset(zeros[:], 0.0).then_inc(zeroed, 1)
            pool.wait_ge(zeroed, 1)
            pool.wait_ge(qk_done, 1)
            with pool.Fori(0, pairs_of_blocks.shape[0]) as i:
                for b in range(2):
                    pool.dma_start(pairs_of_blocks[i, :, b], bc(zeros[:], [P, D // NC, NC], [1])).then_inc(y_zeroed, 16)
            pool.wait_ge(y_zeroed, 2 * 16 * pairs_of_blocks.shape[0])

        VG = 3 * T
        wv = w_in[:, :, 2 * D:].rearrange("p k (s h n) -> p s h k n", s=3, h=H)
        wqk = w_in[:, :, 0:2 * D].rearrange("p k (s h n) -> p s h k n", s=2, h=H)

        @block.sync
        def _(sp):
            with nc.allow_non_contiguous_dma(reason="small constants"):
                sp.dma_start(cos[:], c["ret_cos"].rearrange("p (t a b n) -> p t a b n", t=TL, a=2, b=2)).then_inc(const_in, 16)
                sp.dma_start(sin[:], c["ret_sin"].rearrange("p (t a b n) -> p t a b n", t=TL, a=2, b=2)).then_inc(const_in, 16)
                sp.dma_start(rel[:], c["ret_rel"].rearrange("p (s n) -> p s n", s=2)).then_inc(const_in, 16)
                sp.dma_start(tri[:], c["ret_tri"].rearrange("p (s n) -> p s n", s=2)).then_inc(const_in, 16)
                sp.dma_start(dec[:, 0], a["ret_decay_f"][0].partition_broadcast(P)).then_inc(dec_in, 16)
                sp.dma_start(dec[:, 1], a["ret_decay_b"][0].partition_broadcast(P)).then_inc(dec_in, 16)
                with sp.Fori(0, H) as h:
                    sp.wait_ge(vg_done, VG * h + 1)
                    for s in range(2):
                        sp.dma_start(ring[:, 0, :, s * DK:(s + 1) * DK], wqk[:, s, h]).then_inc(w_qk, 16)
                    sp.dma_start(ring[:, 1], wv[:, 0, h]).then_inc(w_v, 16)
                    sp.wait_ge(qk_done, T * (h + 1))
                    sp.dma_start(ring[:, 0], wv[:, 1, h]).then_inc(w_gf, 16)
                    sp.wait_ge(vg_done, VG * h + T + 1)
                    sp.dma_start(ring[:, 1], wv[:, 2, h]).then_inc(w_gb, 16)

        @block.tensor
        def _(pe):
            for opened in (vg_done, qk_turned, o_turned):
                pe.sem_inc(opened, 1)

            def project(out, slot, t):
                for kk in range(KD):
                    mm = pe.matmul(out, hT[:, kk, t * P:(t + 1) * P], ring[:, slot, kk, :],
                                   start=(kk == 0), stop=(kk == KD - 1))
                return mm

            def turn_qk(h, t):
                pe.wait_ge(qk_ready, T * h + t + 1)
                if t >= 2:
                    pe.wait_ge(qkT_ready, 2 * (T * h + t - 1))
                else:
                    pe.wait_ge(oT_ready, T * h + 1)
                for j in range(4):
                    mm = pe.transpose(turn_ps[t % 2][:, j * P:(j + 1) * P], qk[:, t % 2, j * P:(j + 1) * P], ident[:])
                mm.then_inc(qk_turned, 1)

            def scores(h, i):
                if i >= 2:
                    pe.wait_ge(probs_ready, T * h + i - 1 + 1)
                js = range(TC) if i < TC else range(T)
                for j in js:
                    for d in range(2):
                        mm = pe.matmul(score_ps[i % 2][:, j * P:(j + 1) * P], kT[:, d, j * P:(j + 1) * P],
                                       qT[:, d, i * P:(i + 1) * P], start=(d == 0), stop=(d == 1))
                mm.then_inc(scored, 1)

            def values(h, i):
                pe.wait_ge(probs_ready, T * h + i + 1 + 1)
                for s in range(2):
                    pe.wait_ge(read_ready, 2 * (T * h + i) + 1)
                    js = reached(s, i)
                    for n, j in enumerate(js):
                        mm = pe.matmul(y_ps[s], probs[:, i % 2, s, j * P:(j + 1) * P], v[:, j, :],
                                       start=(n == 0), stop=(n == len(js) - 1))
                    mm.then_inc(y_done, 1)

            def turn_o(h, i):
                pe.wait_ge(o_ready, T * h + i + 1 + 1)
                if i >= 2:
                    pe.wait_ge(oT_ready, T * h + i - 1 + 1)
                for j in range(4):
                    mm = pe.transpose(turn_ps[i % 2][:, j * P:(j + 1) * P], o[:, i % 2, j * P:(j + 1) * P], ident[:])
                mm.then_inc(o_turned, 1)

            with pe.Fori(0, H) as h:
                pe.wait_ge(probs_ready, T * h + 1)
                for ci, (w_sem, w_count) in enumerate(((w_qk, 2), (w_v, 1), (w_gf, 1), (w_gb, 1))):
                    pe.wait_ge(w_sem, 16 * w_count * (h + 1))
                    for t in range(T):
                        if ci == 0:
                            if t >= 2:
                                pe.wait_ge(qk_read, T * h + t - 1)
                            mm = project(qk_ps[t % 2], 0, t)
                            mm.then_inc(qk_done, 1)
                            if t >= 1:
                                turn_qk(h, t - 1)
                        else:
                            m = (ci - 1) * T + t
                            if m >= 2:
                                pe.wait_ge(vg_read, VG * h + m - 1)
                            mm = project(vg_ps[m % 2], ci % 2, t)
                            mm.then_inc(vg_done, 1)
                            if m == 0:
                                turn_qk(h, T - 1)
                pe.wait_ge(qkT_ready, 2 * T * (h + 1))
                pe.wait_ge(vg_read, VG * (h + 1))
                pe.wait_ge(qk_read, T * (h + 1))
                scores(h, 0)
                for i in range(T):
                    if i + 1 < T:
                        scores(h, i + 1)
                    values(h, i)
                    if i >= 1:
                        turn_o(h, i - 1)
                turn_o(h, T - 1)

        @block.scalar
        def _(act):
            for opened in (squares, oT_ready):
                act.sem_inc(opened, 1)
            act.wait_ge(dec_in, 32)
            act.activation(lgp[:], dec[:], ACT.Exp).then_inc(lg_step, 1)
            act.wait_ge(const_in, 64)
            act.wait_ge(lg_step, 2)
            with act.Fori(0, H) as h:
                act.wait_ge(probs_ready, T * h + 1)
                for s in range(2):
                    act.activation(decay[:, s], rel[:, s], ACT.Exp, scale=lg[:, s, bass.ds(h, 1)]).then_inc(table_ready, 1)
                for t in range(T):
                    act.wait_ge(qk_turned, T * h + t + 1 + 1)
                    at = slice(t * P, (t + 1) * P)
                    turned = turn_ps[t % 2].rearrange("p (s d n) -> p s d n", s=2, d=2)
                    act.activation(qT[:, :, at], turned[:, 0], ACT.Copy).then_inc(qkT_ready, 1)
                    act.activation(kT[:, :, at], turned[:, 1], ACT.Copy, scale=DK ** -0.5).then_inc(qkT_ready, 1)
                for m in range(VG):
                    t = m % T
                    act.wait_ge(vg_done, VG * h + m + 1 + 1)
                    if m < T:
                        if m == 0:
                            act.wait_ge(o_ready, T * h + 1)
                        act.activation(v[:, t], vg_ps[m % 2], ACT.Copy).then_inc(vg_read, 1)
                    else:
                        act.activation(gate[:, m // T - 1, t], vg_ps[m % 2], ACT.Silu).then_inc(vg_read, 1)
                def copy_oT(h, i):
                    act.wait_ge(o_turned, T * h + i + 1 + 1)
                    act.activation(oT[:, bass.ds(h * 4, 4), i * P:(i + 1) * P],
                                   turn_ps[i % 2].rearrange("p (d n) -> p d n", d=4), ACT.Copy).then_inc(oT_ready, 1)
                for i in range(T):
                    for s in range(2):
                        n = 2 * (T * h + i) + s
                        act.wait_ge(y_done, n + 1)
                        act.wait_ge(squares, n + 1)
                        act.activation(square[:], y_ps[s], ACT.Square, accum_out=ss[:, s:s + 1]).then_inc(squares, 1)
                        act.wait_ge(ms_ready, n + 1)
                        act.activation(root[:, s:s + 1], mse[:, s:s + 1], ACT.Sqrt).then_inc(root_ready, 1)
                    if i >= 1:
                        copy_oT(h, i - 1)
                copy_oT(h, T - 1)

        @block.vector
        def _(dve):
            for opened in (probs_ready, read_ready, o_ready):
                dve.sem_inc(opened, 1)
            dve.wait_ge(const_in, 64)
            dve.wait_ge(lg_step, 1)
            dve.tensor_scalar(lg[:], lgp[:], -1.0, None, ALU.mult).then_inc(lg_step, 1)
            with dve.Fori(0, H) as h:
                for s in range(2):
                    dve.wait_ge(table_ready, 2 * h + s + 1)
                    at = slice((T - 1) * P, T * P) if s == 0 else slice(0, P)
                    dve.tensor_tensor(decay[:, s, at], decay[:, s, at], tri[:, s], ALU.mult).then_inc(tri_done, 1)
                for t in range(T):
                    n = T * h + t
                    dve.wait_ge(qk_done, n + 1)
                    if t >= 2:
                        dve.wait_ge(qk_turned, n - 1 + 1)
                    else:
                        dve.wait_ge(qk_turned, T * h + 1)
                    if t < TC:
                        dve.tensor_copy(qk[:, t % 2], qk_ps[t % 2]).then_inc(qk_ready, 1)
                        dve.wait_ge(qk_ready, n + 1)
                        dve.sem_inc(qk_read, 1)
                        continue
                    m = TL * h + t - TC
                    src = qk_ps[t % 2].rearrange("p (s a b n) -> p s a b n", s=2, a=2, b=2)
                    dst = qk[:, t % 2].rearrange("p (s a b n) -> p s a b n", s=2, a=2, b=2)
                    lt = t - TC
                    for s in range(2):
                        dve.tensor_tensor(dst[:, s], src[:, s], cos[:, lt], ALU.mult).then_inc(rope_step, 1)
                        for b in range(2):
                            dve.tensor_tensor(rot[:, s, :, b], src[:, s, :, 1 - b], sin[:, lt, :, b], ALU.mult).then_inc(rope_step, 1)
                    dve.wait_ge(rope_step, 6 * (m + 1))
                    dve.sem_inc(qk_read, 1)
                    dve.tensor_tensor(qk[:, t % 2], qk[:, t % 2], rot[:].rearrange("p s a b n -> p (s a b n)"),
                                      ALU.add).then_inc(qk_ready, 1)
                    dve.wait_ge(qk_ready, n + 1)

                def weigh(h, i):
                    n = T * h + i
                    dve.wait_ge(scored, n + 1)
                    if i >= 2:
                        dve.wait_ge(y_done, 2 * (n - 1))
                    sc = score_ps[i % 2]
                    w = (i + 1) * P
                    dve.tensor_tensor(probs[:, i % 2, 0, 0:w], sc[:, 0:w], decay[:, 0, T * P - w:T * P], ALU.mult).then_inc(weighed, 1)
                    if i < TC:
                        w = (TC - i) * P
                        dve.tensor_tensor(probs[:, i % 2, 1, i * P:TC * P], sc[:, i * P:TC * P], decay[:, 1, 0:w],
                                          ALU.mult).then_inc(weighed, 1)
                    else:
                        dve.tensor_tensor(probs[:, i % 2, 1, 0:TC * P], sc[:, 0:TC * P],
                                          decay[:, 1, (T - i) * P:(T - i + TC) * P], ALU.mult)
                        w = (T - i) * P
                        dve.tensor_tensor(probs[:, i % 2, 1, i * P:T * P], sc[:, i * P:T * P], decay[:, 1, 0:w],
                                          ALU.mult).then_inc(weighed, 1)
                    dve.wait_ge(weighed, 2 * (n + 1))
                    dve.sem_inc(probs_ready, 1)

                dve.wait_ge(tri_done, 2 * (h + 1))
                weigh(h, 0)
                for i in range(T):
                    if i + 1 < T:
                        weigh(h, i + 1)
                    n = T * h + i
                    for s in range(2):
                        m = 2 * n + s
                        dve.wait_ge(squares, m + 1 + 1)
                        dve.tensor_scalar(mse[:, s:s + 1], ss[:, s:s + 1], 1.0 / DV, EPS, ALU.mult, ALU.add).then_inc(ms_ready, 1)
                        dve.wait_ge(root_ready, m + 1)
                        dve.reciprocal(rinv[:, s:s + 1], root[:, s:s + 1]).then_inc(rinv_ready, 1)
                        dve.wait_ge(rinv_ready, m + 1)
                        dve.scalar_tensor_tensor(read[:, s], y_ps[s], rinv[:, s:s + 1], gate[:, s, i], ALU.mult,
                                                 ALU.mult).then_inc(read_ready, 1)
                    dve.wait_ge(read_ready, 2 * (n + 1) + 1)
                    if i >= 2:
                        dve.wait_ge(o_turned, n - 1 + 1)
                    else:
                        dve.wait_ge(o_turned, T * h + 1)
                    dve.tensor_tensor(o[:, i % 2], read[:, 0], read[:, 1], ALU.add).then_inc(o_ready, 1)
                    dve.wait_ge(o_ready, n + 1 + 1)


def project_out(k, oT, kt, w, gate_row, mod_dram, x_sb, tiles, x_dram=None):
    nc = k.nc
    n = len(tiles)
    streams = sorted({int(t >= TC) for t in tiles})
    with ExitStack() as ctx:
        w_sb = k.sb(ctx, "wo", [P, 2, kt, NC])
        gate = k.sb(ctx, "gate", [P, 2, D])
        gated = k.sb(ctx, "gated", [P, 2, NC])
        acc = k.ps(ctx, "acc", [P, 4, NC])
        w_in = [k.sem("wo_in0"), k.sem("wo_in1")]
        x_in, gate_in = k.sem("x_in"), k.sem("gate_in")
        product, gated_ready, x_ready = k.sem("product"), k.sem("gated_ready"), k.sem("x_ready")
        block = ctx.enter_context(nc.Block())

        @block.sync
        def _(sp):
            for j in range(2):
                for part in range(2):
                    half = slice(part * kt // 2, (part + 1) * kt // 2)
                    sp.dma_start(w_sb[:, j, half], w.rearrange("(k p) n -> p k n", p=P)[:, half, j * NC:(j + 1) * NC]).then_inc(w_in[j], 16)
            for s in streams:
                sp.dma_start(gate[:, s], mod_dram[s, gate_row[0]][gate_row[1] * D:(gate_row[1] + 1) * D].partition_broadcast(P)).then_inc(gate_in, 16)
            if x_dram is not None:
                sp.dma_start(x_sb[:, 0:TC], x_dram[0].rearrange("b (t p) d -> p (b t) d", p=P)).then_inc(x_in, 16)
                sp.dma_start(x_sb[:, TC:T], x_dram[1].rearrange("b (t p) d -> p (b t) d", p=P)).then_inc(x_in, 16)

        @block.tensor
        def _(pe):
            for j in range(2):
                pe.wait_ge(w_in[j], 32)
                for i in range(n):
                    m = j * n + i
                    if m >= 4:
                        pe.wait_ge(gated_ready, m - 3)
                    for kk in range(kt):
                        mm = pe.matmul(acc[:, m % 4], oT[:, kk, i * P:(i + 1) * P], w_sb[:, j, kk, :],
                                       start=(kk == 0), stop=(kk == kt - 1))
                    mm.then_inc(product, 1)

        @block.vector
        def _(dve):
            dve.wait_ge(gate_in, 16 * len(streams))
            if x_dram is not None:
                dve.wait_ge(x_in, 32)
            for j in range(2):
                at = slice(j * NC, (j + 1) * NC)
                for i, t in enumerate(tiles):
                    m = j * n + i
                    dve.wait_ge(product, m + 1)
                    if m >= 2:
                        dve.wait_ge(x_ready, m - 1)
                    dve.tensor_tensor(gated[:, m % 2], acc[:, m % 4], gate[:, int(t >= TC), at], ALU.mult).then_inc(gated_ready, 1)
                    dve.wait_ge(gated_ready, m + 1)
                    dve.tensor_tensor(x_sb[:, t, at], x_sb[:, t, at], gated[:, m % 2], ALU.add).then_inc(x_ready, 1)


def route(k, ident, layer, hT, tiles, book):
    nc, a, c = k.nc, k.a, k.c
    n = len(tiles)
    NB = book.blocks
    with ExitStack() as ctx:
        rw = k.sb(ctx, "router_w", [P, KD, E])
        bias = k.sb(ctx, "router_bias", [P, E])
        lower = k.sb(ctx, "lower", [P, NG, NG])
        before = k.sb(ctx, "before", [P, P], BF16)
        ones_bf = k.sb(ctx, "ones_bf", [P, P], BF16)
        ones = k.sb(ctx, "ones", [P, E])
        block_no = k.sb(ctx, "block_no", [P, 1])
        block_no_i = k.sb(ctx, "block_no_i", [P, 1], I32)
        token = k.sb(ctx, "token", [P, n], U32)
        zeros = k.sb(ctx, "zeros", [P, NB], U32)
        s = k.sb(ctx, "s", [P, n, E])
        sel = k.sb(ctx, "sel", [P, n, E])
        best = k.sb(ctx, "best", [P, n, NG, 8])
        gs = k.sb(ctx, "gs", [P, n, NG])
        beats = k.sb(ctx, "beats", [P, n, NG, NG])
        ties = k.sb(ctx, "ties", [P, n, NG, NG])
        rank = k.sb(ctx, "rank", [P, n, NG])
        gmask = k.sb(ctx, "gmask", [P, n, NG])
        gpen = k.sb(ctx, "gpen", [P, n, NG])
        top = k.sb(ctx, "top", [P, n, 8])
        left = k.sb(ctx, "left", [P, n, E])
        mask = k.sb(ctx, "mask", [P, n, E])
        mask_bf = k.sb(ctx, "mask_bf", [P, n, E], BF16)
        w = k.sb(ctx, "w", [P, n, E])
        wsum = k.sb(ctx, "wsum", [P, n])
        winv = k.sb(ctx, "winv", [P, n])
        nblk = k.sb(ctx, "nblk", [P, E])
        end = k.sb(ctx, "end", [P, E])
        start = k.sb(ctx, "start", [P, E])
        pos = k.sb(ctx, "pos", [P, n, E])
        top_slot = k.sb(ctx, "top_slot", [P, n, TOPK])
        junk = k.sb(ctx, "junk", [P, E])
        below = k.sb(ctx, "below", [P, 1])
        expert_f = k.sb(ctx, "expert_f", [P, 1])
        expert_i = k.sb(ctx, "expert_i", [P, 1], I32)
        pairs_f = k.sb(ctx, "pairs_f", [P, 1])
        logits = k.ps(ctx, "logits", [P, n, E])
        ranks = k.ps(ctx, "ranks", [P, n, E])
        counts = k.ps(ctx, "counts", [P, E])
        const_in, table_zeroed, scattered, expert_out = k.sem("const_in"), k.sem("table_zeroed"), k.sem("scattered"), k.sem("expert_out")
        made, logits_ready, s_ready, mask_ready, ranks_ready, slots_ready = (
            k.sem(x) for x in ("made", "logits_ready", "s_ready", "mask_ready", "ranks_ready", "slots_ready"))
        step, expert_ready = k.sem("step"), k.sem("expert_ready")
        block = ctx.enter_context(nc.Block())

        @block.sync
        def _(sp):
            sp.dma_start(rw[:], a["router_w"][layer].rearrange("(k p) e -> p k e", p=P)).then_inc(const_in, 16)
            sp.dma_start(bias[:], a["router_bias"][layer].partition_broadcast(P)).then_inc(const_in, 16)
            sp.dma_start(lower[:], c["lower"].rearrange("p (g f) -> p g f", g=NG)).then_inc(const_in, 16)
            sp.wait_ge(made, 1)
            sp.dma_start(book.table_dram.rearrange("(p b) o -> p (b o)", p=P), zeros[:]).then_inc(table_zeroed, 16)
            sp.wait_ge(expert_ready, 1)
            sp.dma_start(book.expert_dram, expert_i[:]).then_inc(expert_out, 16)
            sp.wait_ge(expert_out, 16)

        @block.gpsimd
        def _(pool):
            pool.memset(zeros[:], 0).then_inc(made, 1)
            pool.memset(ones_bf[:], 1.0).then_inc(made, 1)
            pool.memset(ones[:], 1.0).then_inc(made, 1)
            pool.iota(block_no_i[:], [[0, 1]], base=0, channel_multiplier=1).then_inc(made, 1)
            pool.iota(token[:], [[P, n]], base=0, channel_multiplier=1).then_inc(made, 1)
            pool.wait_ge(made, 2)
            pool.affine_select(out=before[:], in_=ones_bf[:], compare_op=ALU.is_gt, fill=0.0, base=0,
                               pattern=[[1, P]], channel_multiplier=-1).then_inc(made, 1)
            pool.wait_ge(made, 6)
            pool.wait_ge(table_zeroed, 16)
            pool.wait_ge(slots_ready, 1)
            for t in range(n):
                for j in range(TOPK):
                    pool.indirect_dma_start(book.table_dram, bass.IndirectOffsetOnAxis(ap=book.slot[:, t, j:j + 1], axis=0),
                                            token[:, t:t + 1], None).then_inc(scattered, 16)
            pool.wait_ge(scattered, 16 * n * TOPK)

        @block.tensor
        def _(pe):
            pe.wait_ge(const_in, 48)
            for t in range(n):
                for kk in range(KD):
                    mm = pe.matmul(logits[:, t], hT[:, kk, t * P:(t + 1) * P], rw[:, kk, :], start=(kk == 0), stop=(kk == KD - 1))
            mm.then_inc(logits_ready, 1)
            pe.wait_ge(mask_ready, 1)
            pe.wait_ge(made, 6)
            for t in range(n):
                for u in range(t + 1):
                    mm = pe.matmul(ranks[:, t], before[:] if u == t else ones_bf[:], mask_bf[:, u, :], start=(u == 0), stop=(u == t))
            for u in range(n):
                mm = pe.matmul(counts[:], ones_bf[:], mask_bf[:, u, :], start=(u == 0), stop=(u == n - 1))
            mm.then_inc(ranks_ready, 1)

        @block.scalar
        def _(act):
            act.wait_ge(logits_ready, 1)
            act.activation(s[:], logits[:], ACT.Sigmoid).then_inc(s_ready, 1)

        @block.vector
        def _(dve):
            count = [0]

            def then(ins):
                count[0] += 1
                ins.then_inc(step, 1)
                dve.wait_ge(step, count[0])

            dve.wait_ge(const_in, 48)
            dve.wait_ge(s_ready, 1)
            then(dve.tensor_tensor(sel[:], s[:], bc(bias[:], [P, n, E], [1]), ALU.add))
            for t in range(n):
                for g in range(NG):
                    ins = dve.max(best[:, t, g], sel[:, t, g * EG:(g + 1) * EG])
            then(ins)
            then(dve.tensor_tensor(gs[:], best[:, :, :, 0], best[:, :, :, 1], ALU.add))
            other = bc(gs[:], [P, n, NG, NG], [2])
            own = bc(gs[:], [P, n, NG, NG], [3])
            dve.tensor_tensor(beats[:], other, own, ALU.is_gt)
            then(dve.tensor_tensor(ties[:], other, own, ALU.is_equal))
            then(dve.tensor_tensor(ties[:], ties[:], bc(lower[:], [P, n, NG, NG], [1]), ALU.mult))
            then(dve.tensor_tensor(beats[:], beats[:], ties[:], ALU.add))
            then(dve.tensor_reduce(rank[:], beats[:], AX_X, ALU.add))
            then(dve.tensor_scalar(gmask[:], rank[:], float(TOPG), None, ALU.is_lt))
            then(dve.tensor_scalar(gpen[:], gmask[:], 1e30, -1e30, ALU.mult, ALU.add))
            sel_g = sel[:].rearrange("p t (g e) -> p t g e", g=NG)
            then(dve.tensor_tensor(sel_g, sel_g, bc(gmask[:], [P, n, NG, EG], [3]), ALU.mult))
            then(dve.tensor_tensor(sel_g, sel_g, bc(gpen[:], [P, n, NG, EG], [3]), ALU.add))
            for t in range(n):
                ins = dve.max(top[:, t], sel[:, t])
            then(ins)
            for t in range(n):
                ins = dve.match_replace(left[:, t], top[:, t], sel[:, t], -3e38)
            then(ins)
            then(dve.tensor_tensor(mask[:], left[:], sel[:], ALU.is_lt))
            dve.tensor_copy(mask_bf[:], mask[:]).then_inc(mask_ready, 1)
            then(dve.tensor_tensor(w[:], s[:], mask[:], ALU.mult))
            then(dve.tensor_reduce(wsum[:], w[:], AX_X, ALU.add))
            then(dve.reciprocal(winv[:], wsum[:]))
            then(dve.tensor_scalar(winv[:], winv[:], ROUTED_SCALE, None, ALU.mult))
            then(dve.tensor_tensor(w[:], w[:], bc(winv[:], [P, n, E], [2]), ALU.mult))
            dve.wait_ge(made, 6)
            then(dve.tensor_copy(block_no[:], block_no_i[:]))
            dve.wait_ge(ranks_ready, 1)
            then(dve.tensor_scalar(nblk[:], counts[:], 0.0, None, ALU.is_gt))
            for m in range(1, n):
                then(dve.scalar_tensor_tensor(nblk[:], counts[:], float(m * P), nblk[:], ALU.is_gt, ALU.add))
            then(dve.tensor_tensor_scan(end[:], ones[:], nblk[:], 0.0, ALU.mult, ALU.add))
            then(dve.tensor_tensor(start[:], end[:], nblk[:], ALU.subtract))
            then(dve.tensor_scalar(start[:], start[:], float(P), 1.0, ALU.mult, ALU.add))
            then(dve.tensor_tensor(pos[:], ranks[:], bc(start[:], [P, n, E], [1]), ALU.add))
            then(dve.tensor_tensor(pos[:], pos[:], mask[:], ALU.mult))
            for t in range(n):
                ins = dve.max(top_slot[:, t], pos[:, t])
            then(ins)
            then(dve.tensor_scalar(book.slot[:], top_slot[:], -1.0, None, ALU.add))
            dve.sem_inc(slots_ready, 1)
            then(dve.tensor_scalar(junk[:], end[:], block_no[:, 0:1], None, ALU.is_le))
            then(dve.tensor_reduce(below[:], junk[:], AX_X, ALU.add))
            then(dve.tensor_scalar(expert_f[:], below[:], float(E - 1), None, ALU.min))
            then(dve.tensor_copy(expert_i[:], expert_f[:]))
            dve.sem_inc(expert_ready, 1)
            then(dve.tensor_scalar(pairs_f[:], end[:, E - 1:E], 0.5, -0.75, ALU.mult, ALU.add))
            then(dve.tensor_copy(book.last_pair[:], pairs_f[:]))
            for t in range(n):
                for j in range(TOPK):
                    then(dve.scalar_tensor_tensor(junk[:], pos[:, t], top_slot[:, t, j:j + 1], w[:, t], ALU.is_equal, ALU.mult,
                                                  accum_out=book.weight[:, t, j:j + 1]))


def experts(k, ident, layer, book, h_dram, y_dram):
    nc, a = k.nc, k.a
    K2 = FF // P
    with ExitStack() as ctx:
        w_gu = k.sb(ctx, "w_gu", [P, 2, KD, 2 * FF])
        w_down = k.sb(ctx, "w_down", [P, 2, K2, D])
        idx = k.sb(ctx, "idx", [P, 2], U32)
        rows = k.sb(ctx, "rows", [P, 2, D])
        xT = k.sb(ctx, "xT", [P, 2, D])
        act_g = k.sb(ctx, "act_g", [P, 2, FF])
        prod = k.sb(ctx, "prod", [P, 2, FF])
        prodT = k.sb(ctx, "prodT", [P, 2, FF])
        y = k.sb(ctx, "y", [P, 2, D])
        bank = k.ps(ctx, "bank", [P, 8, NC])
        turn_ps = bank[:, 0:2].rearrange("p b n -> p (b n)")
        gu_ps = [bank[:, 2], bank[:, 3]]
        small_ps = [bank[:, 4, 0:FF], bank[:, 5, 0:FF]]
        y_ps = bank[:, 6:8].rearrange("p b n -> p (b n)")
        gu_in = [k.sem("gu_in0"), k.sem("gu_in1")]
        down_in = [k.sem("down_in0"), k.sem("down_in1")]
        idx_in = [k.sem("idx_in0"), k.sem("idx_in1")]
        rows_in = [k.sem("rows_in0"), k.sem("rows_in1")]
        y_out = [k.sem("y_out0"), k.sem("y_out1")]
        passed = k.sem("passed")
        turned, xT_ready, gu_done, silu_ready, prod_ready = (k.sem(x) for x in ("turned", "xT_ready", "gu_done", "silu_ready", "prod_ready"))
        prod_turned, prodT_ready, y_done, y_ready = (k.sem(x) for x in ("prod_turned", "prodT_ready", "y_done", "y_ready"))
        block = ctx.enter_context(nc.Block())
        gu_w = a["exp_w_gu"][layer].rearrange("e (k p) n -> e p k n", p=P)
        down_w = a["exp_w_down"][layer].rearrange("e (k p) n -> e p k n", p=P)

        OPEN = 2
        table = book.table_dram.rearrange("(b p) o -> b p o", p=P)
        y_rows = y_dram.rearrange("(b p) d -> b p d", p=P)

        def done(b):
            return b + 1 + OPEN

        def before(b):
            return b + OPEN

        def free(b):
            return b + 1

        def last_pair(eng):
            return eng.value_load(book.last_pair[0:1, 0:1], min_val=1, max_val=book.blocks // 2 - 1)

        @block.sync
        def _(sp):
            last = last_pair(sp)
            with sp.Fori(0, last + 1) as i:
                for j in range(2):
                    b = 2 * i + j
                    e = sp.value_load(book.expert_dram[bass.ds(b, 1), :], min_val=0, max_val=E - 1)
                    sp.wait_ge(gu_done, free(b))
                    sp.dma_start(w_gu[:, j], gu_w[bass.ds(e, 1)].rearrange("o p k n -> p (o k) n")).then_inc(gu_in[j], 16)
                    sp.wait_ge(y_done, free(b))
                    sp.dma_start(w_down[:, j], down_w[bass.ds(e, 1)].rearrange("o p k n -> p (o k) n")).then_inc(down_in[j], 16)

        @block.gpsimd
        def _(pool):
            last = last_pair(pool)
            with pool.Fori(0, last + 1) as i:
                for j in range(2):
                    b = 2 * i + j
                    pool.wait_ge(turned, free(b))
                    pool.dma_start(idx[:, j:j + 1], table[bass.ds(b, 1)].rearrange("o p x -> p (o x)")).then_inc(idx_in[j], 16)
                    pool.wait_ge(idx_in[j], 16 * (i + 1))
                    pool.sem_inc(passed, 1)
                    pool.indirect_dma_start(rows[:, j], None, h_dram,
                                            bass.IndirectOffsetOnAxis(ap=idx[:, j:j + 1], axis=0)).then_inc(rows_in[j], 16)

        @block.tensor
        def _(pe):
            last = last_pair(pe)
            for s_ in (turned, gu_done, prod_turned, y_done):
                pe.sem_inc(s_, OPEN)

            def turn_rows(i, j):
                b = 2 * i + j
                pe.wait_ge(rows_in[j], 16 * (i + 1))
                pe.wait_ge(xT_ready, before(b))
                for kk in range(KD):
                    mm = pe.transpose(turn_ps[:, kk * P:(kk + 1) * P], rows[:, j, kk * P:(kk + 1) * P], ident[:])
                mm.then_inc(turned, 1)

            def gate_up(i, j):
                b = 2 * i + j
                pe.wait_ge(gu_in[j], 16 * (i + 1))
                pe.wait_ge(xT_ready, done(b))
                pe.wait_ge(prod_ready, free(b))
                for kk in range(KD):
                    mm = pe.matmul(gu_ps[j], xT[:, j, kk * P:(kk + 1) * P], w_gu[:, j, kk, :], start=(kk == 0), stop=(kk == KD - 1))
                mm.then_inc(gu_done, 1)

            def turn_prod(i, j):
                b = 2 * i + j
                pe.wait_ge(prod_ready, done(b))
                pe.wait_ge(prodT_ready, free(b))
                for kk in range(K2):
                    mm = pe.transpose(small_ps[j][:, kk * P:(kk + 1) * P], prod[:, j, kk * P:(kk + 1) * P], ident[:])
                mm.then_inc(prod_turned, 1)

            def down(i, j):
                b = 2 * i + j
                pe.wait_ge(down_in[j], 16 * (i + 1))
                pe.wait_ge(prodT_ready, done(b))
                pe.wait_ge(y_ready, before(b))
                for half in range(2):
                    for kk in range(K2):
                        mm = pe.matmul(y_ps[:, half * NC:(half + 1) * NC], prodT[:, j, kk * P:(kk + 1) * P],
                                       w_down[:, j, kk, half * NC:(half + 1) * NC], start=(kk == 0), stop=(kk == K2 - 1))
                mm.then_inc(y_done, 1)

            turn_rows(0, 0)
            gate_up(0, 0)
            turn_rows(0, 1)
            with pe.Fori(0, last) as i:
                for j in range(2):
                    turn_prod(i, j)
                    turn_rows(i + 1, j)
                    gate_up(i + j, 1 - j)
                    down(i, j)
            turn_prod(last, 0)
            gate_up(last, 1)
            down(last, 0)
            turn_prod(last, 1)
            down(last, 1)

        @block.scalar
        def _(act):
            last = last_pair(act)
            act.sem_inc(xT_ready, OPEN)
            act.sem_inc(silu_ready, OPEN)
            act.sem_inc(y_out[0], 16)
            act.sem_inc(y_out[1], 16)

            def copy_xT(i, j):
                b = 2 * i + j
                act.wait_ge(turned, done(b))
                act.wait_ge(gu_done, free(b))
                act.activation(xT[:, j], turn_ps, ACT.Copy).then_inc(xT_ready, 1)

            def silu(i, j):
                b = 2 * i + j
                act.wait_ge(gu_done, done(b))
                act.wait_ge(prod_ready, free(b))
                act.activation(act_g[:, j], gu_ps[j][:, 0:FF], ACT.Silu).then_inc(silu_ready, 1)

            def store(i, j):
                b = 2 * i + j
                act.wait_ge(y_ready, done(b))
                act.dma_start(y_rows[bass.ds(b, 1)].rearrange("o p d -> p (o d)"), y[:, j]).then_inc(y_out[j], 16)

            copy_xT(0, 0)
            silu(0, 0)
            copy_xT(0, 1)
            with act.Fori(0, last) as i:
                for j in range(2):
                    copy_xT(i + 1, j)
                    silu(i + j, 1 - j)
                    store(i, j)
            silu(last, 1)
            store(last, 0)
            store(last, 1)
            for j in range(2):
                act.wait_ge(y_out[j], 16 * (last + 2))
                act.sem_inc(passed, 1)

        @block.vector
        def _(dve):
            last = last_pair(dve)
            for s_ in (prod_ready, prodT_ready, y_ready):
                dve.sem_inc(s_, OPEN)

            def multiply(i, j):
                b = 2 * i + j
                dve.wait_ge(silu_ready, done(b))
                dve.wait_ge(prod_turned, free(b))
                dve.tensor_tensor(prod[:, j], act_g[:, j], gu_ps[j][:, FF:2 * FF], ALU.mult).then_inc(prod_ready, 1)

            def finish(i, j, nxt=None):
                b = 2 * i + j
                dve.wait_ge(prod_turned, done(b))
                dve.wait_ge(y_done, free(b))
                dve.tensor_copy(prodT[:, j], small_ps[j]).then_inc(prodT_ready, 1)
                if nxt:
                    multiply(*nxt)
                dve.wait_ge(y_done, done(b))
                dve.wait_ge(y_out[j], 16 * (i + 1))
                dve.tensor_copy(y[:, j], y_ps).then_inc(y_ready, 1)

            multiply(0, 0)
            with dve.Fori(0, last) as i:
                for j in range(2):
                    finish(i, j, (i + j, 1 - j))
            finish(last, 0, (last, 1))
            finish(last, 1)


def combine(k, ident, layer, hT, x_sb, tiles, book, y_dram, mod_dram):
    nc, a = k.nc, k.a
    n = len(tiles)
    K2 = FF // P
    RING = 4
    streams = sorted({int(t >= TC) for t in tiles})
    with ExitStack() as ctx:
        w_gu = k.sb(ctx, "sh_gu", [P, KD, 2 * FF])
        w_down = k.sb(ctx, "sh_down", [P, K2, D])
        gate = k.sb(ctx, "gate", [P, 2, D])
        act_g = k.sb(ctx, "act_g", [P, 2, FF])
        prod = k.sb(ctx, "prod", [P, 2, FF])
        prodT = k.sb(ctx, "prodT", [P, 2, FF])
        picked = k.sb(ctx, "picked", [P, RING, D])
        acc = k.sb(ctx, "acc", [P, D])
        bank = k.ps(ctx, "bank", [P, 8, NC])
        gu_ps = [bank[:, 0], bank[:, 1]]
        turn_ps = [bank[:, 2, 0:FF], bank[:, 3, 0:FF]]
        y_ps = [bank[:, 4:6].rearrange("p b n -> p (b n)"), bank[:, 6:8].rearrange("p b n -> p (b n)")]
        gu_in, down_in, gate_in = k.sem("gu_in"), k.sem("down_in"), k.sem("gate_in")
        picked_in = [k.sem(f"picked_in{j}") for j in range(RING)]
        gu_done, silu_ready, prod_ready, prod_turned, prodT_ready, y_done = (
            k.sem(x) for x in ("gu_done", "silu_ready", "prod_ready", "prod_turned", "prodT_ready", "y_done"))
        added, x_ready, step = k.sem("added"), k.sem("x_ready"), k.sem("step")
        block = ctx.enter_context(nc.Block())

        @block.sync
        def _(sp):
            sp.dma_start(w_gu[:], a["sh_w_gu"][layer].rearrange("(k p) n -> p k n", p=P)).then_inc(gu_in, 16)
            sp.dma_start(w_down[:], a["sh_w_down"][layer].rearrange("(k p) n -> p k n", p=P)).then_inc(down_in, 16)
            for s in streams:
                sp.dma_start(gate[:, s], mod_dram[s, layer][5 * D:6 * D].partition_broadcast(P)).then_inc(gate_in, 16)

        @block.gpsimd
        def _(pool):
            for t in range(n):
                for j in range(TOPK):
                    m = t * TOPK + j
                    if m >= RING:
                        pool.wait_ge(added, m - RING + 1)
                    pool.indirect_dma_start(picked[:, m % RING], None, y_dram,
                                            bass.IndirectOffsetOnAxis(ap=book.slot[:, t, j:j + 1], axis=0)).then_inc(picked_in[m % RING], 16)

        @block.tensor
        def _(pe):
            def gate_up(t):
                if t >= 2:
                    pe.wait_ge(prod_ready, t - 1)
                for kk in range(KD):
                    mm = pe.matmul(gu_ps[t % 2], hT[:, kk, t * P:(t + 1) * P], w_gu[:, kk, :], start=(kk == 0), stop=(kk == KD - 1))
                mm.then_inc(gu_done, 1)

            pe.wait_ge(gu_in, 16)
            gate_up(0)
            for t in range(n):
                if t + 1 < n:
                    gate_up(t + 1)
                pe.wait_ge(prod_ready, t + 1)
                if t >= 2:
                    pe.wait_ge(prodT_ready, t - 1)
                for kk in range(K2):
                    mm = pe.transpose(turn_ps[t % 2][:, kk * P:(kk + 1) * P], prod[:, t % 2, kk * P:(kk + 1) * P], ident[:])
                mm.then_inc(prod_turned, 1)
                pe.wait_ge(prodT_ready, t + 1)
                if t == 0:
                    pe.wait_ge(down_in, 16)
                if t >= 2:
                    pe.wait_ge(x_ready, t - 1)
                for half in range(2):
                    for kk in range(K2):
                        mm = pe.matmul(y_ps[t % 2][:, half * NC:(half + 1) * NC], prodT[:, t % 2, kk * P:(kk + 1) * P],
                                       w_down[:, kk, half * NC:(half + 1) * NC], start=(kk == 0), stop=(kk == K2 - 1))
                mm.then_inc(y_done, 1)

        @block.scalar
        def _(act):
            def copy_prodT(t):
                act.wait_ge(prod_turned, t + 1)
                if t >= 2:
                    act.wait_ge(y_done, t - 1)
                act.activation(prodT[:, t % 2], turn_ps[t % 2], ACT.Copy).then_inc(prodT_ready, 1)

            for t in range(n):
                act.wait_ge(gu_done, t + 1)
                if t >= 2:
                    act.wait_ge(prod_ready, t - 1)
                act.activation(act_g[:, t % 2], gu_ps[t % 2][:, 0:FF], ACT.Silu).then_inc(silu_ready, 1)
                if t >= 1:
                    copy_prodT(t - 1)
            copy_prodT(n - 1)

        @block.vector
        def _(dve):
            count = [0]

            def then(ins):
                count[0] += 1
                ins.then_inc(step, 1)
                dve.wait_ge(step, count[0])

            def multiply(t):
                dve.wait_ge(silu_ready, t + 1)
                if t >= 2:
                    dve.wait_ge(prod_turned, t - 1)
                dve.tensor_tensor(prod[:, t % 2], act_g[:, t % 2], gu_ps[t % 2][:, FF:2 * FF], ALU.mult).then_inc(prod_ready, 1)

            multiply(0)
            dve.wait_ge(gate_in, 16 * len(streams))
            for i, t in enumerate(tiles):
                if i + 1 < n:
                    multiply(i + 1)
                for j in range(TOPK):
                    m = i * TOPK + j
                    dve.wait_ge(picked_in[m % RING], 16 * (m // RING + 1))
                    pick, weight = picked[:, m % RING], book.weight[:, i, j:j + 1]
                    if j == 0:
                        dve.tensor_scalar(acc[:], pick, weight, None, ALU.mult).then_inc(added, 1)
                    else:
                        dve.scalar_tensor_tensor(acc[:], pick, weight, acc[:], ALU.mult, ALU.add).then_inc(added, 1)
                    dve.wait_ge(added, m + 1)
                dve.wait_ge(y_done, i + 1)
                then(dve.tensor_tensor(acc[:], y_ps[i % 2], acc[:], ALU.add))
                then(dve.tensor_tensor(acc[:], acc[:], gate[:, int(t >= TC)], ALU.mult))
                then(dve.tensor_tensor(x_sb[:, t], x_sb[:, t], acc[:], ALU.add))
                dve.sem_inc(x_ready, 1)


class Book:

    def __init__(self, k, ctx, name, n):
        self.blocks = n * P * TOPK // P + E
        nc = k.nc
        self.slot = k.sb(ctx, "slot", [P, n, TOPK], U32)
        self.weight = k.sb(ctx, "weight", [P, n, TOPK])
        self.last_pair = k.sb(ctx, "last_pair", [P, 1], I32)
        self.table_dram = nc.dram_tensor(f"table_{name}", [self.blocks * P, 1], U32).ap()
        self.expert_dram = nc.dram_tensor(f"expert_{name}", [P, 1], I32).ap()


def expert_layer(k, ident, layer, x_sb, tiles, mod_dram, y_dram):
    nc = k.nc
    n = len(tiles)
    with ExitStack() as ctx:
        hT = k.sb(ctx, "hT", [P, KD, n * P])
        book = Book(k, ctx, str(layer), n)
        h_dram = nc.dram_tensor(f"h_{layer}", [n * P, D], F32).ap()
        norm_modulate(k, ident, layer, 3, k.a["norm_ffn"][layer], mod_dram, tiles, x_sb=x_sb, hT=hT, h_dram=h_dram)
        route(k, ident, layer, hT, tiles, book)
        experts(k, ident, layer, book, h_dram, y_dram)
        combine(k, ident, layer, hT, x_sb, tiles, book, y_dram, mod_dram)

def rotate(eng, then, dst, src, cos, sin, tmp):
    then(eng.tensor_tensor(tmp, src, cos, ALU.mult))
    for b in range(2):
        then(eng.tensor_tensor(dst[:, :, :, b], src[:, :, :, 1 - b], sin[:, :, :, b], ALU.mult))
    then(eng.tensor_tensor(dst, dst, tmp, ALU.add))


def latent_down(k, ident, hT, qaT, kvaT, krT):
    nc, a, c = k.nc, k.a, k.c
    MLA_IN = QR + KVR + ROPE
    with ExitStack() as ctx:
        w = k.sb(ctx, "w_in", [P, KD, MLA_IN])
        gq = k.sb(ctx, "gq", [P, QR])
        gkv = k.sb(ctx, "gkv", [P, KVR])
        gkr = k.sb(ctx, "gkr", [P, ROPE])
        cos = k.sb(ctx, "cos", [P, TL, 2, 2, ROPE // 4])
        sin = k.sb(ctx, "sin", [P, TL, 2, 2, ROPE // 4])
        low = k.sb(ctx, "low", [P, T, MLA_IN])
        kr = k.sb(ctx, "kr", [P, T, ROPE])
        krt = k.sb(ctx, "krt", [P, TL, ROPE])
        krr = k.sb(ctx, "krr", [P, TL, ROPE])
        square = k.sb(ctx, "square", [P, QR])
        S = TL + 2 * T
        ms, mse, root, rinv = (k.sb(ctx, x, [P, S]) for x in ("ms", "mse", "root", "rinv"))
        bank = k.ps(ctx, "bank", [P, 8, NC])
        turn_ps = [bank[:, 4:6].rearrange("p b n -> p (b n)"), bank[:, 6:8].rearrange("p b n -> p (b n)")]
        w_in, rows_in = k.sem("w_in"), k.sem("rows_in")
        product, copied, squared = k.sem("product"), k.sem("copied"), k.sem("squared")
        ms_ready, root_ready, step, tile_ready, tile_turned, tile_out = (
            k.sem(x) for x in ("ms_ready", "root_ready", "step", "tile_ready", "tile_turned", "tile_out"))
        items = []
        for t in range(T):
            items.append((t, t % 2, slice(QR, MLA_IN)))
            if t >= TC:
                items.append((t, 2 + t % 2, slice(0, QR)))
        last_user = {}
        block = ctx.enter_context(nc.Block())

        @block.sync
        def _(sp):
            for half in range(2):
                ks = slice(half * KD // 2, (half + 1) * KD // 2)
                sp.dma_start(w[:, ks], a["mla_w_in"][0].rearrange("(k p) n -> p k n", p=P)[:, ks]).then_inc(w_in, 16)
            sp.dma_start(gq[:], a["mla_q_a_norm"][0].partition_broadcast(P)).then_inc(rows_in, 16)
            sp.dma_start(gkv[:], a["mla_kv_a_norm"][0].partition_broadcast(P)).then_inc(rows_in, 16)
            sp.dma_start(gkr[:], a["mla_k_norm"][0, NOPE:QK].partition_broadcast(P)).then_inc(rows_in, 16)
            sp.dma_start(cos[:], c["mla_cos"].rearrange("p (t a b n) -> p t a b n", t=TL, a=2, b=2)).then_inc(rows_in, 16)
            sp.dma_start(sin[:], c["mla_sin"].rearrange("p (t a b n) -> p t a b n", t=TL, a=2, b=2)).then_inc(rows_in, 16)

        @block.tensor
        def _(pe):
            pe.wait_ge(w_in, 32)
            for m, (t, b, cols) in enumerate(items):
                if b in last_user:
                    pe.wait_ge(copied, last_user[b] + 1)
                last_user[b] = m
                for kk in range(KD):
                    mm = pe.matmul(bank[:, b, 0:cols.stop - cols.start], hT[:, kk, t * P:(t + 1) * P], w[:, kk, cols],
                                   start=(kk == 0), stop=(kk == KD - 1))
                mm.then_inc(product, 1)
            for t in range(T):
                pe.wait_ge(tile_ready, t + 1)
                if t >= 2:
                    pe.wait_ge(tile_out, t - 1)
                for j in range(0 if t >= TC else 3, 5):
                    pe.transpose(turn_ps[t % 2][:, j * P:(j + 1) * P], low[:, t, j * P:(j + 1) * P], ident[:])
                pe.transpose(turn_ps[t % 2][0:ROPE, 5 * P:6 * P], kr[:, t], ident[:]).then_inc(tile_turned, 1)

        @block.scalar
        def _(act):
            for m, (t, b, cols) in enumerate(items):
                act.wait_ge(copied, m + 1)
                if m:
                    act.wait_ge(squared, m)
                parts = [(0, QR, t - TC)] if b >= 2 else [(0, KVR, TL + t), (KVR, KVR + ROPE, TL + T + t)]
                for n, (lo, hi, col) in enumerate(parts):
                    ins = act.activation(square[:, 0:hi - lo] if not n else square[:, KVR:KVR + ROPE], low[:, t, cols.start + lo:cols.start + hi], ACT.Square,
                                         accum_out=ms[:, col:col + 1])
                ins.then_inc(squared, 1)
            act.wait_ge(ms_ready, 1)
            act.activation(root[:], mse[:], ACT.Sqrt).then_inc(root_ready, 1)
            for t in range(T):
                at = slice(t * P, (t + 1) * P)
                act.wait_ge(tile_turned, t + 1)
                ps = turn_ps[t % 2]
                if t >= TC:
                    act.activation(qaT[:, :, (t - TC) * P:(t - TC + 1) * P], ps[:, 0:3 * P].rearrange("p (k m) -> p k m", k=3), ACT.Copy)
                act.activation(kvaT[:, :, at], ps[:, 3 * P:5 * P].rearrange("p (k m) -> p k m", k=2), ACT.Copy)
                act.activation(krT[0:ROPE, at], ps[0:ROPE, 5 * P:6 * P], ACT.Copy).then_inc(tile_out, 1)

        @block.vector
        def _(dve):
            count = [0]

            def then(ins):
                count[0] += 1
                ins.then_inc(step, 1)
                dve.wait_ge(step, count[0])

            for m, (t, b, cols) in enumerate(items):
                dve.wait_ge(product, m + 1)
                dve.tensor_copy(low[:, t, cols], bank[:, b, 0:cols.stop - cols.start]).then_inc(copied, 1)
            dve.wait_ge(squared, len(items))
            dve.wait_ge(copied, len(items))
            for lo, hi, width in ((0, TL, QR), (TL, TL + T, KVR), (TL + T, S, ROPE)):
                then(dve.tensor_scalar(mse[:, lo:hi], ms[:, lo:hi], 1.0 / width, EPS, ALU.mult, ALU.add))
            dve.sem_inc(ms_ready, 1)
            dve.wait_ge(root_ready, 1)
            then(dve.reciprocal(rinv[:], root[:]))
            dve.wait_ge(rows_in, 80)
            for t in range(T):
                col = TL + T + t
                then(dve.scalar_tensor_tensor(kr[:, t], low[:, t, QR + KVR:MLA_IN], rinv[:, col:col + 1], gkr[:], ALU.mult, ALU.mult))
            split = "p t (a b n) -> p t a b n"
            rotate(dve, then, krr[:].rearrange(split, a=2, b=2), kr[:, TC:T].rearrange(split, a=2, b=2), cos[:], sin[:],
                   krt[:].rearrange(split, a=2, b=2))
            then(dve.tensor_copy(kr[:, TC:T], krr[:]))
            for t in range(T):
                if t >= TC:
                    dve.scalar_tensor_tensor(low[:, t, 0:QR], low[:, t, 0:QR], rinv[:, t - TC:t - TC + 1], gq[:], ALU.mult, ALU.mult)
                col = TL + t
                dve.scalar_tensor_tensor(low[:, t, QR:QR + KVR], low[:, t, QR:QR + KVR], rinv[:, col:col + 1], gkv[:],
                                         ALU.mult, ALU.mult).then_inc(tile_ready, 1)


def latent_up(k, qaT, kvaT, q_sb, kv_sb, rq, rk):
    nc, a = k.nc, k.a
    KQ, KK = QR // P, KVR // P
    with ExitStack() as ctx:
        wq = k.sb(ctx, "wq", [P, KQ, MH * QK])
        wkv = k.sb(ctx, "wkv", [P, KK, MH * (NOPE + MV)])
        square = k.sb(ctx, "square", [P, 2, MH * QK])
        msq, rootq = k.sb(ctx, "msq", [P, TL, MH, 2]), k.sb(ctx, "rootq", [P, TL, MH, 2])
        msk, rootk = k.sb(ctx, "msk", [P, T, MH]), k.sb(ctx, "rootk", [P, T, MH])
        bank = k.ps(ctx, "bank", [P, 2, 4 * NC])
        wq_in, wkv_in = k.sem("wq_in"), k.sem("wkv_in")
        product, copied, squared, reduced = k.sem("product"), k.sem("copied"), k.sem("squared"), k.sem("reduced")
        mean_ready, root_ready, step = k.sem("mean_ready"), k.sem("root_ready"), k.sem("step")
        items = [("q", t) for t in range(TL)] + [("kv", t) for t in range(T)]
        block = ctx.enter_context(nc.Block())

        @block.sync
        def _(sp):
            sp.dma_start(wq[:], a["mla_w_q_b"][0].rearrange("(k p) n -> p k n", p=P)).then_inc(wq_in, 16)
            sp.dma_start(wkv[:], a["mla_w_kv_b"][0].rearrange("(k p) n -> p k n", p=P)).then_inc(wkv_in, 16)

        @block.tensor
        def _(pe):
            for m, (what, t) in enumerate(items):
                if m == 0:
                    pe.wait_ge(wq_in, 16)
                if m == TL:
                    pe.wait_ge(wkv_in, 16)
                if m >= 2:
                    pe.wait_ge(copied, m - 1)
                x, w, kt = (qaT, wq, KQ) if what == "q" else (kvaT, wkv, KK)
                for n in range(w.shape[2] // NC):
                    for kk in range(kt):
                        mm = pe.matmul(bank[:, m % 2, n * NC:(n + 1) * NC], x[:, kk, t * P:(t + 1) * P], w[:, kk, n * NC:(n + 1) * NC],
                                       start=(kk == 0), stop=(kk == kt - 1))
                mm.then_inc(product, 1)

        @block.scalar
        def _(act):
            for m, (what, t) in enumerate(items):
                act.wait_ge(copied, m + 1)
                if m >= 2:
                    act.wait_ge(reduced, m - 1)
                if what == "q":
                    ins = act.activation(square[:, m % 2], q_sb[:, t], ACT.Square)
                else:
                    ins = act.activation(square[:, m % 2, 0:MH * NOPE].rearrange("p (h n) -> p h n", h=MH),
                                         kv_sb[:, t].rearrange("p (h n) -> p h n", h=MH)[:, :, 0:NOPE], ACT.Square)
                ins.then_inc(squared, 1)
            act.wait_ge(mean_ready, 1)
            act.activation(rootq[:], msq[:], ACT.Sqrt).then_inc(root_ready, 1)
            act.activation(rootk[:], msk[:], ACT.Sqrt).then_inc(root_ready, 1)

        @block.vector
        def _(dve):
            count = [0]

            def then(ins):
                count[0] += 1
                ins.then_inc(step, 1)
                dve.wait_ge(step, count[0])

            for m, (what, t) in enumerate(items):
                dve.wait_ge(product, m + 1)
                if what == "q":
                    dve.tensor_copy(q_sb[:, t], bank[:, m % 2, 0:MH * QK]).then_inc(copied, 1)
                    dve.wait_ge(squared, m + 1)
                    sq = square[:, m % 2].rearrange("p (h n) -> p h n", h=MH)
                    dve.tensor_reduce(msq[:, t, :, 0], sq[:, :, 0:NOPE], AX_X, ALU.add)
                    dve.tensor_reduce(msq[:, t, :, 1], sq[:, :, NOPE:QK], AX_X, ALU.add).then_inc(reduced, 1)
                else:
                    dve.tensor_copy(kv_sb[:, t], bank[:, m % 2]).then_inc(copied, 1)
                    dve.wait_ge(squared, m + 1)
                    dve.tensor_reduce(msk[:, t], square[:, m % 2, 0:MH * NOPE].rearrange("p (h n) -> p h n", h=MH), AX_X,
                                      ALU.add).then_inc(reduced, 1)
            dve.wait_ge(reduced, len(items))
            then(dve.tensor_scalar(msq[:, :, :, 0], msq[:, :, :, 0], 1.0 / NOPE, EPS, ALU.mult, ALU.add))
            then(dve.tensor_scalar(msq[:, :, :, 1], msq[:, :, :, 1], 1.0 / ROPE, EPS, ALU.mult, ALU.add))
            then(dve.tensor_scalar(msk[:], msk[:], 1.0 / NOPE, EPS, ALU.mult, ALU.add))
            dve.sem_inc(mean_ready, 1)
            dve.wait_ge(root_ready, 2)
            dve.reciprocal(rq[:], rootq[:])
            dve.reciprocal(rk[:], rootk[:])


def attention(k, ident, q_sb, kv_sb, rq, rk, krT, oT):
    nc, a, c = k.nc, k.a, k.c
    NK = T * P
    with ExitStack() as ctx:
        gqn, gqr, gkn = k.sb(ctx, "gqn", [P, NOPE]), k.sb(ctx, "gqr", [P, ROPE]), k.sb(ctx, "gkn", [P, NOPE])
        cos = k.sb(ctx, "cos", [P, TL, 2, 2, ROPE // 4])
        sin = k.sb(ctx, "sin", [P, TL, 2, 2, ROPE // 4])
        qn, qr = k.sb(ctx, "qn", [P, 2, TL, NOPE]), k.sb(ctx, "qr", [P, 2, TL, ROPE])
        qx, qt = k.sb(ctx, "qx", [P, TL, ROPE]), k.sb(ctx, "qt", [P, TL, ROPE])
        kn, vh = k.sb(ctx, "kn", [P, 2, T, NOPE]), k.sb(ctx, "vh", [P, 2, T, MV])
        qnT, qrT = k.sb(ctx, "qnT", [P, 2, SEQ]), k.sb(ctx, "qrT", [ROPE, 2, SEQ])
        knT = k.sb(ctx, "knT", [P, 2, NK])
        top, ntop = k.sb(ctx, "top", [P, 2]), k.sb(ctx, "ntop", [P, 2])
        total, inv = k.sb(ctx, "total", [P, 2]), k.sb(ctx, "inv", [P, 2])
        probs = k.sb(ctx, "probs", [P, 2, NK])
        probsT = k.sb(ctx, "probsT", [P, 2, T, SEQ])
        bank = k.ps(ctx, "bank", [P, 8, NC])
        score_ps = [bank[:, 0:2].rearrange("p b n -> p (b n)")[:, 0:NK], bank[:, 2:4].rearrange("p b n -> p (b n)")[:, 0:NK]]
        probT_ps = bank[:, 4:6].rearrange("p b n -> p (b n)")[:, 0:NK]
        out_ps = bank[:, 6]
        head_ps = bank[:, 7]
        rows_in = k.sem("rows_in")
        passed = k.sem("passed")
        step, staged, head_turned, head_out = k.sem("step"), k.sem("staged"), k.sem("head_turned"), k.sem("head_out")
        scored, top_ready, exp_ready, probs_ready, probs_turned, probsT_ready = (
            k.sem(x) for x in ("scored", "top_ready", "exp_ready", "probs_ready", "probs_turned", "probsT_ready"))
        top_step, inv_step, attended, oT_ready = k.sem("top_step"), k.sem("inv_step"), k.sem("attended"), k.sem("oT_ready")
        block = ctx.enter_context(nc.Block())
        OPEN, R = 2, 4

        def heads(h):
            return h + 1 + OPEN

        def units(h, i):
            return TL * (h + OPEN) + i + 1

        @block.sync
        def _(sp):
            sp.dma_start(gqn[:], a["mla_q_norm"][0, 0:NOPE].partition_broadcast(P)).then_inc(rows_in, 16)
            sp.dma_start(gqr[:], a["mla_q_norm"][0, NOPE:QK].partition_broadcast(P)).then_inc(rows_in, 16)
            sp.dma_start(gkn[:], a["mla_k_norm"][0, 0:NOPE].partition_broadcast(P)).then_inc(rows_in, 16)
            sp.dma_start(cos[:], c["mla_cos"].rearrange("p (t a b n) -> p t a b n", t=TL, a=2, b=2)).then_inc(rows_in, 16)
            sp.dma_start(sin[:], c["mla_sin"].rearrange("p (t a b n) -> p t a b n", t=TL, a=2, b=2)).then_inc(rows_in, 16)

        @block.gpsimd
        def _(pool):
            pool.sem_inc(staged, OPEN)
            pool.wait_ge(rows_in, 80)
            q_h = q_sb[:].rearrange("p t (h n) -> p t h n", h=MH)
            kv_h = kv_sb[:].rearrange("p t (h n) -> p t h n", h=MH)
            STEPS = 9

            with pool.Fori(0, MH // 2) as i:
                for j in range(2):
                    h = 2 * i + j
                    made = [0]

                    def then(ins):
                        made[0] += 1
                        ins.then_inc(step, 1)
                        pool.wait_ge(step, STEPS * h + made[0])

                    def head(x, lo, hi):
                        return x[:, :, bass.ds(h, 1), lo:hi].rearrange("p t o n -> p t (o n)")

                    pool.wait_ge(head_turned, R * (h + 1))
                    pool.wait_ge(attended, h + 1)
                    then(pool.tensor_copy(vh[:, j], head(kv_h, NOPE, NOPE + MV)))
                    then(pool.tensor_tensor(kn[:, j], head(kv_h, 0, NOPE), rk[:, :, bass.ds(h, 1)].broadcast_to([P, T, NOPE]), ALU.mult))
                    then(pool.tensor_tensor(kn[:, j], kn[:, j], bc(gkn[:], [P, T, NOPE], [1]), ALU.mult))
                    then(pool.tensor_tensor(qn[:, j], head(q_h, 0, NOPE), rq[:, :, bass.ds(h, 1), 0].broadcast_to([P, TL, NOPE]), ALU.mult))
                    then(pool.tensor_tensor(qn[:, j], qn[:, j], bc(gqn[:], [P, TL, NOPE], [1]), ALU.mult))
                    then(pool.tensor_tensor(qx[:], head(q_h, NOPE, QK), rq[:, :, bass.ds(h, 1), 1].broadcast_to([P, TL, ROPE]), ALU.mult))
                    then(pool.tensor_tensor(qx[:], qx[:], bc(gqr[:], [P, TL, ROPE], [1]), ALU.mult))
                    split = "p t (a b n) -> p t a b n"
                    x5, d5 = qx[:].rearrange(split, a=2, b=2), qr[:, j].rearrange(split, a=2, b=2)
                    pool.tensor_tensor(qt[:], qx[:], cos[:].rearrange("p t a b n -> p t (a b n)"), ALU.mult)
                    pool.tensor_tensor(d5[:, :, :, 0], x5[:, :, :, 1], sin[:, :, :, 0], ALU.mult)
                    then(pool.tensor_tensor(d5[:, :, :, 1], x5[:, :, :, 0], sin[:, :, :, 1], ALU.mult))
                    then(pool.tensor_tensor(qr[:, j], qr[:, j], qt[:], ALU.add))
                    pool.sem_inc(staged, 1)

        @block.tensor
        def _(pe):
            pe.sem_inc(head_turned, R * OPEN)
            pe.sem_inc(attended, OPEN)
            pe.sem_inc(probs_turned, TL * OPEN)
            pe.sem_inc(scored, TL * OPEN)

            def turn_head(i, j, r):
                h = 2 * i + j
                if r == 0:
                    pe.wait_ge(staged, heads(h))
                pe.wait_ge(head_out, R * (h + OPEN) + r)
                if r == 3:
                    pe.sem_inc(passed, 1)
                if r in (0, 3):
                    src, w = (qn, P) if r == 0 else (qr, ROPE)
                    for t in range(TL):
                        mm = pe.transpose(head_ps[0:w, t * P:(t + 1) * P], src[:, j, t], ident[:])
                else:
                    for n, t in enumerate(range(4) if r == 1 else range(4, T)):
                        mm = pe.transpose(head_ps[:, n * P:(n + 1) * P], kn[:, j, t], ident[:])
                mm.then_inc(head_turned, 1)

            def scores(i, j, t):
                h = 2 * i + j
                if t == 0:
                    pe.wait_ge(head_out, R * heads(h))
                pe.wait_ge(exp_ready, units(h, t) - 2)
                for lo, hi in ((0, NC), (NC, NK)):
                    pe.matmul(score_ps[t % 2][:, lo:hi], qnT[:, j, t * P:(t + 1) * P], knT[:, j, lo:hi], start=True, stop=False)
                    mm = pe.matmul(score_ps[t % 2][:, lo:hi], qrT[:, j, t * P:(t + 1) * P], krT[0:ROPE, lo:hi], start=False, stop=True)
                mm.then_inc(scored, 1)

            def turn_probs(i, j, t):
                h = 2 * i + j
                pe.wait_ge(probs_ready, units(h, t))
                pe.wait_ge(probsT_ready, units(h, t) - 1)
                for n in range(T):
                    mm = pe.transpose(probT_ps[:, n * P:(n + 1) * P], probs[:, t % 2, n * P:(n + 1) * P], ident[:])
                mm.then_inc(probs_turned, 1)

            def values(i, j):
                h = 2 * i + j
                pe.wait_ge(probsT_ready, units(h, TL - 1))
                pe.wait_ge(oT_ready, heads(h) - 1)
                for n in range(T):
                    mm = pe.matmul(out_ps, vh[:, j, n], probsT[:, j, n], start=(n == 0), stop=(n == T - 1))
                mm.then_inc(attended, 1)

            def attend(i, j, nxt):
                if nxt:
                    turn_head(*nxt, 0)
                scores(i, j, 1)
                if nxt:
                    turn_head(*nxt, 1)
                turn_probs(i, j, 0)
                scores(i, j, 2)
                if nxt:
                    turn_head(*nxt, 2)
                turn_probs(i, j, 1)
                scores(i, j, 3)
                if nxt:
                    turn_head(*nxt, 3)
                turn_probs(i, j, 2)
                if nxt:
                    scores(*nxt, 0)
                turn_probs(i, j, 3)
                values(i, j)

            for r in range(R):
                turn_head(0, 0, r)
            scores(0, 0, 0)
            last = MH // 2 - 1
            with pe.Fori(0, last) as i:
                attend(i, 0, (i, 1))
                attend(i, 1, (i + 1, 0))
            attend(last, 0, (last, 1))
            attend(last, 1, None)

        @block.scalar
        def _(act):
            act.sem_inc(head_out, R * OPEN)
            act.sem_inc(exp_ready, TL * OPEN)
            act.sem_inc(probsT_ready, TL * OPEN)
            act.sem_inc(oT_ready, OPEN)

            def copy_head(i, j, r):
                h = 2 * i + j
                act.wait_ge(head_turned, R * (h + OPEN) + r + 1)
                if r == 0:
                    act.wait_ge(scored, units(h, TL - 1) - 2 * TL)
                    act.activation(qnT[:, j], head_ps, ACT.Copy, scale=float(QK) ** -0.5).then_inc(head_out, 1)
                elif r == 1:
                    act.activation(knT[:, j, 0:NC], head_ps, ACT.Copy).then_inc(head_out, 1)
                elif r == 2:
                    act.activation(knT[:, j, NC:NK], head_ps[:, 0:NK - NC], ACT.Copy).then_inc(head_out, 1)
                else:
                    act.activation(qrT[:, j], head_ps[0:ROPE], ACT.Copy, scale=float(QK) ** -0.5).then_inc(head_out, 1)

            def exps(i, j, t):
                h = 2 * i + j
                act.wait_ge(top_ready, units(h, t))
                act.wait_ge(probs_turned, units(h, t) - 2)
                act.activation(probs[:, t % 2], score_ps[t % 2], ACT.Exp, bias=ntop[:, t % 2:t % 2 + 1],
                               accum_out=total[:, t % 2:t % 2 + 1]).then_inc(exp_ready, 1)

            def copy_probs(i, j, t):
                h = 2 * i + j
                act.wait_ge(probs_turned, units(h, t))
                if t == 0:
                    act.wait_ge(attended, heads(h) - 2)
                act.activation(probsT[:, j, :, t * P:(t + 1) * P], probT_ps.rearrange("p (n m) -> p n m", n=T),
                               ACT.Copy).then_inc(probsT_ready, 1)

            def copy_out(i, j):
                h = 2 * i + j
                act.wait_ge(attended, heads(h))
                act.activation(oT[:, bass.ds(h, 1)].rearrange("p o n -> p (o n)"), out_ps, ACT.Copy).then_inc(oT_ready, 1)

            def attend(i, j, nxt):
                if nxt:
                    copy_head(*nxt, 0)
                exps(i, j, 1)
                if nxt:
                    copy_head(*nxt, 1)
                copy_probs(i, j, 0)
                exps(i, j, 2)
                if nxt:
                    copy_head(*nxt, 2)
                copy_probs(i, j, 1)
                exps(i, j, 3)
                if nxt:
                    copy_head(*nxt, 3)
                copy_probs(i, j, 2)
                if nxt:
                    exps(*nxt, 0)
                copy_probs(i, j, 3)
                copy_out(i, j)

            for r in range(R):
                copy_head(0, 0, r)
            exps(0, 0, 0)
            last = MH // 2 - 1
            with act.Fori(0, last) as i:
                attend(i, 0, (i, 1))
                attend(i, 1, (i + 1, 0))
            attend(last, 0, (last, 1))
            attend(last, 1, None)

        @block.vector
        def _(dve):
            dve.sem_inc(top_ready, TL * OPEN)
            dve.sem_inc(probs_ready, TL * OPEN)

            def maximum(h, t):
                n = TL * h + t
                dve.wait_ge(scored, units(h, t))
                dve.tensor_reduce(top[:, t % 2:t % 2 + 1], score_ps[t % 2], AX_X, ALU.max).then_inc(top_step, 1)
                dve.wait_ge(top_step, n + 1)
                dve.tensor_scalar(ntop[:, t % 2:t % 2 + 1], top[:, t % 2:t % 2 + 1], -1.0, None, ALU.mult).then_inc(top_ready, 1)

            def normalise(h, t):
                n = TL * h + t
                dve.wait_ge(exp_ready, units(h, t))
                dve.reciprocal(inv[:, t % 2:t % 2 + 1], total[:, t % 2:t % 2 + 1]).then_inc(inv_step, 1)
                dve.wait_ge(inv_step, n + 1)
                dve.tensor_scalar(probs[:, t % 2], probs[:, t % 2], inv[:, t % 2:t % 2 + 1], None, ALU.mult).then_inc(probs_ready, 1)

            maximum(0, 0)
            with dve.Fori(0, MH - 1) as h:
                for t in range(TL):
                    maximum(h + (t + 1) // TL, (t + 1) % TL)
                    normalise(h, t)
            for t in range(TL):
                if t + 1 < TL:
                    maximum(MH - 1, t + 1)
                normalise(MH - 1, t)


def latent_attention(k, ident, x_sb, mod_dram):
    with ExitStack() as ctx:
        oT = k.sb(ctx, "oT", [P, MH, SEQ])
        with ExitStack() as heads:
            krT = k.sb(heads, "krT", [ROPE, T * P])
            q_sb = k.sb(heads, "q", [P, TL, MH * QK])
            kv_sb = k.sb(heads, "kv", [P, T, MH * (NOPE + MV)])
            rq, rk = k.sb(heads, "rq", [P, TL, MH, 2]), k.sb(heads, "rk", [P, T, MH])
            with ExitStack() as low:
                qaT = k.sb(low, "qaT", [P, QR // P, SEQ])
                kvaT = k.sb(low, "kvaT", [P, KVR // P, T * P])
                with ExitStack() as h:
                    hT = k.sb(h, "hT", [P, KD, T * P])
                    norm_modulate(k, ident, 1, 0, k.a["norm_mix"][1], mod_dram, list(range(T)), x_sb=x_sb, hT=hT)
                    latent_down(k, ident, hT, qaT, kvaT, krT)
                latent_up(k, qaT, kvaT, q_sb, kv_sb, rq, rk)
            attention(k, ident, q_sb, kv_sb, rq, rk, krT, oT)
        project_out(k, oT, MH, k.a["mla_w_o"][0], (1, 2), mod_dram, x_sb, list(range(TC, T)))



def shape_constants():
    out = {"ident": np.eye(P, dtype=np.float32)}

    def angles(rot_dim):
        axis = rot_dim // 2
        inv = (10000.0 ** (-np.arange(0, axis, 2, dtype=np.float32) / axis)).astype(np.float32)
        rows = SEQ // GRID_W
        row = np.repeat(np.arange(rows, dtype=np.float32), GRID_W)
        col = np.tile(np.arange(GRID_W, dtype=np.float32), rows)
        return row[:, None] * inv, col[:, None] * inv

    def rope(rot_dim):
        ang = np.stack(angles(rot_dim), 1).astype(np.float32)
        cos = np.repeat(np.cos(ang)[:, :, None, :], 2, axis=2)
        sin = np.sin(ang)[:, :, None, :] * np.array([-1, 1], np.float32)[None, None, :, None]

        def lay(x):
            return np.ascontiguousarray(x.reshape(TL, P, -1).transpose(1, 0, 2).reshape(P, -1).astype(np.float32))
        return lay(cos), lay(sin)

    out["ret_cos"], out["ret_sin"] = rope(DK)
    out["mla_cos"], out["mla_sin"] = rope(ROPE)
    p, x = np.arange(P)[:, None], np.arange(P)[None, :]
    fwd = np.concatenate([np.maximum(d * P + x - p, 0) for d in reversed(range(T))], 1)
    bwd = np.concatenate([np.maximum(e * P + p - x, 0) for e in range(T)], 1)
    out["ret_rel"] = np.concatenate([fwd, bwd], 1).astype(np.float32)
    out["ret_tri"] = np.concatenate([x >= p, p >= x], 1).astype(np.float32)
    g = np.arange(NG)
    out["lower"] = np.broadcast_to((g[None, :] < g[:, None]).astype(np.float32).reshape(1, -1), (P, NG * NG)).copy()
    return out


def build(nc, a, consts, out, dbg=None):
    k = Kit(nc, a, consts)
    mod_dram = nc.dram_tensor("mod", [2, 2, 6 * D], F32).ap()
    y_dram = nc.dram_tensor("y", [(T * TOPK + E) * P, D], F32).ap()
    with ExitStack() as ctx:
        ident = k.sb(ctx, "ident", [P, P])
        ident_in = k.sem("ident_in")
        with nc.Block() as block:
            @block.sync
            def _(sp):
                sp.dma_start(ident[:], consts["ident"]).then_inc(ident_in, 16)
                sp.wait_ge(ident_in, 16)
        conditioning(k, mod_dram)
        x_sb = k.sb(ctx, "x", [P, T, D])
        with ExitStack() as first:
            oT = k.sb(first, "oT", [P, VW // P, T * P])
            with ExitStack() as mixer:
                hT = k.sb(mixer, "hT", [P, KD, T * P])
                norm_modulate(k, ident, 0, 0, a["norm_mix"][0], mod_dram, list(range(T)), x_sb, hT, x_dram=(a["ctx"], a["x"]))
                retention(k, ident, hT, oT, x_sb, y_dram)
            project_out(k, oT, VW // P, a["ret_w_o"][0], (0, 2), mod_dram, x_sb, list(range(T)), x_dram=(a["ctx"], a["x"]))
        expert_layer(k, ident, 0, x_sb, list(range(T)), mod_dram, y_dram)
        k.recycle_semaphores()
        latent_attention(k, ident, x_sb, mod_dram)
        expert_layer(k, ident, 1, x_sb, list(range(TC, T)), mod_dram, y_dram)
        x_out = k.sem("x_out")
        with nc.Block() as block:
            @block.sync
            def _(sp):
                sp.dma_start(out[0].rearrange("(t p) d -> p t d", p=P), x_sb[:, TC:T]).then_inc(x_out, 16)
                sp.wait_ge(x_out, 16)


_INS = ['x', 'c', 'ctx', 'c_ctx', 'ada_w', 'ada_b', 'norm_mix', 'norm_ffn', 'ret_w_in', 'ret_decay_f', 'ret_decay_b',
        'ret_w_o', 'mla_w_in', 'mla_q_a_norm', 'mla_w_q_b', 'mla_kv_a_norm', 'mla_w_kv_b', 'mla_q_norm', 'mla_k_norm',
        'mla_w_o', 'router_w', 'router_bias', 'exp_w_gu', 'exp_w_down', 'sh_w_gu', 'sh_w_down']


def kernel(**inputs):
    import numpy as _np
    import concourse.bacc as _bacc
    from concourse import mybir as _mybir
    from concourse.bass_utils import run_bass_kernel_spmd as _run

    nc = _bacc.Bacc("TRN2", target_bir_lowering=False, num_devices=1)
    arrays, args, consts = {}, {}, {}
    for name in _INS:
        arr = _np.ascontiguousarray(inputs[name])
        arrays[f"in_{name}"] = arr
        args[name] = nc.dram_tensor(f"in_{name}", arr.shape, _mybir.dt.from_np(arr.dtype), kind="ExternalInput").ap()
    for name, arr in shape_constants().items():
        arrays[f"const_{name}"] = arr
        consts[name] = nc.dram_tensor(f"const_{name}", arr.shape, _mybir.dt.from_np(arr.dtype), kind="ExternalInput").ap()
    out = nc.dram_tensor("out", (1, SEQ, D), _mybir.dt.float32, kind="ExternalOutput").ap()
    build(nc, args, consts, out)
    r = _run(nc, [arrays], core_ids=[0])
    return r.results[0]["out"]
```

```python
from contextlib import ExitStack

import numpy as np

import concourse.bass as bass
from concourse import mybir

ALU = mybir.AluOpType
ACT = mybir.ActivationFunctionType
AX_X = mybir.AxisListType.X
F32 = mybir.dt.float32
F32R = mybir.dt.float32r
BF16 = mybir.dt.bfloat16
U32 = mybir.dt.uint32
I32 = mybir.dt.int32

P = 128
D = 1024
KD = D // P
SEQ, CTX = 512, 256
TC, TL = CTX // P, SEQ // P
T = TC + TL
GRID_W = 64
EPS = 1e-6
H, DK, DV = 4, 256, 512
VW = H * DV
MH, NOPE, ROPE, MV = 8, 128, 64, 128
QK = NOPE + ROPE
QR, KVR = 384, 256
E, TOPK, NG, TOPG = 64, 8, 8, 4
EG = E // NG
FF = 256
ROUTED_SCALE = 2.5
NC = 512


def bc(ap, shape, axes):
    for a in axes:
        ap = ap.unsqueeze(a)
    return ap.broadcast_to(shape)


class Kit:

    def __init__(self, nc, a, consts):
        self.nc, self.a, self.c = nc, a, consts
        self.n = 0
        self.sems = []

    def sem(self, name):
        self.n += 1
        self.sems.append(self.nc.alloc_semaphore(f"{name}_{self.n}"))
        return self.sems[-1]

    def recycle_semaphores(self):
        self.nc.clear_and_free_semaphores(self.sems)
        self.nc.all_engine_barrier()
        self.sems = []

    def sb(self, ctx, name, shape, dt=F32):
        self.n += 1
        return ctx.enter_context(self.nc.sbuf_tensor(f"{name}_{self.n}", shape, dt))

    def ps(self, ctx, name, shape, dt=F32):
        self.n += 1
        return ctx.enter_context(self.nc.psum_tensor(f"{name}_{self.n}", shape, dt))


def conditioning(k, mod_dram):
    nc, a = k.nc, k.a
    depth = a["ada_w"].shape[0]
    W = 6 * D
    RING = 4
    groups = W // NC // RING
    with ExitStack() as ctx:
        cond = k.sb(ctx, "cond", [P, 2, KD])
        silu = k.sb(ctx, "silu", [P, KD, 2])
        ring = k.sb(ctx, "ring", [P, RING, KD, NC])
        bias = k.sb(ctx, "bias", [2, depth * W])
        rows = k.sb(ctx, "rows", [2, depth * W])
        acc = k.ps(ctx, "acc", [P, RING, NC])
        cond_in, bias_in, silu_ready = k.sem("cond_in"), k.sem("bias_in"), k.sem("silu_ready")
        w_in = [k.sem(f"ada_w_in{j}") for j in range(RING)]
        slot_free, bank_free = k.sem("slot_free"), k.sem("bank_free")
        product, rows_ready, rows_out = k.sem("product"), k.sem("rows_ready"), k.sem("rows_out")
        block = ctx.enter_context(nc.Block())

        @block.sync
        def _(sp):
            sp.dma_start(cond[:, 0, :], a["c_ctx"].rearrange("(p k) -> p k", k=KD)).then_inc(cond_in, 16)
            sp.dma_start(cond[:, 1, :], a["c"].rearrange("b (p k) -> p (b k)", k=KD)).then_inc(cond_in, 16)
            sp.dma_start(bias[:], a["ada_b"].rearrange("l n -> (l n)").partition_broadcast(2)).then_inc(bias_in, 16)
            sp.sem_inc(slot_free, RING)
            for l in range(depth):
                w = a["ada_w"][l].rearrange("(p k) (g j n) -> p g j k n", k=KD, j=RING, n=NC)
                with sp.Fori(0, groups) as g:
                    for j in range(RING):
                        sp.wait_ge(slot_free, RING * (l * groups + g) + j + 1)
                        sp.dma_start(ring[:, j], w[:, g, j]).then_inc(w_in[j], 16)
            sp.wait_ge(rows_ready, depth * groups * RING)
            sp.dma_start(mod_dram.rearrange("s l n -> s (l n)"), rows[:]).then_inc(rows_out, 16)
            sp.wait_ge(rows_out, 16)

        @block.scalar
        def _(act):
            act.wait_ge(cond_in, 32)
            act.activation(silu[:].rearrange("p k s -> p s k"), cond[:], ACT.Silu).then_inc(silu_ready, 1)

        @block.tensor
        def _(pe):
            pe.wait_ge(silu_ready, 1)
            with pe.Fori(0, depth * groups) as g:
                for j in range(RING):
                    pe.wait_ge(w_in[j], 16 * (g + 1))
                    pe.wait_ge(bank_free, RING * g + j + 1)
                    for kk in range(KD):
                        mm = pe.matmul(acc[0:2, j, :], silu[:, kk, :], ring[:, j, kk, :],
                                       start=(kk == 0), stop=(kk == KD - 1))
                        if kk == KD - 1:
                            mm.then_inc(product, 1)

        @block.vector
        def _(dve):
            dve.sem_inc(bank_free, RING)
            dve.wait_ge(bias_in, 16)
            with dve.Fori(0, depth * groups) as g:
                for j in range(RING):
                    dve.wait_ge(product, RING * g + j + 1)
                    at = bass.ds((g * RING + j) * NC, NC)
                    dve.tensor_tensor(rows[:, at], acc[0:2, j, :], bias[:, at], ALU.add).then_inc(rows_ready, 1)
                    dve.wait_ge(rows_ready, RING * g + j + 1)
                    dve.sem_inc(bank_free, 1)
                    dve.sem_inc(slot_free, 1)


def norm_modulate(k, ident, layer, which, norm_w, mod_dram, tiles, x_sb, hT, x_dram=None, h_dram=None):
    nc, a = k.nc, k.a
    n = len(tiles)
    t0 = tiles[0]
    streams = sorted({int(t >= TC) for t in tiles})
    with ExitStack() as ctx:
        gain = k.sb(ctx, "gain", [P, D])
        scale = k.sb(ctx, "scale", [P, 2, D])
        shift = k.sb(ctx, "shift", [P, 2, D])
        square = k.sb(ctx, "square", [P, D])
        ms = k.sb(ctx, "ms", [P, T])
        mse = k.sb(ctx, "mse", [P, T])
        root = k.sb(ctx, "root", [P, T])
        rinv = k.sb(ctx, "rinv", [P, T])
        h = k.sb(ctx, "h", [P, 2, D])
        turned = k.ps(ctx, "turned", [P, 2, D])
        x_in, rows_in = k.sem("x_in"), k.sem("rows_in")
        squares, ms_ready, root_ready, rinv_ready = k.sem("squares"), k.sem("ms_ready"), k.sem("root_ready"), k.sem("rinv_ready")
        scale_ready, scaled, h_ready = k.sem("scale_ready"), k.sem("scaled"), k.sem("h_ready")
        h_turned, hT_ready = k.sem("h_turned"), k.sem("hT_ready")
        h_out = [k.sem("h_out0"), k.sem("h_out1")]
        block = ctx.enter_context(nc.Block())

        @block.sync
        def _(sp):
            if x_dram is not None:
                sp.dma_start(x_sb[:, 0:TC], x_dram[0].rearrange("b (t p) d -> p (b t) d", p=P)).then_inc(x_in, 16)
                sp.dma_start(x_sb[:, TC:T], x_dram[1].rearrange("b (t p) d -> p (b t) d", p=P)).then_inc(x_in, 16)
            sp.dma_start(gain[:], norm_w.partition_broadcast(P)).then_inc(rows_in, 16)
            for s in streams:
                row = mod_dram[s, layer]
                sp.dma_start(shift[:, s], row[which * D:(which + 1) * D].partition_broadcast(P)).then_inc(rows_in, 16)
                sp.dma_start(scale[:, s], row[(which + 1) * D:(which + 2) * D].partition_broadcast(P)).then_inc(rows_in, 16)
            if h_dram is not None:
                for i, t in enumerate(tiles):
                    sp.wait_ge(h_ready, i + 1)
                    sp.dma_start(h_dram[i * P:(i + 1) * P, :], h[:, i % 2]).then_inc(h_out[i % 2], 16)
                for j in range(2):
                    sp.wait_ge(h_out[j], 16 * (n // 2))
        @block.scalar
        def _(act):
            if x_dram is not None:
                act.wait_ge(x_in, 32)
            for i, t in enumerate(tiles):
                if i:
                    act.wait_ge(squares, i)
                act.activation(square[:], x_sb[:, t], ACT.Square, accum_out=ms[:, t:t + 1]).then_inc(squares, 1)
            act.wait_ge(ms_ready, 1)
            act.activation(root[:, t0:T], mse[:, t0:T], ACT.Sqrt).then_inc(root_ready, 1)
            for i, t in enumerate(tiles):
                act.wait_ge(h_turned, i + 1)
                act.activation(hT[:, :, i * P:(i + 1) * P], turned[:, i % 2].rearrange("p (k m) -> p k m", k=KD),
                               ACT.Copy).then_inc(hT_ready, 1)

        @block.vector
        def _(dve):
            dve.wait_ge(rows_in, 16 * (1 + 2 * len(streams)))
            for s in streams:
                dve.scalar_tensor_tensor(scale[:, s], scale[:, s], 1.0, gain[:], ALU.add, ALU.mult).then_inc(scale_ready, 1)
            dve.wait_ge(squares, n)
            dve.tensor_scalar(mse[:, t0:T], ms[:, t0:T], 1.0 / D, EPS, ALU.mult, ALU.add).then_inc(ms_ready, 1)
            dve.wait_ge(root_ready, 1)
            dve.reciprocal(rinv[:, t0:T], root[:, t0:T]).then_inc(rinv_ready, 1)
            dve.wait_ge(rinv_ready, 1)
            dve.wait_ge(scale_ready, len(streams))
            for i, t in enumerate(tiles):
                s = int(t >= TC)
                if i >= 2:
                    dve.wait_ge(h_turned, i - 1)
                    if h_dram is not None:
                        dve.wait_ge(h_out[i % 2], 16 * (i // 2))
                dve.scalar_tensor_tensor(h[:, i % 2], x_sb[:, t], rinv[:, t:t + 1], scale[:, s], ALU.mult, ALU.mult).then_inc(scaled, 1)
                dve.wait_ge(scaled, i + 1)
                dve.tensor_tensor(h[:, i % 2], h[:, i % 2], shift[:, s], ALU.add).then_inc(h_ready, 1)

        @block.tensor
        def _(pe):
            for i in range(n):
                pe.wait_ge(h_ready, i + 1)
                if i >= 2:
                    pe.wait_ge(hT_ready, i - 1)
                for kk in range(KD):
                    mm = pe.transpose(turned[:, i % 2, kk * P:(kk + 1) * P], h[:, i % 2, kk * P:(kk + 1) * P], ident[:])
                mm.then_inc(h_turned, 1)


def reached(s, i):
    if s == 0:
        return list(range(i + 1))
    return list(range(i, TC)) if i < TC else list(range(TC)) + list(range(i, T))


def retention(k, ident, hT, oT, x_sb):
    nc, a, c = k.nc, k.a, k.c
    w_in = a["ret_w_in"][0].rearrange("(k p) n -> p k n", p=P)
    with ExitStack() as ctx:
        ring = k.sb(ctx, "w", [P, 2, KD, NC])
        cos = k.sb(ctx, "cos", [P, TL, 2, 2, 64])
        sin = k.sb(ctx, "sin", [P, TL, 2, 2, 64])
        rel = k.sb(ctx, "rel", [P, 2, T * P])
        tri = k.sb(ctx, "tri", [P, 2, P])
        dec = k.sb(ctx, "dec", [P, 2, H])
        lgp = k.sb(ctx, "lgp", [P, 2, H])
        lg = k.sb(ctx, "lg", [P, 2, H])
        decay = k.sb(ctx, "decay", [P, 2, T * P])
        qk = k.sb(ctx, "qk", [P, 2, NC])
        rot = k.sb(ctx, "rot", [P, 2, 2, 2, 64])
        qT = k.sb(ctx, "qT", [P, 2, T * P])
        kT = k.sb(ctx, "kT", [P, 2, T * P])
        v = k.sb(ctx, "v", [P, T, DV])
        gate = x_sb[:].rearrange("p t (s n) -> p s t n", s=2)
        probs = k.sb(ctx, "probs", [P, 2, 2, T * P])
        square = k.sb(ctx, "square", [P, DV])
        ss = k.sb(ctx, "ss", [P, 2])
        mse = k.sb(ctx, "mse", [P, 2])
        root = k.sb(ctx, "root", [P, 2])
        rinv = k.sb(ctx, "rinv", [P, 2])
        read = k.sb(ctx, "read", [P, 2, DV])
        o = k.sb(ctx, "o", [P, 2, DV])
        bank = k.ps(ctx, "bank", [P, 8, NC])
        qk_ps = [bank[:, 0], bank[:, 1]]
        vg_ps = [bank[:, 2], bank[:, 3]]
        turn_ps = [bank[:, 4], bank[:, 5]]
        score_ps = [bank[:, 0:2].rearrange("p b n -> p (b n)"), bank[:, 2:4].rearrange("p b n -> p (b n)")]
        y_ps = [bank[:, 6], bank[:, 7]]

        const_in, dec_in = k.sem("const_in"), k.sem("dec_in")
        w_qk, w_v, w_gf, w_gb = (k.sem(x) for x in ("w_qk", "w_v", "w_gf", "w_gb"))
        weighed = k.sem("weighed")
        qk_done, qk_read, vg_done, vg_read = k.sem("qk_done"), k.sem("qk_read"), k.sem("vg_done"), k.sem("vg_read")
        rope_step, qk_ready, qk_turned, qkT_ready = k.sem("rope_step"), k.sem("qk_ready"), k.sem("qk_turned"), k.sem("qkT_ready")
        lg_step, tri_done, table_ready = k.sem("lg_step"), k.sem("tri_done"), k.sem("table_ready")
        scored, probs_ready = k.sem("scored"), k.sem("probs_ready")
        y_done, squares, ms_ready, root_ready, rinv_ready = (k.sem(x) for x in ("y_done", "squares", "ms_ready", "root_ready", "rinv_ready"))
        read_ready, o_ready, o_turned, oT_ready = k.sem("read_ready"), k.sem("o_ready"), k.sem("o_turned"), k.sem("oT_ready")
        block = ctx.enter_context(nc.Block())

        VG = 3 * T
        wv = w_in[:, :, 2 * D:].rearrange("p k (s h n) -> p s h k n", s=3, h=H)
        wqk = w_in[:, :, 0:2 * D].rearrange("p k (s h n) -> p s h k n", s=2, h=H)

        @block.sync
        def _(sp):
            with nc.allow_non_contiguous_dma(reason="small constants"):
                sp.dma_start(cos[:], c["ret_cos"].rearrange("p (t a b n) -> p t a b n", t=TL, a=2, b=2)).then_inc(const_in, 16)
                sp.dma_start(sin[:], c["ret_sin"].rearrange("p (t a b n) -> p t a b n", t=TL, a=2, b=2)).then_inc(const_in, 16)
                sp.dma_start(rel[:], c["ret_rel"].rearrange("p (s n) -> p s n", s=2)).then_inc(const_in, 16)
                sp.dma_start(tri[:], c["ret_tri"].rearrange("p (s n) -> p s n", s=2)).then_inc(const_in, 16)
                sp.dma_start(dec[:, 0], a["ret_decay_f"][0].partition_broadcast(P)).then_inc(dec_in, 16)
                sp.dma_start(dec[:, 1], a["ret_decay_b"][0].partition_broadcast(P)).then_inc(dec_in, 16)
                with sp.Fori(0, H) as h:
                    sp.wait_ge(vg_done, VG * h + 1)
                    for s in range(2):
                        sp.dma_start(ring[:, 0, :, s * DK:(s + 1) * DK], wqk[:, s, h]).then_inc(w_qk, 16)
                    sp.dma_start(ring[:, 1], wv[:, 0, h]).then_inc(w_v, 16)
                    sp.wait_ge(qk_done, T * (h + 1))
                    sp.dma_start(ring[:, 0], wv[:, 1, h]).then_inc(w_gf, 16)
                    sp.wait_ge(vg_done, VG * h + T + 1)
                    sp.dma_start(ring[:, 1], wv[:, 2, h]).then_inc(w_gb, 16)

        @block.tensor
        def _(pe):
            for opened in (vg_done, qk_turned, o_turned):
                pe.sem_inc(opened, 1)

            def project(out, slot, t):
                for kk in range(KD):
                    mm = pe.matmul(out, hT[:, kk, t * P:(t + 1) * P], ring[:, slot, kk, :],
                                   start=(kk == 0), stop=(kk == KD - 1))
                return mm

            def turn_qk(h, t):
                pe.wait_ge(qk_ready, T * h + t + 1)
                if t >= 2:
                    pe.wait_ge(qkT_ready, 2 * (T * h + t - 1))
                else:
                    pe.wait_ge(oT_ready, T * h + 1)
                for j in range(4):
                    mm = pe.transpose(turn_ps[t % 2][:, j * P:(j + 1) * P], qk[:, t % 2, j * P:(j + 1) * P], ident[:])
                mm.then_inc(qk_turned, 1)

            def scores(h, i):
                if i >= 2:
                    pe.wait_ge(probs_ready, T * h + i - 1 + 1)
                js = range(TC) if i < TC else range(T)
                for j in js:
                    for d in range(2):
                        mm = pe.matmul(score_ps[i % 2][:, j * P:(j + 1) * P], kT[:, d, j * P:(j + 1) * P],
                                       qT[:, d, i * P:(i + 1) * P], start=(d == 0), stop=(d == 1))
                mm.then_inc(scored, 1)

            def values(h, i):
                pe.wait_ge(probs_ready, T * h + i + 1 + 1)
                for s in range(2):
                    pe.wait_ge(read_ready, 2 * (T * h + i) + 1)
                    js = reached(s, i)
                    for n, j in enumerate(js):
                        mm = pe.matmul(y_ps[s], probs[:, i % 2, s, j * P:(j + 1) * P], v[:, j, :],
                                       start=(n == 0), stop=(n == len(js) - 1))
                    mm.then_inc(y_done, 1)

            def turn_o(h, i):
                pe.wait_ge(o_ready, T * h + i + 1 + 1)
                if i >= 2:
                    pe.wait_ge(oT_ready, T * h + i - 1 + 1)
                for j in range(4):
                    mm = pe.transpose(turn_ps[i % 2][:, j * P:(j + 1) * P], o[:, i % 2, j * P:(j + 1) * P], ident[:])
                mm.then_inc(o_turned, 1)

            with pe.Fori(0, H) as h:
                pe.wait_ge(probs_ready, T * h + 1)
                for ci, (w_sem, w_count) in enumerate(((w_qk, 2), (w_v, 1), (w_gf, 1), (w_gb, 1))):
                    pe.wait_ge(w_sem, 16 * w_count * (h + 1))
                    for t in range(T):
                        if ci == 0:
                            if t >= 2:
                                pe.wait_ge(qk_read, T * h + t - 1)
                            mm = project(qk_ps[t % 2], 0, t)
                            mm.then_inc(qk_done, 1)
                            if t >= 1:
                                turn_qk(h, t - 1)
                        else:
                            m = (ci - 1) * T + t
                            if m >= 2:
                                pe.wait_ge(vg_read, VG * h + m - 1)
                            mm = project(vg_ps[m % 2], ci % 2, t)
                            mm.then_inc(vg_done, 1)
                            if m == 0:
                                turn_qk(h, T - 1)
                pe.wait_ge(qkT_ready, 2 * T * (h + 1))
                pe.wait_ge(vg_read, VG * (h + 1))
                pe.wait_ge(qk_read, T * (h + 1))
                scores(h, 0)
                for i in range(T):
                    if i + 1 < T:
                        scores(h, i + 1)
                    values(h, i)
                    if i >= 1:
                        turn_o(h, i - 1)
                turn_o(h, T - 1)

        @block.scalar
        def _(act):
            for opened in (squares, oT_ready):
                act.sem_inc(opened, 1)
            act.wait_ge(dec_in, 32)
            act.activation(lgp[:], dec[:], ACT.Exp).then_inc(lg_step, 1)
            act.wait_ge(const_in, 64)
            act.wait_ge(lg_step, 2)
            with act.Fori(0, H) as h:
                act.wait_ge(probs_ready, T * h + 1)
                for s in range(2):
                    act.activation(decay[:, s], rel[:, s], ACT.Exp, scale=lg[:, s, bass.ds(h, 1)]).then_inc(table_ready, 1)
                for t in range(T):
                    act.wait_ge(qk_turned, T * h + t + 1 + 1)
                    at = slice(t * P, (t + 1) * P)
                    turned = turn_ps[t % 2].rearrange("p (s d n) -> p s d n", s=2, d=2)
                    act.activation(qT[:, :, at], turned[:, 0], ACT.Copy).then_inc(qkT_ready, 1)
                    act.activation(kT[:, :, at], turned[:, 1], ACT.Copy, scale=DK ** -0.5).then_inc(qkT_ready, 1)
                for m in range(VG):
                    t = m % T
                    act.wait_ge(vg_done, VG * h + m + 1 + 1)
                    if m < T:
                        if m == 0:
                            act.wait_ge(o_ready, T * h + 1)
                        act.activation(v[:, t], vg_ps[m % 2], ACT.Copy).then_inc(vg_read, 1)
                    else:
                        act.activation(gate[:, m // T - 1, t], vg_ps[m % 2], ACT.Silu).then_inc(vg_read, 1)
                def copy_oT(h, i):
                    act.wait_ge(o_turned, T * h + i + 1 + 1)
                    act.activation(oT[:, bass.ds(h * 4, 4), i * P:(i + 1) * P],
                                   turn_ps[i % 2].rearrange("p (d n) -> p d n", d=4), ACT.Copy).then_inc(oT_ready, 1)
                for i in range(T):
                    for s in range(2):
                        n = 2 * (T * h + i) + s
                        act.wait_ge(y_done, n + 1)
                        act.wait_ge(squares, n + 1)
                        act.activation(square[:], y_ps[s], ACT.Square, accum_out=ss[:, s:s + 1]).then_inc(squares, 1)
                        act.wait_ge(ms_ready, n + 1)
                        act.activation(root[:, s:s + 1], mse[:, s:s + 1], ACT.Sqrt).then_inc(root_ready, 1)
                    if i >= 1:
                        copy_oT(h, i - 1)
                copy_oT(h, T - 1)

        @block.vector
        def _(dve):
            for opened in (probs_ready, read_ready, o_ready):
                dve.sem_inc(opened, 1)
            dve.wait_ge(const_in, 64)
            dve.wait_ge(lg_step, 1)
            dve.tensor_scalar(lg[:], lgp[:], -1.0, None, ALU.mult).then_inc(lg_step, 1)
            with dve.Fori(0, H) as h:
                for s in range(2):
                    dve.wait_ge(table_ready, 2 * h + s + 1)
                    at = slice((T - 1) * P, T * P) if s == 0 else slice(0, P)
                    dve.tensor_tensor(decay[:, s, at], decay[:, s, at], tri[:, s], ALU.mult).then_inc(tri_done, 1)
                for t in range(T):
                    n = T * h + t
                    dve.wait_ge(qk_done, n + 1)
                    if t >= 2:
                        dve.wait_ge(qk_turned, n - 1 + 1)
                    else:
                        dve.wait_ge(qk_turned, T * h + 1)
                    if t < TC:
                        dve.tensor_copy(qk[:, t % 2], qk_ps[t % 2]).then_inc(qk_ready, 1)
                        dve.wait_ge(qk_ready, n + 1)
                        dve.sem_inc(qk_read, 1)
                        continue
                    m = TL * h + t - TC
                    src = qk_ps[t % 2].rearrange("p (s a b n) -> p s a b n", s=2, a=2, b=2)
                    dst = qk[:, t % 2].rearrange("p (s a b n) -> p s a b n", s=2, a=2, b=2)
                    lt = t - TC
                    for s in range(2):
                        dve.tensor_tensor(dst[:, s], src[:, s], cos[:, lt], ALU.mult).then_inc(rope_step, 1)
                        for b in range(2):
                            dve.tensor_tensor(rot[:, s, :, b], src[:, s, :, 1 - b], sin[:, lt, :, b], ALU.mult).then_inc(rope_step, 1)
                    dve.wait_ge(rope_step, 6 * (m + 1))
                    dve.sem_inc(qk_read, 1)
                    dve.tensor_tensor(qk[:, t % 2], qk[:, t % 2], rot[:].rearrange("p s a b n -> p (s a b n)"),
                                      ALU.add).then_inc(qk_ready, 1)
                    dve.wait_ge(qk_ready, n + 1)

                def weigh(h, i):
                    n = T * h + i
                    dve.wait_ge(scored, n + 1)
                    if i >= 2:
                        dve.wait_ge(y_done, 2 * (n - 1))
                    sc = score_ps[i % 2]
                    w = (i + 1) * P
                    dve.tensor_tensor(probs[:, i % 2, 0, 0:w], sc[:, 0:w], decay[:, 0, T * P - w:T * P], ALU.mult).then_inc(weighed, 1)
                    if i < TC:
                        w = (TC - i) * P
                        dve.tensor_tensor(probs[:, i % 2, 1, i * P:TC * P], sc[:, i * P:TC * P], decay[:, 1, 0:w],
                                          ALU.mult).then_inc(weighed, 1)
                    else:
                        dve.tensor_tensor(probs[:, i % 2, 1, 0:TC * P], sc[:, 0:TC * P],
                                          decay[:, 1, (T - i) * P:(T - i + TC) * P], ALU.mult)
                        w = (T - i) * P
                        dve.tensor_tensor(probs[:, i % 2, 1, i * P:T * P], sc[:, i * P:T * P], decay[:, 1, 0:w],
                                          ALU.mult).then_inc(weighed, 1)
                    dve.wait_ge(weighed, 2 * (n + 1))
                    dve.sem_inc(probs_ready, 1)

                dve.wait_ge(tri_done, 2 * (h + 1))
                weigh(h, 0)
                for i in range(T):
                    if i + 1 < T:
                        weigh(h, i + 1)
                    n = T * h + i
                    for s in range(2):
                        m = 2 * n + s
                        dve.wait_ge(squares, m + 1 + 1)
                        dve.tensor_scalar(mse[:, s:s + 1], ss[:, s:s + 1], 1.0 / DV, EPS, ALU.mult, ALU.add).then_inc(ms_ready, 1)
                        dve.wait_ge(root_ready, m + 1)
                        dve.reciprocal(rinv[:, s:s + 1], root[:, s:s + 1]).then_inc(rinv_ready, 1)
                        dve.wait_ge(rinv_ready, m + 1)
                        dve.scalar_tensor_tensor(read[:, s], y_ps[s], rinv[:, s:s + 1], gate[:, s, i], ALU.mult,
                                                 ALU.mult).then_inc(read_ready, 1)
                    dve.wait_ge(read_ready, 2 * (n + 1) + 1)
                    if i >= 2:
                        dve.wait_ge(o_turned, n - 1 + 1)
                    else:
                        dve.wait_ge(o_turned, T * h + 1)
                    dve.tensor_tensor(o[:, i % 2], read[:, 0], read[:, 1], ALU.add).then_inc(o_ready, 1)
                    dve.wait_ge(o_ready, n + 1 + 1)


def project_out(k, oT, kt, w, gate_row, mod_dram, x_sb, tiles, x_dram=None):
    nc = k.nc
    n = len(tiles)
    streams = sorted({int(t >= TC) for t in tiles})
    with ExitStack() as ctx:
        w_sb = k.sb(ctx, "wo", [P, 2, kt, NC])
        gate = k.sb(ctx, "gate", [P, 2, D])
        gated = k.sb(ctx, "gated", [P, 2, NC])
        acc = k.ps(ctx, "acc", [P, 4, NC])
        w_in = [k.sem("wo_in0"), k.sem("wo_in1")]
        x_in, gate_in = k.sem("x_in"), k.sem("gate_in")
        product, gated_ready, x_ready = k.sem("product"), k.sem("gated_ready"), k.sem("x_ready")
        block = ctx.enter_context(nc.Block())

        @block.sync
        def _(sp):
            for j in range(2):
                for part in range(2):
                    half = slice(part * kt // 2, (part + 1) * kt // 2)
                    sp.dma_start(w_sb[:, j, half], w.rearrange("(k p) n -> p k n", p=P)[:, half, j * NC:(j + 1) * NC]).then_inc(w_in[j], 16)
            for s in streams:
                sp.dma_start(gate[:, s], mod_dram[s, gate_row[0]][gate_row[1] * D:(gate_row[1] + 1) * D].partition_broadcast(P)).then_inc(gate_in, 16)
            if x_dram is not None:
                sp.dma_start(x_sb[:, 0:TC], x_dram[0].rearrange("b (t p) d -> p (b t) d", p=P)).then_inc(x_in, 16)
                sp.dma_start(x_sb[:, TC:T], x_dram[1].rearrange("b (t p) d -> p (b t) d", p=P)).then_inc(x_in, 16)

        @block.tensor
        def _(pe):
            for j in range(2):
                pe.wait_ge(w_in[j], 32)
                for i in range(n):
                    m = j * n + i
                    if m >= 4:
                        pe.wait_ge(gated_ready, m - 3)
                    for kk in range(kt):
                        mm = pe.matmul(acc[:, m % 4], oT[:, kk, i * P:(i + 1) * P], w_sb[:, j, kk, :],
                                       start=(kk == 0), stop=(kk == kt - 1))
                    mm.then_inc(product, 1)

        @block.vector
        def _(dve):
            dve.wait_ge(gate_in, 16 * len(streams))
            if x_dram is not None:
                dve.wait_ge(x_in, 32)
            for j in range(2):
                at = slice(j * NC, (j + 1) * NC)
                for i, t in enumerate(tiles):
                    m = j * n + i
                    dve.wait_ge(product, m + 1)
                    if m >= 2:
                        dve.wait_ge(x_ready, m - 1)
                    dve.tensor_tensor(gated[:, m % 2], acc[:, m % 4], gate[:, int(t >= TC), at], ALU.mult).then_inc(gated_ready, 1)
                    dve.wait_ge(gated_ready, m + 1)
                    dve.tensor_tensor(x_sb[:, t, at], x_sb[:, t, at], gated[:, m % 2], ALU.add).then_inc(x_ready, 1)


def route(k, ident, layer, hT, x_sb, tiles, book, mod_dram):
    nc, a, c = k.nc, k.a, k.c
    n = len(tiles)
    NB = book.blocks
    NOWHERE = 1 << 20
    K2 = FF // P
    GU = 3
    streams = sorted({int(t >= TC) for t in tiles})
    with ExitStack() as ctx:
        w_gu = k.sb(ctx, "sh_gu", [P, KD, 2 * FF])
        w_down = k.sb(ctx, "sh_down", [P, K2, D])
        gate = k.sb(ctx, "gate", [P, 2, D])
        act_g = k.sb(ctx, "act_g", [P, GU, FF])
        prod = k.sb(ctx, "prod", [P, 2, FF])
        prodT = k.sb(ctx, "prodT", [P, 2, FF])
        gated = k.sb(ctx, "gated", [P, 2, D])
        rw = k.sb(ctx, "router_w", [P, KD, E])
        bias = k.sb(ctx, "router_bias", [P, E])
        lower = k.sb(ctx, "lower", [P, NG, NG])
        before = k.sb(ctx, "before", [P, P], BF16)
        ones_bf = k.sb(ctx, "ones_bf", [P, P], BF16)
        ones = k.sb(ctx, "ones", [P, E])
        block_no = k.sb(ctx, "block_no", [P, 1])
        block_no_i = k.sb(ctx, "block_no_i", [P, 1], I32)
        entry = k.sb(ctx, "entry", [P, n, TOPK, 2], U32)
        nowhere = k.sb(ctx, "nowhere", [P, NB * 2], U32)
        s = k.sb(ctx, "s", [P, n, E])
        sel = k.sb(ctx, "sel", [P, n, E])
        best = k.sb(ctx, "best", [P, n, NG, 8])
        gs = k.sb(ctx, "gs", [P, n, NG])
        beats = k.sb(ctx, "beats", [P, n, NG, NG])
        ties = k.sb(ctx, "ties", [P, n, NG, NG])
        rank = k.sb(ctx, "rank", [P, n, NG])
        gmask = k.sb(ctx, "gmask", [P, n, NG])
        gpen = k.sb(ctx, "gpen", [P, n, NG])
        top = k.sb(ctx, "top", [P, n, 8])
        left = k.sb(ctx, "left", [P, n, E])
        mask = k.sb(ctx, "mask", [P, n, E])
        mask_bf = k.sb(ctx, "mask_bf", [P, n, E], BF16)
        w = k.sb(ctx, "w", [P, n, E])
        wsum = k.sb(ctx, "wsum", [P, n])
        winv = k.sb(ctx, "winv", [P, n])
        nblk = k.sb(ctx, "nblk", [P, E])
        end = k.sb(ctx, "end", [P, E])
        start = k.sb(ctx, "start", [P, E])
        pos = k.sb(ctx, "pos", [P, n, E])
        top_slot = k.sb(ctx, "top_slot", [P, n, TOPK])
        junk = k.sb(ctx, "junk", [P, E])
        below = k.sb(ctx, "below", [P, 1])
        expert_f = k.sb(ctx, "expert_f", [P, 1])
        expert_i = k.sb(ctx, "expert_i", [P, 1], I32)
        pairs_f = k.sb(ctx, "pairs_f", [P, 1])
        bank = k.ps(ctx, "bank", [P, 8, NC])
        logits = bank[:, 0, 0:n * E].rearrange("p (t e) -> p t e", t=n)
        counts = bank[:, 0, n * E:(n + 1) * E]
        ranks = bank[:, 1, 0:n * E].rearrange("p (t e) -> p t e", t=n)
        gu_ps = [bank[:, 2 + g] for g in range(GU)]
        turn_ps = bank[:, 5, 0:FF]
        y_ps = bank[:, 6:8].rearrange("p b n -> p (b n)")
        gu_in, down_in, gate_in = k.sem("gu_in"), k.sem("down_in"), k.sem("gate_in")
        gu_done, silu_ready, prod_ready, prod_turned, prodT_ready, y_done, gated_ready, x_ready = (
            k.sem(x) for x in ("gu_done", "silu_ready", "prod_ready", "prod_turned", "prodT_ready", "y_done", "gated_ready", "x_ready"))
        const_in, table_zeroed, scattered, expert_out = k.sem("const_in"), k.sem("table_zeroed"), k.sem("scattered"), k.sem("expert_out")
        made, logits_ready, s_ready, mask_ready, ranks_ready, slots_ready = (
            k.sem(x) for x in ("made", "logits_ready", "s_ready", "mask_ready", "ranks_ready", "slots_ready"))
        step, expert_ready = k.sem("step"), k.sem("expert_ready")
        block = ctx.enter_context(nc.Block())

        @block.sync
        def _(sp):
            sp.dma_start(rw[:], a["router_w"][layer].rearrange("(k p) e -> p k e", p=P)).then_inc(const_in, 16)
            sp.dma_start(bias[:], a["router_bias"][layer].partition_broadcast(P)).then_inc(const_in, 16)
            sp.dma_start(lower[:], c["lower"].rearrange("p (g f) -> p g f", g=NG)).then_inc(const_in, 16)
            sp.wait_ge(made, 1)
            sp.dma_start(book.table_dram.rearrange("(p b) o -> p (b o)", p=P), nowhere[:]).then_inc(table_zeroed, 16)
            sp.dma_start(w_gu[:], a["sh_w_gu"][layer].rearrange("(k p) n -> p k n", p=P)).then_inc(gu_in, 16)
            sp.dma_start(w_down[:], a["sh_w_down"][layer].rearrange("(k p) n -> p k n", p=P)).then_inc(down_in, 16)
            for s in streams:
                sp.dma_start(gate[:, s], mod_dram[s, layer][5 * D:6 * D].partition_broadcast(P)).then_inc(gate_in, 16)
            sp.wait_ge(expert_ready, 1)
            sp.dma_start(book.expert_dram, expert_i[:]).then_inc(expert_out, 16)
            sp.wait_ge(expert_out, 16)

        @block.gpsimd
        def _(pool):
            pool.memset(nowhere[:], NOWHERE).then_inc(made, 1)
            pool.memset(ones_bf[:], 1.0).then_inc(made, 1)
            pool.memset(ones[:], 1.0).then_inc(made, 1)
            pool.iota(block_no_i[:], [[0, 1]], base=0, channel_multiplier=1).then_inc(made, 1)
            pool.iota(entry[:, :, :, 0], [[P, n], [0, TOPK]], base=0, channel_multiplier=1).then_inc(made, 1)
            pool.iota(entry[:, :, :, 1], [[P * TOPK, n], [1, TOPK]], base=0, channel_multiplier=TOPK).then_inc(made, 1)
            pool.wait_ge(made, 2)
            pool.affine_select(out=before[:], in_=ones_bf[:], compare_op=ALU.is_gt, fill=0.0, base=0,
                               pattern=[[1, P]], channel_multiplier=-1).then_inc(made, 1)
            pool.wait_ge(made, 7)
            pool.wait_ge(table_zeroed, 16)
            pool.wait_ge(slots_ready, 1)
            for t in range(n):
                for j in range(TOPK):
                    pool.indirect_dma_start(book.table_dram, bass.IndirectOffsetOnAxis(ap=book.slot[:, t, j:j + 1], axis=0),
                                            entry[:, t, j], None).then_inc(scattered, 16)
            pool.wait_ge(scattered, 16 * n * TOPK)

        @block.tensor
        def _(pe):
            pe.wait_ge(const_in, 48)
            for t in range(n):
                for kk in range(KD):
                    mm = pe.matmul(logits[:, t], hT[:, kk, t * P:(t + 1) * P], rw[:, kk, :], start=(kk == 0), stop=(kk == KD - 1))
            mm.then_inc(logits_ready, 1)

            def gate_up(t):
                if t >= GU:
                    pe.wait_ge(prod_ready, t - GU + 1)
                for kk in range(KD):
                    mm = pe.matmul(gu_ps[t % GU], hT[:, kk, t * P:(t + 1) * P], w_gu[:, kk, :], start=(kk == 0), stop=(kk == KD - 1))
                mm.then_inc(gu_done, 1)

            pe.wait_ge(gu_in, 16)
            gate_up(0)
            gate_up(1)
            pe.wait_ge(mask_ready, 1)
            pe.wait_ge(made, 7)
            for t in range(n):
                for u in range(t + 1):
                    mm = pe.matmul(ranks[:, t], before[:] if u == t else ones_bf[:], mask_bf[:, u, :], start=(u == 0), stop=(u == t))
            for u in range(n):
                mm = pe.matmul(counts, ones_bf[:], mask_bf[:, u, :], start=(u == 0), stop=(u == n - 1))
            mm.then_inc(ranks_ready, 1)
            gate_up(2)
            pe.wait_ge(down_in, 16)
            for t in range(n):
                pe.wait_ge(prod_ready, t + 1)
                for kk in range(K2):
                    mm = pe.transpose(turn_ps[:, kk * P:(kk + 1) * P], prod[:, t % 2, kk * P:(kk + 1) * P], ident[:])
                mm.then_inc(prod_turned, 1)
                if t + GU < n:
                    gate_up(t + GU)
                pe.wait_ge(prodT_ready, t + 1)
                if t:
                    pe.wait_ge(gated_ready, t)
                for half in range(2):
                    for kk in range(K2):
                        mm = pe.matmul(y_ps[:, half * NC:(half + 1) * NC], prodT[:, t % 2, kk * P:(kk + 1) * P],
                                       w_down[:, kk, half * NC:(half + 1) * NC], start=(kk == 0), stop=(kk == K2 - 1))
                mm.then_inc(y_done, 1)

        @block.scalar
        def _(act):
            act.wait_ge(logits_ready, 1)
            act.activation(s[:], logits, ACT.Sigmoid).then_inc(s_ready, 1)

            def silu(t):
                act.wait_ge(gu_done, t + 1)
                if t >= GU:
                    act.wait_ge(prod_ready, t - GU + 1)
                act.activation(act_g[:, t % GU], gu_ps[t % GU][:, 0:FF], ACT.Silu).then_inc(silu_ready, 1)

            for t in range(GU):
                silu(t)
            for t in range(n):
                act.wait_ge(prod_turned, t + 1)
                if t >= 2:
                    act.wait_ge(y_done, t - 1)
                act.activation(prodT[:, t % 2], turn_ps, ACT.Copy).then_inc(prodT_ready, 1)
                if t + GU < n:
                    silu(t + GU)

        @block.vector
        def _(dve):
            count = [0]

            def then(ins):
                count[0] += 1
                ins.then_inc(step, 1)
                dve.wait_ge(step, count[0])

            dve.wait_ge(const_in, 48)
            dve.wait_ge(s_ready, 1)
            then(dve.tensor_tensor(sel[:], s[:], bc(bias[:], [P, n, E], [1]), ALU.add))
            for t in range(n):
                for g in range(NG):
                    ins = dve.max(best[:, t, g], sel[:, t, g * EG:(g + 1) * EG])
            then(ins)
            then(dve.tensor_tensor(gs[:], best[:, :, :, 0], best[:, :, :, 1], ALU.add))
            other = bc(gs[:], [P, n, NG, NG], [2])
            own = bc(gs[:], [P, n, NG, NG], [3])
            dve.tensor_tensor(beats[:], other, own, ALU.is_gt)
            then(dve.tensor_tensor(ties[:], other, own, ALU.is_equal))
            then(dve.tensor_tensor(ties[:], ties[:], bc(lower[:], [P, n, NG, NG], [1]), ALU.mult))
            then(dve.tensor_tensor(beats[:], beats[:], ties[:], ALU.add))
            then(dve.tensor_reduce(rank[:], beats[:], AX_X, ALU.add))
            then(dve.tensor_scalar(gmask[:], rank[:], float(TOPG), None, ALU.is_lt))
            then(dve.tensor_scalar(gpen[:], gmask[:], 1e30, -1e30, ALU.mult, ALU.add))
            sel_g = sel[:].rearrange("p t (g e) -> p t g e", g=NG)
            then(dve.tensor_tensor(sel_g, sel_g, bc(gmask[:], [P, n, NG, EG], [3]), ALU.mult))
            then(dve.tensor_tensor(sel_g, sel_g, bc(gpen[:], [P, n, NG, EG], [3]), ALU.add))
            for t in range(n):
                ins = dve.max(top[:, t], sel[:, t])
            then(ins)
            for t in range(n):
                ins = dve.match_replace(left[:, t], top[:, t], sel[:, t], -3e38)
            then(ins)
            then(dve.tensor_tensor(mask[:], left[:], sel[:], ALU.is_lt))
            dve.tensor_copy(mask_bf[:], mask[:]).then_inc(mask_ready, 1)
            then(dve.tensor_tensor(w[:], s[:], mask[:], ALU.mult))
            then(dve.tensor_reduce(wsum[:], w[:], AX_X, ALU.add))
            then(dve.reciprocal(winv[:], wsum[:]))
            then(dve.tensor_scalar(winv[:], winv[:], ROUTED_SCALE, None, ALU.mult))
            then(dve.tensor_tensor(w[:], w[:], bc(winv[:], [P, n, E], [2]), ALU.mult))
            dve.wait_ge(made, 7)
            then(dve.tensor_copy(block_no[:], block_no_i[:]))
            dve.wait_ge(ranks_ready, 1)
            then(dve.tensor_scalar(nblk[:], counts, 0.0, None, ALU.is_gt))
            for m in range(1, n):
                then(dve.scalar_tensor_tensor(nblk[:], counts, float(m * P), nblk[:], ALU.is_gt, ALU.add))
            then(dve.tensor_tensor_scan(end[:], ones[:], nblk[:], 0.0, ALU.mult, ALU.add))
            then(dve.tensor_tensor(start[:], end[:], nblk[:], ALU.subtract))
            then(dve.tensor_scalar(start[:], start[:], float(P), 1.0, ALU.mult, ALU.add))
            then(dve.tensor_tensor(pos[:], ranks, bc(start[:], [P, n, E], [1]), ALU.add))
            then(dve.tensor_tensor(pos[:], pos[:], mask[:], ALU.mult))
            for t in range(n):
                ins = dve.max(top_slot[:, t], pos[:, t])
            then(ins)
            then(dve.tensor_scalar(book.slot[:], top_slot[:], -1.0, None, ALU.add))
            dve.sem_inc(slots_ready, 1)
            then(dve.tensor_scalar(junk[:], end[:], block_no[:, 0:1], None, ALU.is_le))
            then(dve.tensor_reduce(below[:], junk[:], AX_X, ALU.add))
            then(dve.tensor_scalar(expert_f[:], below[:], float(E - 1), None, ALU.min))
            then(dve.tensor_copy(expert_i[:], expert_f[:]))
            dve.sem_inc(expert_ready, 1)
            then(dve.tensor_scalar(pairs_f[:], end[:, E - 1:E], 0.5, -0.75, ALU.mult, ALU.add))
            then(dve.tensor_copy(book.last_pair[:, 0:1], pairs_f[:]))
            then(dve.tensor_scalar(pairs_f[:], pairs_f[:], -1.0, None, ALU.add))
            then(dve.tensor_copy(book.last_pair[:, 1:2], pairs_f[:]))

            def multiply(t):
                dve.wait_ge(silu_ready, t + 1)
                if t >= 2:
                    dve.wait_ge(prod_turned, t - 1)
                dve.tensor_tensor(prod[:, t % 2], act_g[:, t % GU], gu_ps[t % GU][:, FF:2 * FF], ALU.mult).then_inc(prod_ready, 1)

            multiply(0)
            multiply(1)
            dve.wait_ge(gate_in, 16 * len(streams))
            for i, t in enumerate(tiles):
                for j in range(TOPK):
                    then(dve.scalar_tensor_tensor(junk[:], pos[:, i], top_slot[:, i, j:j + 1], w[:, i], ALU.is_equal, ALU.mult,
                                                  accum_out=book.weight[:, i, j:j + 1]))
                if i + 2 < n:
                    multiply(i + 2)
                dve.wait_ge(y_done, i + 1)
                if i >= 2:
                    dve.wait_ge(x_ready, i - 1)
                dve.tensor_tensor(gated[:, i % 2], y_ps, gate[:, int(t >= TC)], ALU.mult).then_inc(gated_ready, 1)
                dve.wait_ge(gated_ready, i + 1)
                dve.tensor_tensor(x_sb[:, t], x_sb[:, t], gated[:, i % 2], ALU.add).then_inc(x_ready, 1)


def experts(k, ident, layer, book, h_dram, y_dram):
    nc, a = k.nc, k.a
    K2 = FF // P
    HK = KD // 2
    with ExitStack() as ctx:
        raw_gu = k.sb(ctx, "raw_gu", [P, 2, HK, 2 * FF])
        raw_down = k.sb(ctx, "raw_down", [P, K2, D])
        gu_hi = k.sb(ctx, "gu_hi", [P, 2, KD, 2 * FF], F32R)
        gu_lo = k.sb(ctx, "gu_lo", [P, 2, KD, 2 * FF], F32R)
        down_hi = k.sb(ctx, "down_hi", [P, 2, K2, D], F32R)
        down_lo = k.sb(ctx, "down_lo", [P, 2, K2, D], F32R)
        table = k.sb(ctx, "table", [book.blocks, P, 2], U32)
        table_f = k.sb(ctx, "table_f", [book.blocks, 2, P])
        row_of = k.sb(ctx, "row_of", [P, 2, book.blocks], U32)
        from_row = k.sb(ctx, "from_row", [P, 2], U32)
        to_row = k.sb(ctx, "to_row", [P, 2], U32)
        rows = k.sb(ctx, "rows", [P, 2, D])
        xT_hi = k.sb(ctx, "xT_hi", [P, 2, D], F32R)
        xT_lo = k.sb(ctx, "xT_lo", [P, 2, D], F32R)
        act_g = k.sb(ctx, "act_g", [P, FF])
        prod = k.sb(ctx, "prod", [P, FF])
        prodT_hi = k.sb(ctx, "prodT_hi", [P, FF], F32R)
        prodT_lo = k.sb(ctx, "prodT_lo", [P, FF], F32R)
        y = k.sb(ctx, "y", [P, 2, D])
        bank = k.ps(ctx, "bank", [P, 8, NC])
        turn_ps = bank[:, 0:2].rearrange("p b n -> p (b n)")
        gu_ps = [bank[:, 2], bank[:, 3]]
        small_ps = bank[:, 4, 0:FF]
        y_ps = bank[:, 6:8].rearrange("p b n -> p (b n)")
        gu_in = [k.sem("gu_in0"), k.sem("gu_in1")]
        down_in = k.sem("down_in")
        gu_hi_ready = [k.sem("gu_hi_ready0"), k.sem("gu_hi_ready1")]
        gu_ready = [k.sem("gu_ready0"), k.sem("gu_ready1")]
        down_hi_ready, down_ready = k.sem("down_hi_ready"), k.sem("down_ready")
        table_in, table_f_ready, table_turned, row_of_ready = (k.sem(x) for x in ("table_in", "table_f_ready", "table_turned", "row_of_ready"))
        from_ready, to_ready = k.sem("from_ready"), k.sem("to_ready")
        rows_in = [k.sem("rows_in0"), k.sem("rows_in1")]
        y_out, y_left = k.sem("y_out"), k.sem("y_left")
        passed, cleared = k.sem("passed"), k.sem("cleared")
        turned, xT_hi_ready, xT_ready, gu_done, silu_ready, prod_ready = (
            k.sem(x) for x in ("turned", "xT_hi_ready", "xT_ready", "gu_done", "silu_ready", "prod_ready"))
        prod_turned, prodT_hi_ready, prodT_ready, y_done, y_ready = (
            k.sem(x) for x in ("prod_turned", "prodT_hi_ready", "prodT_ready", "y_done", "y_ready"))
        block = ctx.enter_context(nc.Block())
        gu_w = a["exp_w_gu"][layer].rearrange("e (s k p) n -> e s p k n", s=2, p=P)
        down_w = a["exp_w_down"][layer].rearrange("e (k p) n -> e p k n", p=P)

        def last_pair(eng):
            return eng.value_load(book.last_pair[0:1, 0:1], min_val=1, max_val=book.blocks // 2 - 1)

        @block.sync
        def _(sp):
            last = last_pair(sp)

            def expert_of(b):
                return sp.value_load(book.expert_dram[bass.ds(b, 1), :], min_val=0, max_val=E - 1)

            def load_gate_up(b, e, wait=True):
                for s in range(2):
                    if wait:
                        sp.wait_ge(gu_ready[s], b)
                    sp.dma_start(raw_gu[:, s], gu_w[bass.ds(e, 1), s].rearrange("o p k n -> p (o k) n")).then_inc(gu_in[s], 16)

            def load_down(b, e, wait=True):
                if wait:
                    sp.wait_ge(down_ready, b)
                sp.dma_start(raw_down[:], down_w[bass.ds(e, 1)].rearrange("o p k n -> p (o k) n")).then_inc(down_in, 16)

            sp.dma_start(table[:], book.table_dram.rearrange("(b p) o -> b p o", p=P)).then_inc(table_in, 16)
            e0 = expert_of(0)
            load_gate_up(0, e0, wait=False)
            load_down(0, e0, wait=False)
            load_gate_up(1, expert_of(1))
            with sp.Fori(0, last) as i:
                for j in range(2):
                    b = 2 * i + j
                    load_down(b + 1, expert_of(b + 1))
                    load_gate_up(b + 2, expert_of(b + 2))
            load_down(2 * last + 1, expert_of(2 * last + 1))

        @block.gpsimd
        def _(pool):
            last = last_pair(pool)
            before_last = pool.value_load(book.last_pair[0:1, 1:2], min_val=0, max_val=book.blocks // 2 - 2)

            def gather(i, j, first=False):
                b = 2 * i + j
                if not first:
                    pool.wait_ge(turned, b - 1)
                pool.tensor_copy(from_row[:, j:j + 1], row_of[:, 0, bass.ds(b, 1)]).then_inc(from_ready, 1)
                pool.wait_ge(from_ready, b + 1)
                pool.sem_inc(passed, 1)
                pool.indirect_dma_start(rows[:, j], None, h_dram, bass.IndirectOffsetOnAxis(ap=from_row[:, j:j + 1], axis=0),
                                        bounds_check=h_dram.shape[0] - 1, oob_is_err=False).then_inc(rows_in[j], 16)

            def scatter(i, j, first=False):
                b = 2 * i + j
                if not first:
                    pool.wait_ge(y_out, 16 * b)
                    pool.sem_inc(y_left, 1)
                pool.tensor_copy(to_row[:, j:j + 1], row_of[:, 1, bass.ds(b, 1)]).then_inc(to_ready, 1)
                pool.wait_ge(to_ready, b + 1)
                pool.wait_ge(y_ready, b + 2)
                pool.sem_inc(passed, 1)
                pool.indirect_dma_start(y_dram, bass.IndirectOffsetOnAxis(ap=to_row[:, j:j + 1], axis=0), y[:, j], None,
                                        bounds_check=book.picks - 1, oob_is_err=False).then_inc(y_out, 16)

            pool.sem_inc(y_left, 2)
            pool.memset(rows[:], 0.0).then_inc(cleared, 1)
            pool.wait_ge(cleared, 1)
            pool.wait_ge(row_of_ready, 1)
            for i in range(2):
                for j in range(2):
                    gather(i, j, first=(i == 0))
            for j in range(2):
                gather(2, j)
                scatter(0, j, first=(j == 0))
            with pool.Fori(1, before_last) as i:
                for j in range(2):
                    gather(i + 2, j)
                    scatter(i, j)
            for i in (before_last, last):
                for j in range(2):
                    scatter(i, j)
            pool.wait_ge(y_out, 16 * 2 * (last + 1))
            pool.sem_inc(passed, 1)

        @block.tensor
        def _(pe):
            last = last_pair(pe)

            def three(dst, hi, lo, w_hi, w_lo, first, final):
                pe.matmul(dst, hi, w_hi, start=first, stop=False)
                pe.matmul(dst, hi, w_lo, start=False, stop=False)
                return pe.matmul(dst, lo, w_hi, start=False, stop=final)

            def turn_rows(i, j, first=False):
                pe.wait_ge(rows_in[j], 16 * (i + 1))
                if not first:
                    pe.wait_ge(xT_ready, 2 * i + j)
                for kk in range(KD):
                    mm = pe.transpose(turn_ps[:, kk * P:(kk + 1) * P], rows[:, j, kk * P:(kk + 1) * P], ident[:])
                mm.then_inc(turned, 1)

            def gate_up(i, j):
                b = 2 * i + j
                pe.wait_ge(gu_ready[0], b + 1)
                pe.wait_ge(xT_ready, b + 1)
                for kk in range(KD):
                    if kk == HK:
                        pe.wait_ge(gu_ready[1], b + 1)
                    x_at = slice(kk * P, (kk + 1) * P)
                    mm = three(gu_ps[j], xT_hi[:, j, x_at], xT_lo[:, j, x_at], gu_hi[:, j, kk], gu_lo[:, j, kk], kk == 0, kk == KD - 1)
                mm.then_inc(gu_done, 1)

            def turn_prod(i, j):
                pe.wait_ge(prod_ready, 2 * i + j + 1)
                for kk in range(K2):
                    mm = pe.transpose(small_ps[:, kk * P:(kk + 1) * P], prod[:, kk * P:(kk + 1) * P], ident[:])
                mm.then_inc(prod_turned, 1)

            def down(i, j):
                b = 2 * i + j
                pe.wait_ge(down_ready, b + 1)
                pe.wait_ge(prodT_ready, b + 1)
                pe.wait_ge(y_ready, b + 1)
                for half in range(2):
                    at = slice(half * NC, (half + 1) * NC)
                    for kk in range(K2):
                        x_at = slice(kk * P, (kk + 1) * P)
                        mm = three(y_ps[:, at], prodT_hi[:, x_at], prodT_lo[:, x_at], down_hi[:, j, kk, at], down_lo[:, j, kk, at],
                                   kk == 0, kk == K2 - 1)
                mm.then_inc(y_done, 1)

            pe.wait_ge(table_f_ready, 1)
            for way in range(2):
                mm = pe.transpose(small_ps[:, way * book.blocks:(way + 1) * book.blocks], table_f[:, way],
                                  ident[0:book.blocks, 0:book.blocks])
            mm.then_inc(table_turned, 1)
            turn_rows(0, 0, first=True)
            turn_rows(0, 1)
            gate_up(0, 0)
            with pe.Fori(0, last) as i:
                for j in range(2):
                    turn_rows(i + 1, j)
                    turn_prod(i, j)
                    gate_up(i + j, 1 - j)
                    down(i, j)
            turn_prod(last, 0)
            gate_up(last, 1)
            down(last, 0)
            turn_prod(last, 1)
            down(last, 1)

        @block.scalar
        def _(act):
            last = last_pair(act)
            act.sem_inc(y_ready, 1)

            def split_gate_up(i, j, s):
                b = 2 * i + j
                act.wait_ge(gu_in[s], 16 * (b + 1))
                act.activation(gu_hi[:, j, s * HK:(s + 1) * HK], raw_gu[:, s], ACT.Copy).then_inc(gu_hi_ready[s], 1)

            def split_down(i, j):
                act.wait_ge(down_in, 16 * (2 * i + j + 1))
                act.activation(down_hi[:, j], raw_down[:], ACT.Copy).then_inc(down_hi_ready, 1)

            def copy_xT(i, j, wait=True):
                b = 2 * i + j
                act.wait_ge(turned, b + 1)
                if wait:
                    act.wait_ge(gu_done, b - 1)
                act.activation(xT_hi[:, j], turn_ps, ACT.Copy).then_inc(xT_hi_ready, 1)

            def silu(i, j):
                act.wait_ge(gu_done, 2 * i + j + 1)
                act.activation(act_g[:], gu_ps[j][:, 0:FF], ACT.Silu).then_inc(silu_ready, 1)

            def copy_prodT(i, j):
                act.wait_ge(prod_turned, 2 * i + j + 1)
                act.activation(prodT_hi[:], small_ps, ACT.Copy).then_inc(prodT_hi_ready, 1)

            def copy_y(i, j):
                act.wait_ge(y_done, 2 * i + j + 1)
                act.wait_ge(y_left, 2 * i + j + 1)
                act.activation(y[:, j], y_ps, ACT.Copy).then_inc(y_ready, 1)

            split_gate_up(0, 0, 0)
            split_gate_up(0, 0, 1)
            copy_xT(0, 0, wait=False)
            copy_xT(0, 1, wait=False)
            split_down(0, 0)
            silu(0, 0)
            split_gate_up(0, 1, 0)
            split_gate_up(0, 1, 1)
            with act.Fori(0, last) as i:
                for j in range(2):
                    copy_xT(i + 1, j)
                    copy_prodT(i, j)
                    split_down(i + j, 1 - j)
                    split_gate_up(i + 1, j, 0)
                    silu(i + j, 1 - j)
                    split_gate_up(i + 1, j, 1)
                    copy_y(i, j)
            copy_prodT(last, 0)
            split_down(last, 1)
            silu(last, 1)
            copy_y(last, 0)
            copy_prodT(last, 1)
            copy_y(last, 1)

        @block.vector
        def _(dve):
            last = last_pair(dve)

            def split_gate_up(i, j, s):
                b = 2 * i + j
                at = slice(s * HK, (s + 1) * HK)
                dve.wait_ge(gu_hi_ready[s], b + 1)
                dve.tensor_tensor(gu_lo[:, j, at], raw_gu[:, s], gu_hi[:, j, at].bitcast(F32), ALU.subtract).then_inc(gu_ready[s], 1)

            def split_down(i, j):
                dve.wait_ge(down_hi_ready, 2 * i + j + 1)
                dve.tensor_tensor(down_lo[:, j], raw_down[:], down_hi[:, j].bitcast(F32), ALU.subtract).then_inc(down_ready, 1)

            def copy_xT(i, j):
                dve.wait_ge(xT_hi_ready, 2 * i + j + 1)
                dve.tensor_tensor(xT_lo[:, j], turn_ps, xT_hi[:, j].bitcast(F32), ALU.subtract).then_inc(xT_ready, 1)

            def multiply(i, j):
                dve.wait_ge(silu_ready, 2 * i + j + 1)
                dve.tensor_tensor(prod[:], act_g[:], gu_ps[j][:, FF:2 * FF], ALU.mult).then_inc(prod_ready, 1)

            def copy_prodT(i, j):
                dve.wait_ge(prodT_hi_ready, 2 * i + j + 1)
                dve.tensor_tensor(prodT_lo[:], small_ps, prodT_hi[:].bitcast(F32), ALU.subtract).then_inc(prodT_ready, 1)

            dve.wait_ge(table_in, 16)
            dve.tensor_copy(table_f[:].rearrange("b o p -> b p o"), table[:]).then_inc(table_f_ready, 1)
            dve.wait_ge(table_turned, 1)
            dve.tensor_copy(row_of[:].rearrange("p o b -> p (o b)"), small_ps[:, 0:2 * book.blocks]).then_inc(row_of_ready, 1)
            split_gate_up(0, 0, 0)
            split_gate_up(0, 0, 1)
            copy_xT(0, 0)
            copy_xT(0, 1)
            split_down(0, 0)
            multiply(0, 0)
            split_gate_up(0, 1, 0)
            split_gate_up(0, 1, 1)
            with dve.Fori(0, last) as i:
                for j in range(2):
                    copy_xT(i + 1, j)
                    copy_prodT(i, j)
                    split_down(i + j, 1 - j)
                    split_gate_up(i + 1, j, 0)
                    multiply(i + j, 1 - j)
                    split_gate_up(i + 1, j, 1)
            copy_prodT(last, 0)
            split_down(last, 1)
            multiply(last, 1)
            copy_prodT(last, 1)


def combine(k, layer, x_sb, tiles, book, y_dram, mod_dram):
    nc = k.nc
    n = len(tiles)
    HALF = TOPK // 2
    RING = 4
    streams = sorted({int(t >= TC) for t in tiles})
    with ExitStack() as ctx:
        gate = k.sb(ctx, "gate", [P, 2, D])
        picked = k.sb(ctx, "picked", [P, RING, HALF, D])
        acc = k.sb(ctx, "acc", [P, D])
        gate_in, added = k.sem("gate_in"), k.sem("added")
        picked_in = [k.sem(f"picked_in{r}") for r in range(RING)]
        block = ctx.enter_context(nc.Block())
        y_rows = y_dram[0:book.picks].rearrange("(t p s j) d -> t s p j d", p=P, s=2, j=HALF)
        STEPS = TOPK + 2

        @block.sync
        def _(sp):
            for s in streams:
                sp.dma_start(gate[:, s], mod_dram[s, layer][5 * D:6 * D].partition_broadcast(P)).then_inc(gate_in, 16)
            for t in range(n):
                for s in range(2):
                    m = 2 * t + s
                    if m >= RING:
                        sp.wait_ge(added, STEPS * ((m - RING) // 2) + HALF * (s + 1))
                    sp.dma_start(picked[:, m % RING], y_rows[t, s]).then_inc(picked_in[m % RING], 16)

        @block.vector
        def _(dve):
            count = [0]

            def then(ins):
                count[0] += 1
                ins.then_inc(added, 1)
                dve.wait_ge(added, count[0])

            dve.wait_ge(gate_in, 16 * len(streams))
            for i, t in enumerate(tiles):
                for j in range(TOPK):
                    m = 2 * i + j // HALF
                    if j % HALF == 0:
                        dve.wait_ge(picked_in[m % RING], 16 * (m // RING + 1))
                    pick, weight = picked[:, m % RING, j % HALF], book.weight[:, i, j:j + 1]
                    if j == 0:
                        then(dve.tensor_scalar(acc[:], pick, weight, None, ALU.mult))
                    else:
                        then(dve.scalar_tensor_tensor(acc[:], pick, weight, acc[:], ALU.mult, ALU.add))
                then(dve.tensor_tensor(acc[:], acc[:], gate[:, int(t >= TC)], ALU.mult))
                then(dve.tensor_tensor(x_sb[:, t], x_sb[:, t], acc[:], ALU.add))


class Book:

    def __init__(self, k, ctx, name, n):
        self.picks = n * P * TOPK
        self.blocks = self.picks // P + E
        nc = k.nc
        self.slot = k.sb(ctx, "slot", [P, n, TOPK], U32)
        self.weight = k.sb(ctx, "weight", [P, n, TOPK])
        self.last_pair = k.sb(ctx, "last_pair", [P, 2], I32)
        self.table_dram = nc.dram_tensor(f"table_{name}", [self.blocks * P, 2], U32).ap()
        self.expert_dram = nc.dram_tensor(f"expert_{name}", [P, 1], I32).ap()


def expert_layer(k, ident, layer, x_sb, tiles, mod_dram, y_dram):
    nc = k.nc
    n = len(tiles)
    with ExitStack() as ctx:
        book = Book(k, ctx, str(layer), n)
        h_dram = nc.dram_tensor(f"h_{layer}", [n * P, D], F32).ap()
        with ExitStack() as normed:
            hT = k.sb(normed, "hT", [P, KD, n * P])
            norm_modulate(k, ident, layer, 3, k.a["norm_ffn"][layer], mod_dram, tiles, x_sb=x_sb, hT=hT, h_dram=h_dram)
            route(k, ident, layer, hT, x_sb, tiles, book, mod_dram)
        experts(k, ident, layer, book, h_dram, y_dram)
        combine(k, layer, x_sb, tiles, book, y_dram, mod_dram)


def rotate(eng, then, dst, src, cos, sin, tmp):
    then(eng.tensor_tensor(tmp, src, cos, ALU.mult))
    for b in range(2):
        then(eng.tensor_tensor(dst[:, :, :, b], src[:, :, :, 1 - b], sin[:, :, :, b], ALU.mult))
    then(eng.tensor_tensor(dst, dst, tmp, ALU.add))


def latent_down(k, ident, hT, qaT, kvaT, krT):
    nc, a, c = k.nc, k.a, k.c
    MLA_IN = QR + KVR + ROPE
    with ExitStack() as ctx:
        w = k.sb(ctx, "w_in", [P, KD, MLA_IN])
        gq = k.sb(ctx, "gq", [P, QR])
        gkv = k.sb(ctx, "gkv", [P, KVR])
        gkr = k.sb(ctx, "gkr", [P, ROPE])
        cos = k.sb(ctx, "cos", [P, TL, 2, 2, ROPE // 4])
        sin = k.sb(ctx, "sin", [P, TL, 2, 2, ROPE // 4])
        low = k.sb(ctx, "low", [P, T, MLA_IN])
        kr = k.sb(ctx, "kr", [P, T, ROPE])
        krt = k.sb(ctx, "krt", [P, TL, ROPE])
        krr = k.sb(ctx, "krr", [P, TL, ROPE])
        square = k.sb(ctx, "square", [P, QR])
        S = TL + 2 * T
        ms, mse, root, rinv = (k.sb(ctx, x, [P, S]) for x in ("ms", "mse", "root", "rinv"))
        bank = k.ps(ctx, "bank", [P, 8, NC])
        turn_ps = [bank[:, 4:6].rearrange("p b n -> p (b n)"), bank[:, 6:8].rearrange("p b n -> p (b n)")]
        w_in, rows_in = k.sem("w_in"), k.sem("rows_in")
        product, copied, squared = k.sem("product"), k.sem("copied"), k.sem("squared")
        ms_ready, root_ready, step, tile_ready, tile_turned, tile_out = (
            k.sem(x) for x in ("ms_ready", "root_ready", "step", "tile_ready", "tile_turned", "tile_out"))
        items = []
        for t in range(T):
            items.append((t, t % 2, slice(QR, MLA_IN)))
            if t >= TC:
                items.append((t, 2 + t % 2, slice(0, QR)))
        last_user = {}
        block = ctx.enter_context(nc.Block())

        @block.sync
        def _(sp):
            for half in range(2):
                ks = slice(half * KD // 2, (half + 1) * KD // 2)
                sp.dma_start(w[:, ks], a["mla_w_in"][0].rearrange("(k p) n -> p k n", p=P)[:, ks]).then_inc(w_in, 16)
            sp.dma_start(gq[:], a["mla_q_a_norm"][0].partition_broadcast(P)).then_inc(rows_in, 16)
            sp.dma_start(gkv[:], a["mla_kv_a_norm"][0].partition_broadcast(P)).then_inc(rows_in, 16)
            sp.dma_start(gkr[:], a["mla_k_norm"][0, NOPE:QK].partition_broadcast(P)).then_inc(rows_in, 16)
            sp.dma_start(cos[:], c["mla_cos"].rearrange("p (t a b n) -> p t a b n", t=TL, a=2, b=2)).then_inc(rows_in, 16)
            sp.dma_start(sin[:], c["mla_sin"].rearrange("p (t a b n) -> p t a b n", t=TL, a=2, b=2)).then_inc(rows_in, 16)

        @block.tensor
        def _(pe):
            pe.wait_ge(w_in, 32)
            for m, (t, b, cols) in enumerate(items):
                if b in last_user:
                    pe.wait_ge(copied, last_user[b] + 1)
                last_user[b] = m
                for kk in range(KD):
                    mm = pe.matmul(bank[:, b, 0:cols.stop - cols.start], hT[:, kk, t * P:(t + 1) * P], w[:, kk, cols],
                                   start=(kk == 0), stop=(kk == KD - 1))
                mm.then_inc(product, 1)
            for t in range(T):
                pe.wait_ge(tile_ready, t + 1)
                if t >= 2:
                    pe.wait_ge(tile_out, t - 1)
                for j in range(0 if t >= TC else 3, 5):
                    pe.transpose(turn_ps[t % 2][:, j * P:(j + 1) * P], low[:, t, j * P:(j + 1) * P], ident[:])
                pe.transpose(turn_ps[t % 2][0:ROPE, 5 * P:6 * P], kr[:, t], ident[:]).then_inc(tile_turned, 1)

        @block.scalar
        def _(act):
            for m, (t, b, cols) in enumerate(items):
                act.wait_ge(copied, m + 1)
                if m:
                    act.wait_ge(squared, m)
                parts = [(0, QR, t - TC)] if b >= 2 else [(0, KVR, TL + t), (KVR, KVR + ROPE, TL + T + t)]
                for n, (lo, hi, col) in enumerate(parts):
                    ins = act.activation(square[:, 0:hi - lo] if not n else square[:, KVR:KVR + ROPE], low[:, t, cols.start + lo:cols.start + hi], ACT.Square,
                                         accum_out=ms[:, col:col + 1])
                ins.then_inc(squared, 1)
            act.wait_ge(ms_ready, 1)
            act.activation(root[:], mse[:], ACT.Sqrt).then_inc(root_ready, 1)
            for t in range(T):
                at = slice(t * P, (t + 1) * P)
                act.wait_ge(tile_turned, t + 1)
                ps = turn_ps[t % 2]
                if t >= TC:
                    act.activation(qaT[:, :, (t - TC) * P:(t - TC + 1) * P], ps[:, 0:3 * P].rearrange("p (k m) -> p k m", k=3), ACT.Copy)
                act.activation(kvaT[:, :, at], ps[:, 3 * P:5 * P].rearrange("p (k m) -> p k m", k=2), ACT.Copy)
                act.activation(krT[0:ROPE, at], ps[0:ROPE, 5 * P:6 * P], ACT.Copy).then_inc(tile_out, 1)

        @block.vector
        def _(dve):
            count = [0]

            def then(ins):
                count[0] += 1
                ins.then_inc(step, 1)
                dve.wait_ge(step, count[0])

            for m, (t, b, cols) in enumerate(items):
                dve.wait_ge(product, m + 1)
                dve.tensor_copy(low[:, t, cols], bank[:, b, 0:cols.stop - cols.start]).then_inc(copied, 1)
            dve.wait_ge(squared, len(items))
            dve.wait_ge(copied, len(items))
            for lo, hi, width in ((0, TL, QR), (TL, TL + T, KVR), (TL + T, S, ROPE)):
                then(dve.tensor_scalar(mse[:, lo:hi], ms[:, lo:hi], 1.0 / width, EPS, ALU.mult, ALU.add))
            dve.sem_inc(ms_ready, 1)
            dve.wait_ge(root_ready, 1)
            then(dve.reciprocal(rinv[:], root[:]))
            dve.wait_ge(rows_in, 80)
            for t in range(T):
                col = TL + T + t
                then(dve.scalar_tensor_tensor(kr[:, t], low[:, t, QR + KVR:MLA_IN], rinv[:, col:col + 1], gkr[:], ALU.mult, ALU.mult))
            split = "p t (a b n) -> p t a b n"
            rotate(dve, then, krr[:].rearrange(split, a=2, b=2), kr[:, TC:T].rearrange(split, a=2, b=2), cos[:], sin[:],
                   krt[:].rearrange(split, a=2, b=2))
            then(dve.tensor_copy(kr[:, TC:T], krr[:]))
            for t in range(T):
                if t >= TC:
                    dve.scalar_tensor_tensor(low[:, t, 0:QR], low[:, t, 0:QR], rinv[:, t - TC:t - TC + 1], gq[:], ALU.mult, ALU.mult)
                col = TL + t
                dve.scalar_tensor_tensor(low[:, t, QR:QR + KVR], low[:, t, QR:QR + KVR], rinv[:, col:col + 1], gkv[:],
                                         ALU.mult, ALU.mult).then_inc(tile_ready, 1)


def latent_up(k, qaT, kvaT, q_sb, kv_sb, rq, rk):
    nc, a = k.nc, k.a
    KQ, KK = QR // P, KVR // P
    with ExitStack() as ctx:
        wq = k.sb(ctx, "wq", [P, KQ, MH * QK])
        wkv = k.sb(ctx, "wkv", [P, KK, MH * (NOPE + MV)])
        square = k.sb(ctx, "square", [P, 2, MH * QK])
        msq, rootq = k.sb(ctx, "msq", [P, TL, MH, 2]), k.sb(ctx, "rootq", [P, TL, MH, 2])
        msk, rootk = k.sb(ctx, "msk", [P, T, MH]), k.sb(ctx, "rootk", [P, T, MH])
        bank = k.ps(ctx, "bank", [P, 2, 4 * NC])
        wq_in, wkv_in = k.sem("wq_in"), k.sem("wkv_in")
        product, copied, squared, reduced = k.sem("product"), k.sem("copied"), k.sem("squared"), k.sem("reduced")
        mean_ready, root_ready, step = k.sem("mean_ready"), k.sem("root_ready"), k.sem("step")
        items = [("q", t) for t in range(TL)] + [("kv", t) for t in range(T)]
        block = ctx.enter_context(nc.Block())

        @block.sync
        def _(sp):
            sp.dma_start(wq[:], a["mla_w_q_b"][0].rearrange("(k p) n -> p k n", p=P)).then_inc(wq_in, 16)
            sp.dma_start(wkv[:], a["mla_w_kv_b"][0].rearrange("(k p) n -> p k n", p=P)).then_inc(wkv_in, 16)

        @block.tensor
        def _(pe):
            for m, (what, t) in enumerate(items):
                if m == 0:
                    pe.wait_ge(wq_in, 16)
                if m == TL:
                    pe.wait_ge(wkv_in, 16)
                if m >= 2:
                    pe.wait_ge(copied, m - 1)
                x, w, kt = (qaT, wq, KQ) if what == "q" else (kvaT, wkv, KK)
                for n in range(w.shape[2] // NC):
                    for kk in range(kt):
                        mm = pe.matmul(bank[:, m % 2, n * NC:(n + 1) * NC], x[:, kk, t * P:(t + 1) * P], w[:, kk, n * NC:(n + 1) * NC],
                                       start=(kk == 0), stop=(kk == kt - 1))
                mm.then_inc(product, 1)

        @block.scalar
        def _(act):
            for m, (what, t) in enumerate(items):
                act.wait_ge(copied, m + 1)
                if m >= 2:
                    act.wait_ge(reduced, m - 1)
                if what == "q":
                    ins = act.activation(square[:, m % 2], q_sb[:, t], ACT.Square)
                else:
                    ins = act.activation(square[:, m % 2, 0:MH * NOPE].rearrange("p (h n) -> p h n", h=MH),
                                         kv_sb[:, t].rearrange("p (h n) -> p h n", h=MH)[:, :, 0:NOPE], ACT.Square)
                ins.then_inc(squared, 1)
            act.wait_ge(mean_ready, 1)
            act.activation(rootq[:], msq[:], ACT.Sqrt).then_inc(root_ready, 1)
            act.activation(rootk[:], msk[:], ACT.Sqrt).then_inc(root_ready, 1)

        @block.vector
        def _(dve):
            count = [0]

            def then(ins):
                count[0] += 1
                ins.then_inc(step, 1)
                dve.wait_ge(step, count[0])

            for m, (what, t) in enumerate(items):
                dve.wait_ge(product, m + 1)
                if what == "q":
                    dve.tensor_copy(q_sb[:, t], bank[:, m % 2, 0:MH * QK]).then_inc(copied, 1)
                    dve.wait_ge(squared, m + 1)
                    sq = square[:, m % 2].rearrange("p (h n) -> p h n", h=MH)
                    dve.tensor_reduce(msq[:, t, :, 0], sq[:, :, 0:NOPE], AX_X, ALU.add)
                    dve.tensor_reduce(msq[:, t, :, 1], sq[:, :, NOPE:QK], AX_X, ALU.add).then_inc(reduced, 1)
                else:
                    dve.tensor_copy(kv_sb[:, t], bank[:, m % 2]).then_inc(copied, 1)
                    dve.wait_ge(squared, m + 1)
                    dve.tensor_reduce(msk[:, t], square[:, m % 2, 0:MH * NOPE].rearrange("p (h n) -> p h n", h=MH), AX_X,
                                      ALU.add).then_inc(reduced, 1)
            dve.wait_ge(reduced, len(items))
            then(dve.tensor_scalar(msq[:, :, :, 0], msq[:, :, :, 0], 1.0 / NOPE, EPS, ALU.mult, ALU.add))
            then(dve.tensor_scalar(msq[:, :, :, 1], msq[:, :, :, 1], 1.0 / ROPE, EPS, ALU.mult, ALU.add))
            then(dve.tensor_scalar(msk[:], msk[:], 1.0 / NOPE, EPS, ALU.mult, ALU.add))
            dve.sem_inc(mean_ready, 1)
            dve.wait_ge(root_ready, 2)
            dve.reciprocal(rq[:], rootq[:])
            dve.reciprocal(rk[:], rootk[:])


def attention(k, ident, q_sb, kv_sb, rq, rk, krT, oT):
    nc, a, c = k.nc, k.a, k.c
    NK = T * P
    with ExitStack() as ctx:
        gqn, gqr, gkn = k.sb(ctx, "gqn", [P, NOPE]), k.sb(ctx, "gqr", [P, ROPE]), k.sb(ctx, "gkn", [P, NOPE])
        cos = k.sb(ctx, "cos", [P, TL, 2, 2, ROPE // 4])
        sin = k.sb(ctx, "sin", [P, TL, 2, 2, ROPE // 4])
        qn, qr = k.sb(ctx, "qn", [P, 2, TL, NOPE]), k.sb(ctx, "qr", [P, 2, TL, ROPE])
        qx, qt = k.sb(ctx, "qx", [P, TL, ROPE]), k.sb(ctx, "qt", [P, TL, ROPE])
        kn, vh = k.sb(ctx, "kn", [P, 2, T, NOPE]), k.sb(ctx, "vh", [P, 2, T, MV])
        qnT, qrT = k.sb(ctx, "qnT", [P, 2, SEQ]), k.sb(ctx, "qrT", [ROPE, 2, SEQ])
        knT = k.sb(ctx, "knT", [P, 2, NK])
        top, ntop = k.sb(ctx, "top", [P, 2]), k.sb(ctx, "ntop", [P, 2])
        total, inv = k.sb(ctx, "total", [P, 2]), k.sb(ctx, "inv", [P, 2])
        probs = k.sb(ctx, "probs", [P, 2, NK])
        probsT = k.sb(ctx, "probsT", [P, 2, T, SEQ])
        bank = k.ps(ctx, "bank", [P, 8, NC])
        score_ps = [bank[:, 0:2].rearrange("p b n -> p (b n)")[:, 0:NK], bank[:, 2:4].rearrange("p b n -> p (b n)")[:, 0:NK]]
        probT_ps = bank[:, 4:6].rearrange("p b n -> p (b n)")[:, 0:NK]
        out_ps = bank[:, 6]
        head_ps = bank[:, 7]
        rows_in = k.sem("rows_in")
        passed = k.sem("passed")
        step, staged, head_turned, head_out = k.sem("step"), k.sem("staged"), k.sem("head_turned"), k.sem("head_out")
        values_staged = k.sem("values_staged")
        scored, top_ready, exp_ready, probs_ready, probs_turned, probsT_ready = (
            k.sem(x) for x in ("scored", "top_ready", "exp_ready", "probs_ready", "probs_turned", "probsT_ready"))
        top_step, inv_step, attended, oT_ready = k.sem("top_step"), k.sem("inv_step"), k.sem("attended"), k.sem("oT_ready")
        block = ctx.enter_context(nc.Block())
        OPEN, R = 2, 4

        def heads(h):
            return h + 1 + OPEN

        def units(h, i):
            return TL * (h + OPEN) + i + 1

        @block.sync
        def _(sp):
            sp.dma_start(gqn[:], a["mla_q_norm"][0, 0:NOPE].partition_broadcast(P)).then_inc(rows_in, 16)
            sp.dma_start(gqr[:], a["mla_q_norm"][0, NOPE:QK].partition_broadcast(P)).then_inc(rows_in, 16)
            sp.dma_start(gkn[:], a["mla_k_norm"][0, 0:NOPE].partition_broadcast(P)).then_inc(rows_in, 16)
            sp.dma_start(cos[:], c["mla_cos"].rearrange("p (t a b n) -> p t a b n", t=TL, a=2, b=2)).then_inc(rows_in, 16)
            sp.dma_start(sin[:], c["mla_sin"].rearrange("p (t a b n) -> p t a b n", t=TL, a=2, b=2)).then_inc(rows_in, 16)

        @block.gpsimd
        def _(pool):
            pool.sem_inc(staged, OPEN)
            pool.wait_ge(rows_in, 80)
            q_h = q_sb[:].rearrange("p t (h n) -> p t h n", h=MH)
            kv_h = kv_sb[:].rearrange("p t (h n) -> p t h n", h=MH)
            STEPS = 9

            with pool.Fori(0, MH // 2) as i:
                for j in range(2):
                    h = 2 * i + j
                    made = [0]

                    def then(ins):
                        made[0] += 1
                        ins.then_inc(step, 1)
                        pool.wait_ge(step, STEPS * h + made[0])

                    def head(x, lo, hi):
                        return x[:, :, bass.ds(h, 1), lo:hi].rearrange("p t o n -> p t (o n)")

                    pool.wait_ge(head_turned, R * (h + 1))
                    then(pool.tensor_tensor(kn[:, j], head(kv_h, 0, NOPE), rk[:, :, bass.ds(h, 1)].broadcast_to([P, T, NOPE]), ALU.mult))
                    then(pool.tensor_tensor(kn[:, j], kn[:, j], bc(gkn[:], [P, T, NOPE], [1]), ALU.mult))
                    then(pool.tensor_tensor(qn[:, j], head(q_h, 0, NOPE), rq[:, :, bass.ds(h, 1), 0].broadcast_to([P, TL, NOPE]), ALU.mult))
                    then(pool.tensor_tensor(qn[:, j], qn[:, j], bc(gqn[:], [P, TL, NOPE], [1]), ALU.mult))
                    then(pool.tensor_tensor(qx[:], head(q_h, NOPE, QK), rq[:, :, bass.ds(h, 1), 1].broadcast_to([P, TL, ROPE]), ALU.mult))
                    then(pool.tensor_tensor(qx[:], qx[:], bc(gqr[:], [P, TL, ROPE], [1]), ALU.mult))
                    split = "p t (a b n) -> p t a b n"
                    x5, d5 = qx[:].rearrange(split, a=2, b=2), qr[:, j].rearrange(split, a=2, b=2)
                    pool.tensor_tensor(qt[:], qx[:], cos[:].rearrange("p t a b n -> p t (a b n)"), ALU.mult)
                    pool.tensor_tensor(d5[:, :, :, 0], x5[:, :, :, 1], sin[:, :, :, 0], ALU.mult)
                    then(pool.tensor_tensor(d5[:, :, :, 1], x5[:, :, :, 0], sin[:, :, :, 1], ALU.mult))
                    then(pool.tensor_tensor(qr[:, j], qr[:, j], qt[:], ALU.add))
                    pool.sem_inc(staged, 1)
                    pool.wait_ge(attended, h + 1)
                    then(pool.tensor_copy(vh[:, j], head(kv_h, NOPE, NOPE + MV)))
                    pool.sem_inc(values_staged, 1)

        @block.tensor
        def _(pe):
            pe.sem_inc(head_turned, R * OPEN)
            pe.sem_inc(attended, OPEN)
            pe.sem_inc(probs_turned, TL * OPEN)
            pe.sem_inc(scored, TL * OPEN)

            def turn_head(i, j, r):
                h = 2 * i + j
                if r == 0:
                    pe.wait_ge(staged, heads(h))
                pe.wait_ge(head_out, R * (h + OPEN) + r)
                if r == 3:
                    pe.sem_inc(passed, 1)
                if r in (0, 3):
                    src, w = (qn, P) if r == 0 else (qr, ROPE)
                    for t in range(TL):
                        mm = pe.transpose(head_ps[0:w, t * P:(t + 1) * P], src[:, j, t], ident[:])
                else:
                    for n, t in enumerate(range(4) if r == 1 else range(4, T)):
                        mm = pe.transpose(head_ps[:, n * P:(n + 1) * P], kn[:, j, t], ident[:])
                mm.then_inc(head_turned, 1)

            def scores(i, j, t):
                h = 2 * i + j
                if t == 0:
                    pe.wait_ge(head_out, R * heads(h))
                pe.wait_ge(exp_ready, units(h, t) - 2)
                for lo, hi in ((0, NC), (NC, NK)):
                    pe.matmul(score_ps[t % 2][:, lo:hi], qnT[:, j, t * P:(t + 1) * P], knT[:, j, lo:hi], start=True, stop=False)
                    mm = pe.matmul(score_ps[t % 2][:, lo:hi], qrT[:, j, t * P:(t + 1) * P], krT[0:ROPE, lo:hi], start=False, stop=True)
                mm.then_inc(scored, 1)

            def turn_probs(i, j, t):
                h = 2 * i + j
                pe.wait_ge(probs_ready, units(h, t))
                pe.wait_ge(probsT_ready, units(h, t) - 1)
                for n in range(T):
                    mm = pe.transpose(probT_ps[:, n * P:(n + 1) * P], probs[:, t % 2, n * P:(n + 1) * P], ident[:])
                mm.then_inc(probs_turned, 1)

            def values(i, j):
                h = 2 * i + j
                pe.wait_ge(probsT_ready, units(h, TL - 1))
                pe.wait_ge(values_staged, h + 1)
                pe.wait_ge(oT_ready, heads(h) - 1)
                for n in range(T):
                    mm = pe.matmul(out_ps, vh[:, j, n], probsT[:, j, n], start=(n == 0), stop=(n == T - 1))
                mm.then_inc(attended, 1)

            def attend(i, j, nxt):
                if nxt:
                    turn_head(*nxt, 0)
                scores(i, j, 1)
                if nxt:
                    turn_head(*nxt, 1)
                turn_probs(i, j, 0)
                scores(i, j, 2)
                if nxt:
                    turn_head(*nxt, 2)
                turn_probs(i, j, 1)
                scores(i, j, 3)
                if nxt:
                    turn_head(*nxt, 3)
                turn_probs(i, j, 2)
                if nxt:
                    scores(*nxt, 0)
                turn_probs(i, j, 3)
                values(i, j)

            for r in range(R):
                turn_head(0, 0, r)
            scores(0, 0, 0)
            last = MH // 2 - 1
            with pe.Fori(0, last) as i:
                attend(i, 0, (i, 1))
                attend(i, 1, (i + 1, 0))
            attend(last, 0, (last, 1))
            attend(last, 1, None)

        @block.scalar
        def _(act):
            act.sem_inc(head_out, R * OPEN)
            act.sem_inc(exp_ready, TL * OPEN)
            act.sem_inc(probsT_ready, TL * OPEN)
            act.sem_inc(oT_ready, OPEN)

            def copy_head(i, j, r):
                h = 2 * i + j
                act.wait_ge(head_turned, R * (h + OPEN) + r + 1)
                if r == 0:
                    act.wait_ge(scored, units(h, TL - 1) - 2 * TL)
                    act.activation(qnT[:, j], head_ps, ACT.Copy, scale=float(QK) ** -0.5).then_inc(head_out, 1)
                elif r == 1:
                    act.activation(knT[:, j, 0:NC], head_ps, ACT.Copy).then_inc(head_out, 1)
                elif r == 2:
                    act.activation(knT[:, j, NC:NK], head_ps[:, 0:NK - NC], ACT.Copy).then_inc(head_out, 1)
                else:
                    act.activation(qrT[:, j], head_ps[0:ROPE], ACT.Copy, scale=float(QK) ** -0.5).then_inc(head_out, 1)

            def exps(i, j, t):
                h = 2 * i + j
                act.wait_ge(top_ready, units(h, t))
                act.wait_ge(probs_turned, units(h, t) - 2)
                act.activation(probs[:, t % 2], score_ps[t % 2], ACT.Exp, bias=ntop[:, t % 2:t % 2 + 1],
                               accum_out=total[:, t % 2:t % 2 + 1]).then_inc(exp_ready, 1)

            def copy_probs(i, j, t):
                h = 2 * i + j
                act.wait_ge(probs_turned, units(h, t))
                if t == 0:
                    act.wait_ge(attended, heads(h) - 2)
                act.activation(probsT[:, j, :, t * P:(t + 1) * P], probT_ps.rearrange("p (n m) -> p n m", n=T),
                               ACT.Copy).then_inc(probsT_ready, 1)

            def copy_out(i, j):
                h = 2 * i + j
                act.wait_ge(attended, heads(h))
                act.activation(oT[:, bass.ds(h, 1)].rearrange("p o n -> p (o n)"), out_ps, ACT.Copy).then_inc(oT_ready, 1)

            def attend(i, j, nxt):
                if nxt:
                    copy_head(*nxt, 0)
                exps(i, j, 1)
                if nxt:
                    copy_head(*nxt, 1)
                copy_probs(i, j, 0)
                exps(i, j, 2)
                if nxt:
                    copy_head(*nxt, 2)
                copy_probs(i, j, 1)
                exps(i, j, 3)
                if nxt:
                    copy_head(*nxt, 3)
                copy_probs(i, j, 2)
                if nxt:
                    exps(*nxt, 0)
                copy_probs(i, j, 3)
                copy_out(i, j)

            for r in range(R):
                copy_head(0, 0, r)
            exps(0, 0, 0)
            last = MH // 2 - 1
            with act.Fori(0, last) as i:
                attend(i, 0, (i, 1))
                attend(i, 1, (i + 1, 0))
            attend(last, 0, (last, 1))
            attend(last, 1, None)

        @block.vector
        def _(dve):
            dve.sem_inc(top_ready, TL * OPEN)
            dve.sem_inc(probs_ready, TL * OPEN)

            def maximum(h, t):
                n = TL * h + t
                dve.wait_ge(scored, units(h, t))
                dve.tensor_reduce(top[:, t % 2:t % 2 + 1], score_ps[t % 2], AX_X, ALU.max).then_inc(top_step, 1)
                dve.wait_ge(top_step, n + 1)
                dve.tensor_scalar(ntop[:, t % 2:t % 2 + 1], top[:, t % 2:t % 2 + 1], -1.0, None, ALU.mult).then_inc(top_ready, 1)

            def normalise(h, t):
                n = TL * h + t
                dve.wait_ge(exp_ready, units(h, t))
                dve.reciprocal(inv[:, t % 2:t % 2 + 1], total[:, t % 2:t % 2 + 1]).then_inc(inv_step, 1)
                dve.wait_ge(inv_step, n + 1)
                dve.tensor_scalar(probs[:, t % 2], probs[:, t % 2], inv[:, t % 2:t % 2 + 1], None, ALU.mult).then_inc(probs_ready, 1)

            with dve.Fori(0, MH) as h:
                for t in range(TL):
                    maximum(h, t)
                    normalise(h, t)


def latent_attention(k, ident, x_sb, mod_dram):
    with ExitStack() as ctx:
        oT = k.sb(ctx, "oT", [P, MH, SEQ])
        with ExitStack() as heads:
            krT = k.sb(heads, "krT", [ROPE, T * P])
            q_sb = k.sb(heads, "q", [P, TL, MH * QK])
            kv_sb = k.sb(heads, "kv", [P, T, MH * (NOPE + MV)])
            rq, rk = k.sb(heads, "rq", [P, TL, MH, 2]), k.sb(heads, "rk", [P, T, MH])
            with ExitStack() as low:
                qaT = k.sb(low, "qaT", [P, QR // P, SEQ])
                kvaT = k.sb(low, "kvaT", [P, KVR // P, T * P])
                with ExitStack() as h:
                    hT = k.sb(h, "hT", [P, KD, T * P])
                    norm_modulate(k, ident, 1, 0, k.a["norm_mix"][1], mod_dram, list(range(T)), x_sb=x_sb, hT=hT)
                    latent_down(k, ident, hT, qaT, kvaT, krT)
                latent_up(k, qaT, kvaT, q_sb, kv_sb, rq, rk)
            attention(k, ident, q_sb, kv_sb, rq, rk, krT, oT)
        project_out(k, oT, MH, k.a["mla_w_o"][0], (1, 2), mod_dram, x_sb, list(range(TC, T)))



def shape_constants():
    out = {"ident": np.eye(P, dtype=np.float32)}

    def angles(rot_dim):
        axis = rot_dim // 2
        inv = (10000.0 ** (-np.arange(0, axis, 2, dtype=np.float32) / axis)).astype(np.float32)
        rows = SEQ // GRID_W
        row = np.repeat(np.arange(rows, dtype=np.float32), GRID_W)
        col = np.tile(np.arange(GRID_W, dtype=np.float32), rows)
        return row[:, None] * inv, col[:, None] * inv

    def rope(rot_dim):
        ang = np.stack(angles(rot_dim), 1).astype(np.float32)
        cos = np.repeat(np.cos(ang)[:, :, None, :], 2, axis=2)
        sin = np.sin(ang)[:, :, None, :] * np.array([-1, 1], np.float32)[None, None, :, None]

        def lay(x):
            return np.ascontiguousarray(x.reshape(TL, P, -1).transpose(1, 0, 2).reshape(P, -1).astype(np.float32))
        return lay(cos), lay(sin)

    out["ret_cos"], out["ret_sin"] = rope(DK)
    out["mla_cos"], out["mla_sin"] = rope(ROPE)
    p, x = np.arange(P)[:, None], np.arange(P)[None, :]
    fwd = np.concatenate([np.maximum(d * P + x - p, 0) for d in reversed(range(T))], 1)
    bwd = np.concatenate([np.maximum(e * P + p - x, 0) for e in range(T)], 1)
    out["ret_rel"] = np.concatenate([fwd, bwd], 1).astype(np.float32)
    out["ret_tri"] = np.concatenate([x >= p, p >= x], 1).astype(np.float32)
    g = np.arange(NG)
    out["lower"] = np.broadcast_to((g[None, :] < g[:, None]).astype(np.float32).reshape(1, -1), (P, NG * NG)).copy()
    return out


def build(nc, a, consts, out, dbg=None):
    k = Kit(nc, a, consts)
    mod_dram = nc.dram_tensor("mod", [2, 2, 6 * D], F32).ap()
    y_dram = nc.dram_tensor("y", [T * TOPK * P, D], F32).ap()
    with ExitStack() as ctx:
        ident = k.sb(ctx, "ident", [P, P])
        ident_in = k.sem("ident_in")
        with nc.Block() as block:
            @block.sync
            def _(sp):
                sp.dma_start(ident[:], consts["ident"]).then_inc(ident_in, 16)
                sp.wait_ge(ident_in, 16)
        conditioning(k, mod_dram)
        x_sb = k.sb(ctx, "x", [P, T, D])
        with ExitStack() as first:
            oT = k.sb(first, "oT", [P, VW // P, T * P])
            with ExitStack() as mixer:
                hT = k.sb(mixer, "hT", [P, KD, T * P])
                norm_modulate(k, ident, 0, 0, a["norm_mix"][0], mod_dram, list(range(T)), x_sb, hT, x_dram=(a["ctx"], a["x"]))
                retention(k, ident, hT, oT, x_sb)
            project_out(k, oT, VW // P, a["ret_w_o"][0], (0, 2), mod_dram, x_sb, list(range(T)), x_dram=(a["ctx"], a["x"]))
        expert_layer(k, ident, 0, x_sb, list(range(T)), mod_dram, y_dram)
        k.recycle_semaphores()
        latent_attention(k, ident, x_sb, mod_dram)
        expert_layer(k, ident, 1, x_sb, list(range(TC, T)), mod_dram, y_dram)
        x_out = k.sem("x_out")
        with nc.Block() as block:
            @block.sync
            def _(sp):
                sp.dma_start(out[0].rearrange("(t p) d -> p t d", p=P), x_sb[:, TC:T]).then_inc(x_out, 16)
                sp.wait_ge(x_out, 16)


_INS = ['x', 'c', 'ctx', 'c_ctx', 'ada_w', 'ada_b', 'norm_mix', 'norm_ffn', 'ret_w_in', 'ret_decay_f', 'ret_decay_b',
        'ret_w_o', 'mla_w_in', 'mla_q_a_norm', 'mla_w_q_b', 'mla_kv_a_norm', 'mla_w_kv_b', 'mla_q_norm', 'mla_k_norm',
        'mla_w_o', 'router_w', 'router_bias', 'exp_w_gu', 'exp_w_down', 'sh_w_gu', 'sh_w_down']


def kernel(**inputs):
    import numpy as _np
    import concourse.bacc as _bacc
    from concourse import mybir as _mybir
    from concourse.bass_utils import run_bass_kernel_spmd as _run

    nc = _bacc.Bacc("TRN2", target_bir_lowering=False, num_devices=1)
    arrays, args, consts = {}, {}, {}
    for name in _INS:
        arr = _np.ascontiguousarray(inputs[name])
        arrays[f"in_{name}"] = arr
        args[name] = nc.dram_tensor(f"in_{name}", arr.shape, _mybir.dt.from_np(arr.dtype), kind="ExternalInput").ap()
    for name, arr in shape_constants().items():
        arrays[f"const_{name}"] = arr
        consts[name] = nc.dram_tensor(f"const_{name}", arr.shape, _mybir.dt.from_np(arr.dtype), kind="ExternalInput").ap()
    out = nc.dram_tensor("out", (1, SEQ, D), _mybir.dt.float32, kind="ExternalOutput").ap()
    build(nc, args, consts, out)
    r = _run(nc, [arrays], core_ids=[0])
    return r.results[0]["out"]
```

```python
from contextlib import ExitStack

import numpy as np

import concourse.bass as bass
from concourse import mybir

ALU = mybir.AluOpType
ACT = mybir.ActivationFunctionType
AX_X = mybir.AxisListType.X
F32 = mybir.dt.float32
F32R = mybir.dt.float32r
BF16 = mybir.dt.bfloat16
U32 = mybir.dt.uint32
I32 = mybir.dt.int32

P = 128
D = 1024
KD = D // P
SEQ, CTX = 512, 256
TC, TL = CTX // P, SEQ // P
T = TC + TL
GRID_W = 64
EPS = 1e-6
H, DK, DV = 4, 256, 512
VW = H * DV
MH, NOPE, ROPE, MV = 8, 128, 64, 128
QK = NOPE + ROPE
QR, KVR = 384, 256
E, TOPK, NG, TOPG = 64, 8, 8, 4
EG = E // NG
FF = 256
ROUTED_SCALE = 2.5
NC = 512


def bc(ap, shape, axes):
    for a in axes:
        ap = ap.unsqueeze(a)
    return ap.broadcast_to(shape)


class Kit:

    def __init__(self, nc, a, consts):
        self.nc, self.a, self.c = nc, a, consts
        self.n = 0
        self.sems = []

    def sem(self, name):
        self.n += 1
        self.sems.append(self.nc.alloc_semaphore(f"{name}_{self.n}"))
        return self.sems[-1]

    def recycle_semaphores(self):
        self.nc.clear_and_free_semaphores(self.sems)
        self.nc.all_engine_barrier()
        self.sems = []

    def sb(self, ctx, name, shape, dt=F32):
        self.n += 1
        return ctx.enter_context(self.nc.sbuf_tensor(f"{name}_{self.n}", shape, dt))

    def ps(self, ctx, name, shape, dt=F32):
        self.n += 1
        return ctx.enter_context(self.nc.psum_tensor(f"{name}_{self.n}", shape, dt))


def three_passes(pe, out, hi, lo, w_hi, w_lo, first, final):
    pe.matmul(out, hi, w_hi, start=first, stop=False)
    pe.matmul(out, hi, w_lo, start=False, stop=False)
    return pe.matmul(out, lo, w_hi, start=False, stop=final)


def conditioning(k, mod_dram):
    nc, a = k.nc, k.a
    depth = a["ada_w"].shape[0]
    W = 6 * D
    RING = 3
    groups = W // NC // RING
    with ExitStack() as ctx:
        cond = k.sb(ctx, "cond", [P, 2, KD])
        silu = k.sb(ctx, "silu", [P, KD, 2])
        silu_hi, silu_lo = k.sb(ctx, "silu_hi", [P, KD, 2], F32R), k.sb(ctx, "silu_lo", [P, KD, 2], F32R)
        w_hi, w_lo = k.sb(ctx, "ada_hi", [P, RING, KD, NC], F32R), k.sb(ctx, "ada_lo", [P, RING, KD, NC], F32R)
        ring = k.sb(ctx, "ring", [P, RING, KD, NC])
        rows = k.sb(ctx, "rows", [2, depth * W])
        acc = k.ps(ctx, "acc", [P, RING, NC])
        cond_in, bias_in, silu_ready = k.sem("cond_in"), k.sem("bias_in"), k.sem("silu_ready")
        w_in = [k.sem(f"ada_w_in{j}") for j in range(RING)]
        silu_split, w_hi_ready, w_ready, bank_free = (k.sem(x) for x in ("silu_split", "w_hi_ready", "w_ready", "bank_free"))
        product, rows_ready, rows_out = k.sem("product"), k.sem("rows_ready"), k.sem("rows_out")
        block = ctx.enter_context(nc.Block())

        @block.sync
        def _(sp):
            sp.dma_start(cond[:, 0, :], a["c_ctx"].rearrange("(p k) -> p k", k=KD)).then_inc(cond_in, 16)
            sp.dma_start(cond[:, 1, :], a["c"].rearrange("b (p k) -> p (b k)", k=KD)).then_inc(cond_in, 16)
            sp.dma_start(rows[:], a["ada_b"].rearrange("l n -> (l n)").partition_broadcast(2)).then_inc(bias_in, 16)
            for l in range(depth):
                w = a["ada_w"][l].rearrange("(p k) (g j n) -> p g j k n", k=KD, j=RING, n=NC)
                with sp.Fori(0, groups) as g:
                    for j in range(RING):
                        sp.wait_ge(w_ready, RING * (l * groups + g) + j + 1)
                        sp.dma_start(ring[:, j], w[:, g, j]).then_inc(w_in[j], 16)
            sp.wait_ge(rows_ready, depth * groups * RING)
            sp.dma_start(mod_dram.rearrange("s l n -> s (l n)"), rows[:]).then_inc(rows_out, 16)
            sp.wait_ge(rows_out, 16)

        @block.scalar
        def _(act):
            act.wait_ge(cond_in, 32)
            act.activation(silu[:].rearrange("p k s -> p s k"), cond[:], ACT.Silu).then_inc(silu_ready, 1)
            act.wait_ge(silu_ready, 1)
            act.activation(silu_hi[:], silu[:], ACT.Copy).then_inc(silu_split, 1)
            with act.Fori(0, depth * groups) as g:
                for j in range(RING):
                    act.wait_ge(w_in[j], 16 * (g + 1))
                    act.wait_ge(product, RING * g + j + 1)
                    act.activation(w_hi[:, j], ring[:, j], ACT.Copy).then_inc(w_hi_ready, 1)

        @block.tensor
        def _(pe):
            pe.sem_inc(product, RING)
            pe.wait_ge(silu_split, 2)
            with pe.Fori(0, depth * groups) as g:
                for j in range(RING):
                    pe.wait_ge(w_ready, RING * (g + 1) + j + 1)
                    pe.wait_ge(bank_free, RING * g + j + 1)
                    for kk in range(KD):
                        mm = three_passes(pe, acc[0:2, j, :], silu_hi[:, kk, :], silu_lo[:, kk, :], w_hi[:, j, kk], w_lo[:, j, kk],
                                          kk == 0, kk == KD - 1)
                    mm.then_inc(product, 1)

        @block.vector
        def _(dve):
            dve.sem_inc(bank_free, RING)
            dve.sem_inc(w_ready, RING)
            dve.wait_ge(silu_split, 1)
            dve.tensor_tensor(silu_lo[:], silu[:], silu_hi[:].bitcast(F32), ALU.subtract).then_inc(silu_split, 1)

            def split(g, j):
                dve.wait_ge(w_hi_ready, RING * g + j + 1)
                dve.tensor_tensor(w_lo[:, j], ring[:, j], w_hi[:, j].bitcast(F32), ALU.subtract).then_inc(w_ready, 1)

            def add_bias(g, j):
                dve.wait_ge(product, RING * g + j + 1 + RING)
                at = bass.ds((g * RING + j) * NC, NC)
                dve.tensor_tensor(rows[:, at], acc[0:2, j, :], rows[:, at], ALU.add).then_inc(rows_ready, 1)
                dve.wait_ge(rows_ready, RING * g + j + 1)
                dve.sem_inc(bank_free, 1)

            split(0, 0)
            dve.wait_ge(bias_in, 16)
            last = depth * groups - 1
            with dve.Fori(0, last) as g:
                for j in range(RING):
                    split(g + (j + 1) // RING, (j + 1) % RING)
                    add_bias(g, j)
            for j in range(RING):
                if j + 1 < RING:
                    split(last, j + 1)
                add_bias(last, j)


def norm_modulate(k, ident, layer, which, norm_w, mod_dram, tiles, x_sb, hT, hT_lo=None, x_dram=None, h_dram=None, prefetch=()):
    nc = k.nc
    n = len(tiles)
    t0 = tiles[0]
    streams = sorted({int(t >= TC) for t in tiles})
    with ExitStack() as ctx:
        gain = k.sb(ctx, "gain", [P, D])
        scale = k.sb(ctx, "scale", [P, 2, D])
        shift = k.sb(ctx, "shift", [P, 2, D])
        square = k.sb(ctx, "square", [P, D])
        ms = k.sb(ctx, "ms", [P, T])
        mse = k.sb(ctx, "mse", [P, T])
        root = k.sb(ctx, "root", [P, T])
        rinv = k.sb(ctx, "rinv", [P, T])
        h = k.sb(ctx, "h", [P, 2, D])
        turned = k.ps(ctx, "turned", [P, 2, D])
        x_in, scale_in, shift_in = [k.sem("ctx_in"), k.sem("x_in")], k.sem("scale_in"), k.sem("shift_in")
        squares, ms_ready, root_ready, rinv_ready = k.sem("squares"), k.sem("ms_ready"), k.sem("root_ready"), k.sem("rinv_ready")
        scale_ready, scaled, h_ready = k.sem("scale_ready"), k.sem("scaled"), k.sem("h_ready")
        h_turned, hT_ready, lo_ready = k.sem("h_turned"), k.sem("hT_ready"), k.sem("lo_ready")
        h_out, prefetched = [k.sem("h_out0"), k.sem("h_out1")], k.sem("prefetched")
        block = ctx.enter_context(nc.Block())

        @block.sync
        def _(sp):
            if x_dram is not None:
                sp.dma_start(x_sb[:, 0:TC], x_dram[0].rearrange("b (t p) d -> p (b t) d", p=P)).then_inc(x_in[0], 16)
                sp.dma_start(x_sb[:, TC:T], x_dram[1].rearrange("b (t p) d -> p (b t) d", p=P)).then_inc(x_in[1], 16)
            sp.dma_start(gain[:], norm_w.partition_broadcast(P)).then_inc(scale_in, 16)
            for s in streams:
                row = mod_dram[s, layer]
                sp.dma_start(scale[:, s], row[(which + 1) * D:(which + 2) * D].partition_broadcast(P)).then_inc(scale_in, 16)
            for s in streams:
                row = mod_dram[s, layer]
                sp.dma_start(shift[:, s], row[which * D:(which + 1) * D].partition_broadcast(P)).then_inc(shift_in, 16)
            for dst, src in prefetch:
                sp.dma_start(dst, src).then_inc(prefetched, 16)
            if h_dram is not None:
                for i, t in enumerate(tiles):
                    sp.wait_ge(h_ready, i + 1)
                    sp.dma_start(h_dram[i * P:(i + 1) * P, :], h[:, i % 2]).then_inc(h_out[i % 2], 16)
                for j in range(2):
                    sp.wait_ge(h_out[j], 16 * (n // 2))
            if prefetch:
                sp.wait_ge(prefetched, 16 * len(prefetch))

        @block.scalar
        def _(act):
            for i, t in enumerate(tiles):
                if x_dram is not None and t in (0, TC):
                    act.wait_ge(x_in[t // TC], 16)
                if i:
                    act.wait_ge(squares, i)
                act.activation(square[:], x_sb[:, t], ACT.Square, accum_out=ms[:, t:t + 1]).then_inc(squares, 1)
            act.wait_ge(ms_ready, 1)
            act.activation(root[:, t0:T], mse[:, t0:T], ACT.Sqrt).then_inc(root_ready, 1)
            for i, t in enumerate(tiles):
                act.wait_ge(h_turned, i + 1)
                act.activation(hT[:, :, i * P:(i + 1) * P], turned[:, i % 2].rearrange("p (k m) -> p k m", k=KD),
                               ACT.Copy).then_inc(hT_ready, 1)

        @block.vector
        def _(dve):
            def split(i):
                dve.wait_ge(hT_ready, i + 1)
                at = slice(i * P, (i + 1) * P)
                dve.tensor_tensor(hT_lo[:, :, at], turned[:, i % 2].rearrange("p (k m) -> p k m", k=KD), hT[:, :, at].bitcast(F32),
                                  ALU.subtract).then_inc(lo_ready, 1)

            dve.wait_ge(scale_in, 16 * (1 + len(streams)))
            for s in streams:
                dve.scalar_tensor_tensor(scale[:, s], scale[:, s], 1.0, gain[:], ALU.add, ALU.mult).then_inc(scale_ready, 1)
            dve.wait_ge(squares, n)
            dve.tensor_scalar(mse[:, t0:T], ms[:, t0:T], 1.0 / D, EPS, ALU.mult, ALU.add).then_inc(ms_ready, 1)
            dve.wait_ge(root_ready, 1)
            dve.reciprocal(rinv[:, t0:T], root[:, t0:T]).then_inc(rinv_ready, 1)
            dve.wait_ge(rinv_ready, 1)
            dve.wait_ge(scale_ready, len(streams))
            for i, t in enumerate(tiles):
                s = int(t >= TC)
                if i >= 2:
                    dve.wait_ge(h_turned, i - 1)
                    if h_dram is not None:
                        dve.wait_ge(h_out[i % 2], 16 * (i // 2))
                dve.scalar_tensor_tensor(h[:, i % 2], x_sb[:, t], rinv[:, t:t + 1], scale[:, s], ALU.mult, ALU.mult).then_inc(scaled, 1)
                dve.wait_ge(scaled, i + 1)
                if i == 0:
                    dve.wait_ge(shift_in, 16 * len(streams))
                dve.tensor_tensor(h[:, i % 2], h[:, i % 2], shift[:, s], ALU.add).then_inc(h_ready, 1)
                if hT_lo is not None and i:
                    split(i - 1)
            if hT_lo is not None:
                split(n - 1)

        @block.tensor
        def _(pe):
            for i in range(n):
                pe.wait_ge(h_ready, i + 1)
                if i >= 2:
                    pe.wait_ge(hT_ready if hT_lo is None else lo_ready, i - 1)
                for kk in range(KD):
                    mm = pe.transpose(turned[:, i % 2, kk * P:(kk + 1) * P], h[:, i % 2, kk * P:(kk + 1) * P], ident[:])
                mm.then_inc(h_turned, 1)


def reached(s, i):
    if s == 0:
        return list(range(i + 1))
    return list(range(i, TC)) if i < TC else list(range(TC)) + list(range(i, T))


def retention_piece(w, h, piece):
    w_in = w.rearrange("(k p) n -> p k n", p=P)
    if piece < 2:
        return w_in[:, :, 0:2 * D].rearrange("p k (s h n) -> p s h k n", s=2, h=H)[:, piece, h]
    return w_in[:, :, 2 * D:].rearrange("p k (s h f n) -> p s f h k n", s=3, h=H, f=2)[:, piece // 2 - 1, piece % 2, h]


def retention_constants(k, ctx):
    a, c = k.a, k.c
    cos, sin = (k.sb(ctx, x, [P, TL, 2, 2, 64]) for x in ("cos", "sin"))
    rel = k.sb(ctx, "rel", [P, 2, T * P])
    tri = k.sb(ctx, "tri", [P, 2, P])
    dec = k.sb(ctx, "dec", [P, 2, H])
    loads = [(dec[:, 0], a["ret_decay_f"][0].partition_broadcast(P)), (dec[:, 1], a["ret_decay_b"][0].partition_broadcast(P)),
             (cos[:], c["ret_cos"].rearrange("p (t a b n) -> p t a b n", t=TL, a=2, b=2)),
             (sin[:], c["ret_sin"].rearrange("p (t a b n) -> p t a b n", t=TL, a=2, b=2)),
             (rel[:], c["ret_rel"].rearrange("p (s n) -> p s n", s=2)), (tri[:], c["ret_tri"].rearrange("p (s n) -> p s n", s=2))]
    return (cos, sin, rel, tri, dec), loads


def retention(k, ident, hT, hT_lo, oT_dram, x_sb, raw, consts):
    nc, a = k.nc, k.a
    cos, sin, rel, tri, dec = consts
    with ExitStack() as ctx:
        w_hi = k.sb(ctx, "w_hi", [P, 2, KD, DK], F32R)
        w_lo = k.sb(ctx, "w_lo", [P, 2, KD, DK], F32R)
        oT = k.sb(ctx, "oT", [P, 4, T * P])
        lgp = k.sb(ctx, "lgp", [P, 2, H])
        lg = k.sb(ctx, "lg", [P, 2, H])
        decay = k.sb(ctx, "decay", [P, 2, T * P])
        qk = k.sb(ctx, "qk", [P, 2, DK])
        rot = k.sb(ctx, "rot", [P, 2, 2, 64])
        qT = k.sb(ctx, "qT", [P, 2, T * P])
        kT = k.sb(ctx, "kT", [P, 2, T * P])
        v = k.sb(ctx, "v", [P, T, DV])
        gate = x_sb[:].rearrange("p t (s n) -> p s t n", s=2)
        probs = k.sb(ctx, "probs", [P, 2, 2, T * P])
        square = k.sb(ctx, "square", [P, DV])
        ss = k.sb(ctx, "ss", [P, 2])
        mse = k.sb(ctx, "mse", [P, 2])
        root = k.sb(ctx, "root", [P, 2])
        rinv = k.sb(ctx, "rinv", [P, 2])
        read = k.sb(ctx, "read", [P, 2, DV])
        o = k.sb(ctx, "o", [P, 2, DV])
        bank = k.ps(ctx, "bank", [P, 8, NC])
        qk_ps = [bank[:, 0], bank[:, 1]]
        vg_ps = [bank[:, 2], bank[:, 3]]
        turn_ps = [bank[:, 4], bank[:, 5]]
        score_ps = [bank[:, 0:2].rearrange("p b n -> p (b n)"), bank[:, 2:4].rearrange("p b n -> p (b n)")]
        y_ps = [bank[:, 6], bank[:, 7]]

        w_in_raw = [k.sem("w_in0"), k.sem("w_in1")]
        w_hi_ready, w_ready, oT_out = k.sem("w_hi_ready"), k.sem("w_ready"), k.sem("oT_out")
        weighed = k.sem("weighed")
        qk_done, qk_read, vg_done, vg_read = k.sem("qk_done"), k.sem("qk_read"), k.sem("vg_done"), k.sem("vg_read")
        rope_step, qk_ready, qk_turned, qkT_ready = k.sem("rope_step"), k.sem("qk_ready"), k.sem("qk_turned"), k.sem("qkT_ready")
        lg_step, tri_done, table_ready = k.sem("lg_step"), k.sem("tri_done"), k.sem("table_ready")
        scored, probs_ready = k.sem("scored"), k.sem("probs_ready")
        y_done, squares, ms_ready, root_ready, rinv_ready = (k.sem(x) for x in ("y_done", "squares", "ms_ready", "root_ready", "rinv_ready"))
        read_ready, o_ready, o_turned, oT_ready = k.sem("read_ready"), k.sem("o_ready"), k.sem("o_turned"), k.sem("oT_ready")
        block = ctx.enter_context(nc.Block())

        PIECES = 8
        QU = 2 * T
        VG = 6 * T

        @block.sync
        def _(sp):
            def load(h, piece):
                sp.wait_ge(w_ready, 2 * (PIECES * h + piece + 1))
                sp.dma_start(raw[:, piece % 2], retention_piece(a["ret_w_in"][0], h, piece)).then_inc(w_in_raw[piece % 2], 16)

            sp.sem_inc(w_in_raw[0], 16)
            sp.sem_inc(w_in_raw[1], 16)
            for piece in range(2, PIECES):
                load(0, piece)
            with sp.Fori(1, H) as h:
                for piece in range(PIECES):
                    load(h, piece)
            sp.wait_ge(oT_out, 16 * (H + T))

        @block.tensor
        def _(pe):
            for opened in (vg_done, qk_turned, o_turned):
                pe.sem_inc(opened, 1)

            def project(out, slot, t):
                for kk in range(KD):
                    at = slice(t * P, (t + 1) * P)
                    mm = three_passes(pe, out, hT[:, kk, at], hT_lo[:, kk, at], w_hi[:, slot, kk], w_lo[:, slot, kk],
                                      kk == 0, kk == KD - 1)
                return mm

            def turn_qk(h, u):
                pe.wait_ge(qk_ready, QU * h + u + 1)
                if u >= 2:
                    pe.wait_ge(qkT_ready, QU * h + u - 1)
                else:
                    pe.wait_ge(oT_ready, T * h + 1)
                for j in range(2):
                    mm = pe.transpose(turn_ps[u % 2][:, j * P:(j + 1) * P], qk[:, u % 2, j * P:(j + 1) * P], ident[:])
                mm.then_inc(qk_turned, 1)

            def scores(h, i):
                if i >= 2:
                    pe.wait_ge(probs_ready, T * h + i)
                js = range(TC) if i < TC else range(T)
                for j in js:
                    for d in range(2):
                        mm = pe.matmul(score_ps[i % 2][:, j * P:(j + 1) * P], kT[:, d, j * P:(j + 1) * P],
                                       qT[:, d, i * P:(i + 1) * P], start=(d == 0), stop=(d == 1))
                mm.then_inc(scored, 1)

            def values(h, i):
                pe.wait_ge(probs_ready, T * h + i + 1 + 1)
                for s in range(2):
                    pe.wait_ge(read_ready, 2 * (T * h + i) + 1)
                    js = reached(s, i)
                    for n, j in enumerate(js):
                        mm = pe.matmul(y_ps[s], probs[:, i % 2, s, j * P:(j + 1) * P], v[:, j, :],
                                       start=(n == 0), stop=(n == len(js) - 1))
                    mm.then_inc(y_done, 1)

            def turn_o(h, i):
                pe.wait_ge(o_ready, T * h + i + 1 + 1)
                if i >= 2:
                    pe.wait_ge(oT_ready, T * h + i)
                for j in range(4):
                    mm = pe.transpose(turn_ps[i % 2][:, j * P:(j + 1) * P], o[:, i % 2, j * P:(j + 1) * P], ident[:])
                mm.then_inc(o_turned, 1)

            with pe.Fori(0, H) as h:
                pe.wait_ge(probs_ready, T * h + 1)
                for piece in range(PIECES):
                    pe.wait_ge(w_ready, 2 * (PIECES * h + piece + 1 + 2))
                    for t in range(T):
                        if piece < 2:
                            u = piece * T + t
                            if u >= 2:
                                pe.wait_ge(qk_read, QU * h + u - 1)
                            project(qk_ps[u % 2][:, 0:DK], piece % 2, t).then_inc(qk_done, 1)
                            if u >= 1:
                                turn_qk(h, u - 1)
                        else:
                            m = (piece - 2) * T + t
                            if m >= 2:
                                pe.wait_ge(vg_read, VG * h + m - 1)
                            project(vg_ps[m % 2][:, 0:DK], piece % 2, t).then_inc(vg_done, 1)
                            if m == 0:
                                turn_qk(h, QU - 1)
                pe.wait_ge(qkT_ready, QU * (h + 1))
                pe.wait_ge(vg_read, VG * (h + 1))
                pe.wait_ge(qk_read, QU * (h + 1))
                scores(h, 0)
                for i in range(T):
                    if i + 1 < T:
                        scores(h, i + 1)
                    values(h, i)
                    if i >= 1:
                        turn_o(h, i - 1)
                turn_o(h, T - 1)

        @block.scalar
        def _(act):
            for opened in (squares, oT_ready):
                act.sem_inc(opened, 1)
            act.sem_inc(oT_out, 16)

            def split(n, slot):
                act.wait_ge(w_in_raw[slot], 8 * (n + 2 - slot))
                act.activation(w_hi[:, slot], raw[:, slot], ACT.Copy).then_inc(w_hi_ready, 1)

            def head(h, more):
                for piece in range(PIECES):
                    for t in range(T):
                        if piece == 3 and t in (2, 4):
                            s = t // 2 - 1
                            act.wait_ge(probs_ready, T * h + 1)
                            act.activation(decay[:, s], rel[:, s], ACT.Exp, scale=lg[:, s, bass.ds(h, 1)]).then_inc(table_ready, 1)
                        if piece < 2:
                            u = piece * T + t
                            act.wait_ge(qk_turned, QU * h + u + 1 + 1)
                            dst, scale = (qT, 1.0) if piece == 0 else (kT, DK ** -0.5)
                            act.activation(dst[:, :, t * P:(t + 1) * P], turn_ps[u % 2][:, 0:DK].rearrange("p (d n) -> p d n", d=2),
                                           ACT.Copy, scale=scale).then_inc(qkT_ready, 1)
                            if u == T:
                                split(PIECES * h + 2, 0)
                            continue
                        m = (piece - 2) * T + t
                        act.wait_ge(vg_done, VG * h + m + 1 + 1)
                        half = slice(piece % 2 * DK, (piece % 2 + 1) * DK)
                        if piece < 4:
                            if m == 0:
                                act.wait_ge(o_ready, T * h + 1)
                            act.activation(v[:, t, half], vg_ps[m % 2][:, 0:DK], ACT.Copy).then_inc(vg_read, 1)
                        else:
                            act.activation(gate[:, piece // 2 - 2, t, half], vg_ps[m % 2][:, 0:DK], ACT.Silu).then_inc(vg_read, 1)
                    if 1 <= piece < PIECES - 2 or (piece == PIECES - 2 and more):
                        split(PIECES * h + piece + 2, piece % 2)

                def copy_oT(i):
                    act.wait_ge(o_turned, T * h + i + 1 + 1)
                    if i == 0:
                        act.wait_ge(oT_out, 16 * (h + 1))
                    act.activation(oT[:, :, i * P:(i + 1) * P], turn_ps[i % 2].rearrange("p (d n) -> p d n", d=4),
                                   ACT.Copy).then_inc(oT_ready, 1)

                def write_out(i):
                    act.wait_ge(oT_ready, T * h + i + 1 + 1)
                    at = slice(i * P, (i + 1) * P)
                    act.dma_start(oT_dram[h][:, :, at], oT[:, :, at]).then_inc(oT_out, 16)

                for i in range(T):
                    for s in range(2):
                        n = 2 * (T * h + i) + s
                        act.wait_ge(y_done, n + 1)
                        act.wait_ge(squares, n + 1)
                        act.activation(square[:], y_ps[s], ACT.Square, accum_out=ss[:, s:s + 1]).then_inc(squares, 1)
                        act.wait_ge(ms_ready, n + 1)
                        act.activation(root[:, s:s + 1], mse[:, s:s + 1], ACT.Sqrt).then_inc(root_ready, 1)
                    if i >= 1:
                        copy_oT(i - 1)
                        if not more:
                            write_out(i - 1)
                    if i == 1 and more:
                        split(PIECES * (h + 1) + 1, 1)
                copy_oT(T - 1)
                if more:
                    act.wait_ge(oT_ready, T * (h + 1) + 1)
                    act.dma_start(oT_dram[bass.ds(h, 1)].rearrange("o p d n -> p (o d) n"), oT[:]).then_inc(oT_out, 16)
                else:
                    write_out(T - 1)

            split(0, 0)
            split(1, 1)
            act.activation(lgp[:], dec[:], ACT.Exp).then_inc(lg_step, 1)
            act.wait_ge(lg_step, 2)
            with act.Fori(0, H - 1) as h:
                head(h, more=True)
            head(H - 1, more=False)

        @block.vector
        def _(dve):
            def split_half(slot, n, half):
                dve.wait_ge(w_hi_ready, n + 1)
                ks = slice(half * KD // 2, (half + 1) * KD // 2)
                return dve.tensor_tensor(w_lo[:, slot, ks], raw[:, slot, ks], w_hi[:, slot, ks].bitcast(F32), ALU.subtract)

            def split(slot, n):
                dve.wait_ge(w_hi_ready, n + 1)
                dve.tensor_tensor(w_lo[:, slot], raw[:, slot], w_hi[:, slot].bitcast(F32), ALU.subtract).then_inc(w_ready, 2)

            for opened in (probs_ready, read_ready, o_ready):
                dve.sem_inc(opened, 1)
            dve.sem_inc(w_ready, 2 * 2)

            def head(h, more):
                for piece in range(PIECES):
                    for t in range(T if piece < 2 else 0):
                        u = piece * T + t
                        n = QU * h + u
                        dve.wait_ge(qk_done, n + 1)
                        if u >= 2:
                            dve.wait_ge(qk_turned, n)
                        else:
                            dve.wait_ge(qk_turned, QU * h + 1)
                        if t < TC:
                            dve.tensor_copy(qk[:, u % 2], qk_ps[u % 2][:, 0:DK]).then_inc(qk_ready, 1)
                            dve.wait_ge(qk_ready, n + 1)
                            dve.sem_inc(qk_read, 1)
                            if piece == 1:
                                split_half(0, PIECES * h + 2, t).then_inc(w_ready, 1)
                            continue
                        m = 2 * TL * h + TL * piece + t - TC
                        src = qk_ps[u % 2][:, 0:DK].rearrange("p (a b n) -> p a b n", a=2, b=2)
                        dst = qk[:, u % 2].rearrange("p (a b n) -> p a b n", a=2, b=2)
                        lt = t - TC
                        dve.tensor_tensor(dst, src, cos[:, lt], ALU.mult).then_inc(rope_step, 1)
                        for b in range(2):
                            dve.tensor_tensor(rot[:, :, b], src[:, :, 1 - b], sin[:, lt, :, b], ALU.mult).then_inc(rope_step, 1)
                        dve.wait_ge(rope_step, 3 * (m + 1))
                        dve.sem_inc(qk_read, 1)
                        dve.tensor_tensor(qk[:, u % 2], qk[:, u % 2], rot[:].rearrange("p a b n -> p (a b n)"),
                                          ALU.add).then_inc(qk_ready, 1)
                        dve.wait_ge(qk_ready, n + 1)
                    if 1 <= piece < PIECES - 2 or (piece == PIECES - 2 and more):
                        split(piece % 2, PIECES * h + piece + 2)

                def weigh(h, i):
                    n = T * h + i
                    dve.wait_ge(scored, n + 1)
                    if i >= 2:
                        dve.wait_ge(y_done, 2 * (n - 1))
                    sc = score_ps[i % 2]
                    w = (i + 1) * P
                    dve.tensor_tensor(probs[:, i % 2, 0, 0:w], sc[:, 0:w], decay[:, 0, T * P - w:T * P], ALU.mult).then_inc(weighed, 1)
                    if i < TC:
                        w = (TC - i) * P
                        dve.tensor_tensor(probs[:, i % 2, 1, i * P:TC * P], sc[:, i * P:TC * P], decay[:, 1, 0:w],
                                          ALU.mult).then_inc(weighed, 1)
                    else:
                        dve.tensor_tensor(probs[:, i % 2, 1, 0:TC * P], sc[:, 0:TC * P],
                                          decay[:, 1, (T - i) * P:(T - i + TC) * P], ALU.mult)
                        w = (T - i) * P
                        dve.tensor_tensor(probs[:, i % 2, 1, i * P:T * P], sc[:, i * P:T * P], decay[:, 1, 0:w],
                                          ALU.mult).then_inc(weighed, 1)
                    dve.wait_ge(weighed, 2 * (n + 1))
                    dve.sem_inc(probs_ready, 1)

                for s in range(2):
                    dve.wait_ge(table_ready, 2 * h + s + 1)
                    at = slice((T - 1) * P, T * P) if s == 0 else slice(0, P)
                    dve.tensor_tensor(decay[:, s, at], decay[:, s, at], tri[:, s], ALU.mult).then_inc(tri_done, 1)
                dve.wait_ge(tri_done, 2 * (h + 1))
                weigh(h, 0)
                for i in range(T):
                    if i + 1 < T:
                        weigh(h, i + 1)
                    n = T * h + i
                    for s in range(2):
                        m = 2 * n + s
                        dve.wait_ge(squares, m + 1 + 1)
                        dve.tensor_scalar(mse[:, s:s + 1], ss[:, s:s + 1], 1.0 / DV, EPS, ALU.mult, ALU.add).then_inc(ms_ready, 1)
                        dve.wait_ge(root_ready, m + 1)
                        dve.reciprocal(rinv[:, s:s + 1], root[:, s:s + 1]).then_inc(rinv_ready, 1)
                        dve.wait_ge(rinv_ready, m + 1)
                        dve.scalar_tensor_tensor(read[:, s], y_ps[s], rinv[:, s:s + 1], gate[:, s, i], ALU.mult,
                                                 ALU.mult).then_inc(read_ready, 1)
                    dve.wait_ge(read_ready, 2 * (n + 1) + 1)
                    if i >= 2:
                        dve.wait_ge(o_turned, n)
                    else:
                        dve.wait_ge(o_turned, T * h + 1)
                    dve.tensor_tensor(o[:, i % 2], read[:, 0], read[:, 1], ALU.add).then_inc(o_ready, 1)
                    dve.wait_ge(o_ready, n + 1 + 1)
                    if i == 1 and more:
                        split(1, PIECES * (h + 1) + 1)

            split(0, 0)
            split(1, 1)
            dve.wait_ge(lg_step, 1)
            dve.tensor_scalar(lg[:], lgp[:], -1.0, None, ALU.mult).then_inc(lg_step, 1)
            with dve.Fori(0, H - 1) as h:
                head(h, more=True)
            head(H - 1, more=False)


def project_out(k, kt, w, gate_row, mod_dram, x_sb, tiles, oT=None, oT_dram=None, x_dram=None):
    nc = k.nc
    n = len(tiles)
    KP = 4
    pieces = kt // KP
    streams = sorted({int(t >= TC) for t in tiles})
    with ExitStack() as ctx:
        raw_w = k.sb(ctx, "raw_wo", [P, KP, NC])
        raw_o = k.sb(ctx, "raw_oT", [P, KP, n * P]) if oT is None else None
        w_hi, w_lo = k.sb(ctx, "wo_hi", [P, 2, KP, NC], F32R), k.sb(ctx, "wo_lo", [P, 2, KP, NC], F32R)
        o_hi, o_lo = k.sb(ctx, "oT_hi", [P, kt, n * P], F32R), k.sb(ctx, "oT_lo", [P, kt, n * P], F32R)
        gate = k.sb(ctx, "gate", [P, 2, D])
        gated = k.sb(ctx, "gated", [P, 2, NC])
        acc = k.ps(ctx, "acc", [P, 8, NC])
        w_in, o_in = k.sem("wo_in"), k.sem("oT_in")
        w_hi_ready, w_ready, o_hi_ready, o_split = (k.sem(x) for x in ("w_hi_ready", "w_ready", "o_hi_ready", "o_split"))
        x_in, gate_in = k.sem("x_in"), k.sem("gate_in")
        product, w_used, gated_ready, x_ready = k.sem("product"), k.sem("w_used"), k.sem("gated_ready"), k.sem("x_ready")
        block = ctx.enter_context(nc.Block())

        def o_piece(q):
            return raw_o[:] if oT is None else oT[:, q * KP:(q + 1) * KP]

        @block.sync
        def _(sp):
            for j in range(2):
                for q in range(pieces):
                    m = j * pieces + q
                    if m == pieces - 1:
                        for s in streams:
                            sp.dma_start(gate[:, s], mod_dram[s, gate_row[0]][gate_row[1] * D:(gate_row[1] + 1) * D].partition_broadcast(P)).then_inc(gate_in, 16)
                        if x_dram is not None:
                            sp.dma_start(x_sb[:, 0:TC], x_dram[0].rearrange("b (t p) d -> p (b t) d", p=P)).then_inc(x_in, 16)
                            sp.dma_start(x_sb[:, TC:T], x_dram[1].rearrange("b (t p) d -> p (b t) d", p=P)).then_inc(x_in, 16)
                    if m:
                        sp.wait_ge(w_ready, m)
                    sp.dma_start(raw_w[:], w.rearrange("(k p) n -> p k n", p=P)[:, q * KP:(q + 1) * KP, j * NC:(j + 1) * NC]).then_inc(w_in, 16)
                    if j == 0 and oT is None:
                        if q:
                            sp.wait_ge(o_split, q)
                        sp.dma_start(raw_o[:], oT_dram[q]).then_inc(o_in, 16)

        @block.tensor
        def _(pe):
            for j in range(2):
                for q in range(pieces):
                    slot = (j * pieces + q) % 2
                    pe.wait_ge(w_ready, j * pieces + q + 1)
                    if j == 0:
                        pe.wait_ge(o_split, q + 1)
                    for i in range(n):
                        m = j * n + i
                        if q == 0 and m >= 8:
                            pe.wait_ge(gated_ready, m - 7)
                        at = slice(i * P, (i + 1) * P)
                        for kk in range(q * KP, (q + 1) * KP):
                            mm = three_passes(pe, acc[:, m % 8], o_hi[:, kk, at], o_lo[:, kk, at], w_hi[:, slot, kk % KP], w_lo[:, slot, kk % KP],
                                              kk == 0, kk == kt - 1)
                        if q == pieces - 1:
                            mm.then_inc(product, 1)
                    if q < pieces - 1:
                        mm.then_inc(w_used, 1)

        @block.scalar
        def _(act):
            for m in range(2 * pieces):
                act.wait_ge(w_in, 16 * (m + 1))
                if m >= 2:
                    j, q = divmod(m - 2, pieces)
                    if q == pieces - 1:
                        act.wait_ge(product, (j + 1) * n)
                    else:
                        act.wait_ge(w_used, j * (pieces - 1) + q + 1)
                act.activation(w_hi[:, m % 2], raw_w[:], ACT.Copy).then_inc(w_hi_ready, 1)
                if m < pieces:
                    if oT is None:
                        act.wait_ge(o_in, 16 * (m + 1))
                    act.activation(o_hi[:, m * KP:(m + 1) * KP], o_piece(m), ACT.Copy).then_inc(o_hi_ready, 1)

        @block.vector
        def _(dve):
            def split(m):
                dve.wait_ge(w_hi_ready, m + 1)
                dve.tensor_tensor(w_lo[:, m % 2], raw_w[:], w_hi[:, m % 2].bitcast(F32), ALU.subtract).then_inc(w_ready, 1)
                if m < pieces:
                    dve.wait_ge(o_hi_ready, m + 1)
                    at = slice(m * KP, (m + 1) * KP)
                    dve.tensor_tensor(o_lo[:, at], o_piece(m), o_hi[:, at].bitcast(F32), ALU.subtract).then_inc(o_split, 1)

            def add(j):
                at = slice(j * NC, (j + 1) * NC)
                for i, t in enumerate(tiles):
                    m = j * n + i
                    dve.wait_ge(product, m + 1)
                    if m >= 2:
                        dve.wait_ge(x_ready, m - 1)
                    dve.tensor_tensor(gated[:, m % 2], acc[:, m % 8], gate[:, int(t >= TC), at], ALU.mult).then_inc(gated_ready, 1)
                    dve.wait_ge(gated_ready, m + 1)
                    dve.tensor_tensor(x_sb[:, t, at], x_sb[:, t, at], gated[:, m % 2], ALU.add).then_inc(x_ready, 1)

            for m in range(pieces + 1):
                split(m)
            dve.wait_ge(gate_in, 16 * len(streams))
            if x_dram is not None:
                dve.wait_ge(x_in, 32)
            add(0)
            for m in range(pieces + 1, 2 * pieces):
                split(m)
            add(1)


def route(k, ident, layer, hT, x_sb, tiles, book, mod_dram, rw, bias, lower):
    nc, a = k.nc, k.a
    n = len(tiles)
    NB = book.blocks
    NOWHERE = 1 << 20
    K2 = FF // P
    GU = 3
    streams = sorted({int(t >= TC) for t in tiles})
    with ExitStack() as ctx:
        w_gu = k.sb(ctx, "sh_gu", [P, KD, 2 * FF])
        w_down = k.sb(ctx, "sh_down", [P, K2, D])
        gate = k.sb(ctx, "gate", [P, 2, D])
        act_g = k.sb(ctx, "act_g", [P, GU, FF])
        prod = k.sb(ctx, "prod", [P, 2, FF])
        prodT = k.sb(ctx, "prodT", [P, 2, FF])
        gated = k.sb(ctx, "gated", [P, 2, D])
        before = k.sb(ctx, "before", [P, P], BF16)
        ones_bf = k.sb(ctx, "ones_bf", [P, P], BF16)
        ones = k.sb(ctx, "ones", [P, E])
        block_no = k.sb(ctx, "block_no", [P, 1])
        block_no_i = k.sb(ctx, "block_no_i", [P, 1], I32)
        entry = k.sb(ctx, "entry", [P, n, TOPK, 2], U32)
        nowhere = k.sb(ctx, "nowhere", [P, NB * 2], U32)
        s = k.sb(ctx, "s", [P, n, E])
        sel = k.sb(ctx, "sel", [P, n, E])
        best = k.sb(ctx, "best", [P, n, NG, 8])
        gs = k.sb(ctx, "gs", [P, n, NG])
        beats = k.sb(ctx, "beats", [P, n, NG, NG])
        ties = k.sb(ctx, "ties", [P, n, NG, NG])
        rank = k.sb(ctx, "rank", [P, n, NG])
        gmask = k.sb(ctx, "gmask", [P, n, NG])
        gpen = k.sb(ctx, "gpen", [P, n, NG])
        top = k.sb(ctx, "top", [P, n, 8])
        left = k.sb(ctx, "left", [P, n, E])
        mask = k.sb(ctx, "mask", [P, n, E])
        mask_bf = k.sb(ctx, "mask_bf", [P, n, E], BF16)
        w = k.sb(ctx, "w", [P, n, E])
        wsum = k.sb(ctx, "wsum", [P, n])
        winv = k.sb(ctx, "winv", [P, n])
        nblk = k.sb(ctx, "nblk", [P, E])
        end = k.sb(ctx, "end", [P, E])
        start = k.sb(ctx, "start", [P, E])
        pos = k.sb(ctx, "pos", [P, n, E])
        top_slot = k.sb(ctx, "top_slot", [P, n, TOPK])
        junk = k.sb(ctx, "junk", [P, E])
        below = k.sb(ctx, "below", [P, 1])
        expert_f = k.sb(ctx, "expert_f", [P, 1])
        expert_i = k.sb(ctx, "expert_i", [P, 1], I32)
        pairs_f = k.sb(ctx, "pairs_f", [P, 1])
        bank = k.ps(ctx, "bank", [P, 8, NC])
        logits = bank[:, 0, 0:n * E].rearrange("p (t e) -> p t e", t=n)
        counts = bank[:, 0, n * E:(n + 1) * E]
        ranks = bank[:, 1, 0:n * E].rearrange("p (t e) -> p t e", t=n)
        gu_ps = [bank[:, 2 + g] for g in range(GU)]
        turn_ps = bank[:, 5, 0:FF]
        y_ps = bank[:, 6:8].rearrange("p b n -> p (b n)")
        gu_in, down_in, gate_in = k.sem("gu_in"), k.sem("down_in"), k.sem("gate_in")
        gu_done, silu_ready, prod_ready, prod_turned, prodT_ready, y_done, gated_ready, x_ready = (
            k.sem(x) for x in ("gu_done", "silu_ready", "prod_ready", "prod_turned", "prodT_ready", "y_done", "gated_ready", "x_ready"))
        table_zeroed, scattered, expert_out = k.sem("table_zeroed"), k.sem("scattered"), k.sem("expert_out")
        made, logits_ready, s_ready, mask_ready, ranks_ready, slots_ready = (
            k.sem(x) for x in ("made", "logits_ready", "s_ready", "mask_ready", "ranks_ready", "slots_ready"))
        step, expert_ready = k.sem("step"), k.sem("expert_ready")
        block = ctx.enter_context(nc.Block())

        @block.sync
        def _(sp):
            sp.dma_start(w_gu[:], a["sh_w_gu"][layer].rearrange("(k p) n -> p k n", p=P)).then_inc(gu_in, 16)
            sp.wait_ge(made, 1)
            sp.dma_start(book.table_dram.rearrange("(p b) o -> p (b o)", p=P), nowhere[:]).then_inc(table_zeroed, 16)
            sp.dma_start(w_down[:], a["sh_w_down"][layer].rearrange("(k p) n -> p k n", p=P)).then_inc(down_in, 16)
            for s in streams:
                sp.dma_start(gate[:, s], mod_dram[s, layer][5 * D:6 * D].partition_broadcast(P)).then_inc(gate_in, 16)
            sp.wait_ge(expert_ready, 1)
            sp.dma_start(book.expert_dram, expert_i[:]).then_inc(expert_out, 16)
            sp.wait_ge(expert_out, 16)

        @block.gpsimd
        def _(pool):
            pool.memset(nowhere[:], NOWHERE).then_inc(made, 1)
            pool.memset(ones_bf[:], 1.0).then_inc(made, 1)
            pool.memset(ones[:], 1.0).then_inc(made, 1)
            pool.iota(block_no_i[:], [[0, 1]], base=0, channel_multiplier=1).then_inc(made, 1)
            pool.iota(entry[:, :, :, 0], [[P, n], [0, TOPK]], base=0, channel_multiplier=1).then_inc(made, 1)
            pool.iota(entry[:, :, :, 1], [[P * TOPK, n], [1, TOPK]], base=0, channel_multiplier=TOPK).then_inc(made, 1)
            pool.wait_ge(made, 2)
            pool.affine_select(out=before[:], in_=ones_bf[:], compare_op=ALU.is_gt, fill=0.0, base=0,
                               pattern=[[1, P]], channel_multiplier=-1).then_inc(made, 1)
            pool.wait_ge(made, 7)
            pool.wait_ge(table_zeroed, 16)
            pool.wait_ge(slots_ready, 1)
            for t in range(n):
                for j in range(TOPK):
                    pool.indirect_dma_start(book.table_dram, bass.IndirectOffsetOnAxis(ap=book.slot[:, t, j:j + 1], axis=0),
                                            entry[:, t, j], None).then_inc(scattered, 16)
            pool.wait_ge(scattered, 16 * n * TOPK)

        @block.tensor
        def _(pe):
            for t in range(n):
                for kk in range(KD):
                    mm = pe.matmul(logits[:, t], hT[:, kk, t * P:(t + 1) * P], rw[:, kk, :], start=(kk == 0), stop=(kk == KD - 1))
            mm.then_inc(logits_ready, 1)

            def gate_up(t):
                if t >= GU:
                    pe.wait_ge(prod_ready, t - GU + 1)
                for kk in range(KD):
                    mm = pe.matmul(gu_ps[t % GU], hT[:, kk, t * P:(t + 1) * P], w_gu[:, kk, :], start=(kk == 0), stop=(kk == KD - 1))
                mm.then_inc(gu_done, 1)

            pe.wait_ge(gu_in, 16)
            gate_up(0)
            gate_up(1)
            pe.wait_ge(mask_ready, 1)
            pe.wait_ge(made, 7)
            for t in range(n):
                for u in range(t + 1):
                    mm = pe.matmul(ranks[:, t], before[:] if u == t else ones_bf[:], mask_bf[:, u, :], start=(u == 0), stop=(u == t))
            for u in range(n):
                mm = pe.matmul(counts, ones_bf[:], mask_bf[:, u, :], start=(u == 0), stop=(u == n - 1))
            mm.then_inc(ranks_ready, 1)
            gate_up(2)
            pe.wait_ge(down_in, 16)
            for t in range(n):
                pe.wait_ge(prod_ready, t + 1)
                for kk in range(K2):
                    mm = pe.transpose(turn_ps[:, kk * P:(kk + 1) * P], prod[:, t % 2, kk * P:(kk + 1) * P], ident[:])
                mm.then_inc(prod_turned, 1)
                if t + GU < n:
                    gate_up(t + GU)
                pe.wait_ge(prodT_ready, t + 1)
                if t:
                    pe.wait_ge(gated_ready, t)
                for half in range(2):
                    for kk in range(K2):
                        mm = pe.matmul(y_ps[:, half * NC:(half + 1) * NC], prodT[:, t % 2, kk * P:(kk + 1) * P],
                                       w_down[:, kk, half * NC:(half + 1) * NC], start=(kk == 0), stop=(kk == K2 - 1))
                mm.then_inc(y_done, 1)

        @block.scalar
        def _(act):
            act.wait_ge(logits_ready, 1)
            act.activation(s[:], logits, ACT.Sigmoid).then_inc(s_ready, 1)

            def silu(t):
                act.wait_ge(gu_done, t + 1)
                if t >= GU:
                    act.wait_ge(prod_ready, t - GU + 1)
                act.activation(act_g[:, t % GU], gu_ps[t % GU][:, 0:FF], ACT.Silu).then_inc(silu_ready, 1)

            for t in range(GU):
                silu(t)
            for t in range(n):
                act.wait_ge(prod_turned, t + 1)
                if t >= 2:
                    act.wait_ge(y_done, t - 1)
                act.activation(prodT[:, t % 2], turn_ps, ACT.Copy).then_inc(prodT_ready, 1)
                if t + GU < n:
                    silu(t + GU)

        @block.vector
        def _(dve):
            count = [0]

            def then(ins):
                count[0] += 1
                ins.then_inc(step, 1)
                dve.wait_ge(step, count[0])

            dve.wait_ge(s_ready, 1)
            then(dve.tensor_tensor(sel[:], s[:], bc(bias[:], [P, n, E], [1]), ALU.add))
            for t in range(n):
                for g in range(NG):
                    ins = dve.max(best[:, t, g], sel[:, t, g * EG:(g + 1) * EG])
            then(ins)
            then(dve.tensor_tensor(gs[:], best[:, :, :, 0], best[:, :, :, 1], ALU.add))
            other = bc(gs[:], [P, n, NG, NG], [2])
            own = bc(gs[:], [P, n, NG, NG], [3])
            dve.tensor_tensor(beats[:], other, own, ALU.is_gt)
            then(dve.tensor_tensor(ties[:], other, own, ALU.is_equal))
            then(dve.tensor_tensor(ties[:], ties[:], bc(lower[:], [P, n, NG, NG], [1]), ALU.mult))
            then(dve.tensor_tensor(beats[:], beats[:], ties[:], ALU.add))
            then(dve.tensor_reduce(rank[:], beats[:], AX_X, ALU.add))
            then(dve.tensor_scalar(gmask[:], rank[:], float(TOPG), None, ALU.is_lt))
            then(dve.tensor_scalar(gpen[:], gmask[:], 1e30, -1e30, ALU.mult, ALU.add))
            sel_g = sel[:].rearrange("p t (g e) -> p t g e", g=NG)
            then(dve.tensor_tensor(sel_g, sel_g, bc(gmask[:], [P, n, NG, EG], [3]), ALU.mult))
            then(dve.tensor_tensor(sel_g, sel_g, bc(gpen[:], [P, n, NG, EG], [3]), ALU.add))
            for t in range(n):
                ins = dve.max(top[:, t], sel[:, t])
            then(ins)
            for t in range(n):
                ins = dve.match_replace(left[:, t], top[:, t], sel[:, t], -3e38)
            then(ins)
            then(dve.tensor_tensor(mask[:], left[:], sel[:], ALU.is_lt))
            dve.tensor_copy(mask_bf[:], mask[:]).then_inc(mask_ready, 1)
            then(dve.tensor_tensor(w[:], s[:], mask[:], ALU.mult))
            then(dve.tensor_reduce(wsum[:], w[:], AX_X, ALU.add))
            then(dve.reciprocal(winv[:], wsum[:]))
            then(dve.tensor_scalar(winv[:], winv[:], ROUTED_SCALE, None, ALU.mult))
            then(dve.tensor_tensor(w[:], w[:], bc(winv[:], [P, n, E], [2]), ALU.mult))
            dve.wait_ge(made, 7)
            then(dve.tensor_copy(block_no[:], block_no_i[:]))
            dve.wait_ge(ranks_ready, 1)
            then(dve.tensor_scalar(nblk[:], counts, 0.0, None, ALU.is_gt))
            for m in range(1, n):
                then(dve.scalar_tensor_tensor(nblk[:], counts, float(m * P), nblk[:], ALU.is_gt, ALU.add))
            then(dve.tensor_tensor_scan(end[:], ones[:], nblk[:], 0.0, ALU.mult, ALU.add))
            then(dve.tensor_tensor(start[:], end[:], nblk[:], ALU.subtract))
            then(dve.tensor_scalar(start[:], start[:], float(P), 1.0, ALU.mult, ALU.add))
            then(dve.tensor_tensor(pos[:], ranks, bc(start[:], [P, n, E], [1]), ALU.add))
            then(dve.tensor_tensor(pos[:], pos[:], mask[:], ALU.mult))
            for t in range(n):
                ins = dve.max(top_slot[:, t], pos[:, t])
            then(ins)
            then(dve.tensor_scalar(book.slot[:], top_slot[:], -1.0, None, ALU.add))
            dve.sem_inc(slots_ready, 1)
            then(dve.tensor_scalar(junk[:], end[:], block_no[:, 0:1], None, ALU.is_le))
            then(dve.tensor_reduce(below[:], junk[:], AX_X, ALU.add))
            then(dve.tensor_scalar(expert_f[:], below[:], float(E - 1), None, ALU.min))
            then(dve.tensor_copy(expert_i[:], expert_f[:]))
            dve.sem_inc(expert_ready, 1)
            then(dve.tensor_scalar(pairs_f[:], end[:, E - 1:E], 0.5, -0.75, ALU.mult, ALU.add))
            then(dve.tensor_copy(book.last_pair[:, 0:1], pairs_f[:]))
            then(dve.tensor_scalar(pairs_f[:], pairs_f[:], -1.0, None, ALU.add))
            then(dve.tensor_copy(book.last_pair[:, 1:2], pairs_f[:]))

            def multiply(t):
                dve.wait_ge(silu_ready, t + 1)
                if t >= 2:
                    dve.wait_ge(prod_turned, t - 1)
                dve.tensor_tensor(prod[:, t % 2], act_g[:, t % GU], gu_ps[t % GU][:, FF:2 * FF], ALU.mult).then_inc(prod_ready, 1)

            multiply(0)
            multiply(1)
            dve.wait_ge(gate_in, 16 * len(streams))
            for i, t in enumerate(tiles):
                for j in range(TOPK):
                    then(dve.scalar_tensor_tensor(junk[:], pos[:, i], top_slot[:, i, j:j + 1], w[:, i], ALU.is_equal, ALU.mult,
                                                  accum_out=book.weight[:, i, j:j + 1]))
                if i + 2 < n:
                    multiply(i + 2)
                dve.wait_ge(y_done, i + 1)
                if i >= 2:
                    dve.wait_ge(x_ready, i - 1)
                dve.tensor_tensor(gated[:, i % 2], y_ps, gate[:, int(t >= TC)], ALU.mult).then_inc(gated_ready, 1)
                dve.wait_ge(gated_ready, i + 1)
                dve.tensor_tensor(x_sb[:, t], x_sb[:, t], gated[:, i % 2], ALU.add).then_inc(x_ready, 1)


def experts(k, ident, layer, book, h_dram, y_dram):
    nc, a = k.nc, k.a
    K2 = FF // P
    HK = KD // 2
    with ExitStack() as ctx:
        raw_gu = k.sb(ctx, "raw_gu", [P, 2, HK, 2 * FF])
        raw_down = k.sb(ctx, "raw_down", [P, K2, D])
        gu_hi = k.sb(ctx, "gu_hi", [P, 2, KD, 2 * FF], F32R)
        gu_lo = k.sb(ctx, "gu_lo", [P, 2, KD, 2 * FF], F32R)
        down_hi = k.sb(ctx, "down_hi", [P, 2, K2, D], F32R)
        down_lo = k.sb(ctx, "down_lo", [P, 2, K2, D], F32R)
        expert = k.sb(ctx, "expert", [1, P], I32)
        table = k.sb(ctx, "table", [book.blocks, P, 2], U32)
        table_f = k.sb(ctx, "table_f", [book.blocks, 2, P])
        row_of = k.sb(ctx, "row_of", [P, 2, book.blocks], U32)
        from_row = k.sb(ctx, "from_row", [P, 2], U32)
        to_row = k.sb(ctx, "to_row", [P, 2], U32)
        rows = k.sb(ctx, "rows", [P, 2, D])
        xT_hi = k.sb(ctx, "xT_hi", [P, 2, D], F32R)
        xT_lo = k.sb(ctx, "xT_lo", [P, 2, D], F32R)
        act_g = k.sb(ctx, "act_g", [P, FF])
        prod = k.sb(ctx, "prod", [P, FF])
        prodT_hi = k.sb(ctx, "prodT_hi", [P, FF], F32R)
        prodT_lo = k.sb(ctx, "prodT_lo", [P, FF], F32R)
        y = k.sb(ctx, "y", [P, 2, D])
        bank = k.ps(ctx, "bank", [P, 8, NC])
        turn_ps = bank[:, 0:2].rearrange("p b n -> p (b n)")
        gu_ps = [bank[:, 2], bank[:, 3]]
        small_ps = bank[:, 4, 0:FF]
        y_ps = bank[:, 6:8].rearrange("p b n -> p (b n)")
        gu_in = [k.sem("gu_in0"), k.sem("gu_in1")]
        down_in, expert_in = k.sem("down_in"), k.sem("expert_in")
        gu_hi_ready = [k.sem("gu_hi_ready0"), k.sem("gu_hi_ready1")]
        gu_ready = [k.sem("gu_ready0"), k.sem("gu_ready1")]
        down_hi_ready, down_ready = k.sem("down_hi_ready"), k.sem("down_ready")
        table_in, table_f_ready, table_turned, row_of_ready = (k.sem(x) for x in ("table_in", "table_f_ready", "table_turned", "row_of_ready"))
        from_ready, to_ready = k.sem("from_ready"), k.sem("to_ready")
        rows_in = [k.sem("rows_in0"), k.sem("rows_in1")]
        y_out, y_left = k.sem("y_out"), k.sem("y_left")
        passed, cleared = k.sem("passed"), k.sem("cleared")
        turned, xT_hi_ready, xT_ready, gu_done, silu_ready, prod_ready = (
            k.sem(x) for x in ("turned", "xT_hi_ready", "xT_ready", "gu_done", "silu_ready", "prod_ready"))
        prod_turned, prodT_hi_ready, prodT_ready, y_done, y_ready = (
            k.sem(x) for x in ("prod_turned", "prodT_hi_ready", "prodT_ready", "y_done", "y_ready"))
        block = ctx.enter_context(nc.Block())
        gu_w = a["exp_w_gu"][layer].rearrange("e (s k p) n -> e s p k n", s=2, p=P)
        down_w = a["exp_w_down"][layer].rearrange("e (k p) n -> e p k n", p=P)

        def last_pair(eng):
            return eng.value_load(book.last_pair[0:1, 0:1], min_val=1, max_val=book.blocks // 2 - 1)

        @block.sync
        def _(sp):
            last = last_pair(sp)

            def expert_of(b):
                return sp.value_load(expert[0:1, bass.ds(b, 1)], min_val=0, max_val=E - 1)

            def load_if_new(e, before, dst, src, arrived):
                with sp.If(e > before):
                    sp.dma_start(dst, src.rearrange("o p k n -> p (o k) n")).then_inc(arrived, 16)
                with sp.If(e <= before):
                    sp.sem_inc(arrived, 16)

            def load_gate_up(b, e, before):
                for s in range(2):
                    sp.wait_ge(gu_ready[s], b)
                    sp.sem_inc(passed, 1)
                    load_if_new(e, before, raw_gu[:, s], gu_w[bass.ds(e, 1), s], gu_in[s])

            def load_down(b, e, before):
                sp.wait_ge(down_ready, b)
                sp.sem_inc(passed, 1)
                load_if_new(e, before, raw_down[:], down_w[bass.ds(e, 1)], down_in)

            sp.dma_start(expert[:], book.expert_dram.rearrange("b o -> o b")).then_inc(expert_in, 16)
            sp.dma_start(table[:], book.table_dram.rearrange("(b p) o -> b p o", p=P)).then_inc(table_in, 16)
            sp.wait_ge(expert_in, 16)
            e0, e1 = expert_of(0), expert_of(1)
            for s in range(2):
                sp.dma_start(raw_gu[:, s], gu_w[bass.ds(e0, 1), s].rearrange("o p k n -> p (o k) n")).then_inc(gu_in[s], 16)
            sp.dma_start(raw_down[:], down_w[bass.ds(e0, 1)].rearrange("o p k n -> p (o k) n")).then_inc(down_in, 16)
            load_gate_up(1, e1, e0)
            with sp.Fori(0, last) as i:
                e = [expert_of(2 * i + n) for n in range(4)]
                for j in range(2):
                    b = 2 * i + j
                    load_down(b + 1, e[j + 1], e[j])
                    load_gate_up(b + 2, e[j + 2], e[j + 1])
            load_down(2 * last + 1, expert_of(2 * last + 1), expert_of(2 * last))

        @block.gpsimd
        def _(pool):
            last = last_pair(pool)
            before_last = pool.value_load(book.last_pair[0:1, 1:2], min_val=0, max_val=book.blocks // 2 - 2)

            def gather(i, j, first=False):
                b = 2 * i + j
                if not first:
                    pool.wait_ge(turned, b - 1)
                pool.tensor_copy(from_row[:, j:j + 1], row_of[:, 0, bass.ds(b, 1)]).then_inc(from_ready, 1)
                pool.wait_ge(from_ready, b + 1)
                pool.sem_inc(passed, 1)
                pool.indirect_dma_start(rows[:, j], None, h_dram, bass.IndirectOffsetOnAxis(ap=from_row[:, j:j + 1], axis=0),
                                        bounds_check=h_dram.shape[0] - 1, oob_is_err=False).then_inc(rows_in[j], 16)

            def scatter(i, j, first=False):
                b = 2 * i + j
                if not first:
                    pool.wait_ge(y_out, 16 * b)
                    pool.sem_inc(y_left, 1)
                pool.tensor_copy(to_row[:, j:j + 1], row_of[:, 1, bass.ds(b, 1)]).then_inc(to_ready, 1)
                pool.wait_ge(to_ready, b + 1)
                pool.wait_ge(y_ready, b + 2)
                pool.sem_inc(passed, 1)
                pool.indirect_dma_start(y_dram, bass.IndirectOffsetOnAxis(ap=to_row[:, j:j + 1], axis=0), y[:, j], None,
                                        bounds_check=book.picks - 1, oob_is_err=False).then_inc(y_out, 16)

            pool.sem_inc(y_left, 2)
            pool.memset(rows[:], 0.0).then_inc(cleared, 1)
            pool.wait_ge(cleared, 1)
            pool.wait_ge(row_of_ready, 1)
            for i in range(2):
                for j in range(2):
                    gather(i, j, first=(i == 0))
            for j in range(2):
                gather(2, j)
                scatter(0, j, first=(j == 0))
            with pool.Fori(1, before_last) as i:
                for j in range(2):
                    gather(i + 2, j)
                    scatter(i, j)
            for i in (before_last, last):
                for j in range(2):
                    scatter(i, j)
            pool.wait_ge(y_out, 16 * 2 * (last + 1))
            pool.sem_inc(passed, 1)

        @block.tensor
        def _(pe):
            last = last_pair(pe)

            def turn_rows(i, j, first=False):
                pe.wait_ge(rows_in[j], 16 * (i + 1))
                if not first:
                    pe.wait_ge(xT_ready, 2 * i + j)
                for kk in range(KD):
                    mm = pe.transpose(turn_ps[:, kk * P:(kk + 1) * P], rows[:, j, kk * P:(kk + 1) * P], ident[:])
                mm.then_inc(turned, 1)

            def gate_up(i, j):
                b = 2 * i + j
                pe.wait_ge(gu_ready[0], b + 1)
                pe.wait_ge(xT_ready, b + 1)
                for kk in range(KD):
                    if kk == HK:
                        pe.wait_ge(gu_ready[1], b + 1)
                    x_at = slice(kk * P, (kk + 1) * P)
                    mm = three_passes(pe, gu_ps[j], xT_hi[:, j, x_at], xT_lo[:, j, x_at], gu_hi[:, j, kk], gu_lo[:, j, kk], kk == 0, kk == KD - 1)
                mm.then_inc(gu_done, 1)

            def turn_prod(i, j):
                pe.wait_ge(prod_ready, 2 * i + j + 1)
                for kk in range(K2):
                    mm = pe.transpose(small_ps[:, kk * P:(kk + 1) * P], prod[:, kk * P:(kk + 1) * P], ident[:])
                mm.then_inc(prod_turned, 1)

            def down(i, j):
                b = 2 * i + j
                pe.wait_ge(down_ready, b + 1)
                pe.wait_ge(prodT_ready, b + 1)
                pe.wait_ge(y_ready, b + 1)
                for half in range(2):
                    at = slice(half * NC, (half + 1) * NC)
                    for kk in range(K2):
                        x_at = slice(kk * P, (kk + 1) * P)
                        mm = three_passes(pe, y_ps[:, at], prodT_hi[:, x_at], prodT_lo[:, x_at], down_hi[:, j, kk, at], down_lo[:, j, kk, at],
                                   kk == 0, kk == K2 - 1)
                mm.then_inc(y_done, 1)

            pe.wait_ge(table_f_ready, 1)
            for way in range(2):
                mm = pe.transpose(small_ps[:, way * book.blocks:(way + 1) * book.blocks], table_f[:, way],
                                  ident[0:book.blocks, 0:book.blocks])
            mm.then_inc(table_turned, 1)
            turn_rows(0, 0, first=True)
            turn_rows(0, 1)
            gate_up(0, 0)
            with pe.Fori(0, last) as i:
                for j in range(2):
                    turn_rows(i + 1, j)
                    turn_prod(i, j)
                    gate_up(i + j, 1 - j)
                    down(i, j)
            turn_prod(last, 0)
            gate_up(last, 1)
            down(last, 0)
            turn_prod(last, 1)
            down(last, 1)

        @block.scalar
        def _(act):
            last = last_pair(act)
            act.sem_inc(y_ready, 1)

            def split_gate_up(i, j, s):
                b = 2 * i + j
                act.wait_ge(gu_in[s], 16 * (b + 1))
                act.activation(gu_hi[:, j, s * HK:(s + 1) * HK], raw_gu[:, s], ACT.Copy).then_inc(gu_hi_ready[s], 1)

            def split_down(i, j):
                act.wait_ge(down_in, 16 * (2 * i + j + 1))
                act.activation(down_hi[:, j], raw_down[:], ACT.Copy).then_inc(down_hi_ready, 1)

            def copy_xT(i, j, wait=True):
                b = 2 * i + j
                act.wait_ge(turned, b + 1)
                if wait:
                    act.wait_ge(gu_done, b - 1)
                act.activation(xT_hi[:, j], turn_ps, ACT.Copy).then_inc(xT_hi_ready, 1)

            def silu(i, j):
                act.wait_ge(gu_done, 2 * i + j + 1)
                act.activation(act_g[:], gu_ps[j][:, 0:FF], ACT.Silu).then_inc(silu_ready, 1)

            def copy_prodT(i, j):
                act.wait_ge(prod_turned, 2 * i + j + 1)
                act.activation(prodT_hi[:], small_ps, ACT.Copy).then_inc(prodT_hi_ready, 1)

            def copy_y(i, j):
                act.wait_ge(y_done, 2 * i + j + 1)
                act.wait_ge(y_left, 2 * i + j + 1)
                act.activation(y[:, j], y_ps, ACT.Copy).then_inc(y_ready, 1)

            split_gate_up(0, 0, 0)
            split_gate_up(0, 0, 1)
            copy_xT(0, 0, wait=False)
            copy_xT(0, 1, wait=False)
            split_down(0, 0)
            silu(0, 0)
            split_gate_up(0, 1, 0)
            split_gate_up(0, 1, 1)
            with act.Fori(0, last) as i:
                for j in range(2):
                    copy_xT(i + 1, j)
                    copy_prodT(i, j)
                    split_down(i + j, 1 - j)
                    split_gate_up(i + 1, j, 0)
                    silu(i + j, 1 - j)
                    split_gate_up(i + 1, j, 1)
                    copy_y(i, j)
            copy_prodT(last, 0)
            split_down(last, 1)
            silu(last, 1)
            copy_y(last, 0)
            copy_prodT(last, 1)
            copy_y(last, 1)

        @block.vector
        def _(dve):
            last = last_pair(dve)

            def split_gate_up(i, j, s):
                b = 2 * i + j
                at = slice(s * HK, (s + 1) * HK)
                dve.wait_ge(gu_hi_ready[s], b + 1)
                dve.tensor_tensor(gu_lo[:, j, at], raw_gu[:, s], gu_hi[:, j, at].bitcast(F32), ALU.subtract).then_inc(gu_ready[s], 1)

            def split_down(i, j):
                dve.wait_ge(down_hi_ready, 2 * i + j + 1)
                dve.tensor_tensor(down_lo[:, j], raw_down[:], down_hi[:, j].bitcast(F32), ALU.subtract).then_inc(down_ready, 1)

            def copy_xT(i, j):
                dve.wait_ge(xT_hi_ready, 2 * i + j + 1)
                dve.tensor_tensor(xT_lo[:, j], turn_ps, xT_hi[:, j].bitcast(F32), ALU.subtract).then_inc(xT_ready, 1)

            def multiply(i, j):
                dve.wait_ge(silu_ready, 2 * i + j + 1)
                dve.tensor_tensor(prod[:], act_g[:], gu_ps[j][:, FF:2 * FF], ALU.mult).then_inc(prod_ready, 1)

            def copy_prodT(i, j):
                dve.wait_ge(prodT_hi_ready, 2 * i + j + 1)
                dve.tensor_tensor(prodT_lo[:], small_ps, prodT_hi[:].bitcast(F32), ALU.subtract).then_inc(prodT_ready, 1)

            dve.wait_ge(table_in, 16)
            dve.tensor_copy(table_f[:].rearrange("b o p -> b p o"), table[:]).then_inc(table_f_ready, 1)
            dve.wait_ge(table_turned, 1)
            dve.tensor_copy(row_of[:].rearrange("p o b -> p (o b)"), small_ps[:, 0:2 * book.blocks]).then_inc(row_of_ready, 1)
            split_gate_up(0, 0, 0)
            split_gate_up(0, 0, 1)
            copy_xT(0, 0)
            copy_xT(0, 1)
            split_down(0, 0)
            multiply(0, 0)
            split_gate_up(0, 1, 0)
            split_gate_up(0, 1, 1)
            with dve.Fori(0, last) as i:
                for j in range(2):
                    copy_xT(i + 1, j)
                    copy_prodT(i, j)
                    split_down(i + j, 1 - j)
                    split_gate_up(i + 1, j, 0)
                    multiply(i + j, 1 - j)
                    split_gate_up(i + 1, j, 1)
            copy_prodT(last, 0)
            split_down(last, 1)
            multiply(last, 1)
            copy_prodT(last, 1)


def combine(k, layer, x_sb, tiles, book, y_dram, mod_dram, out=None):
    nc = k.nc
    n = len(tiles)
    HALF = TOPK // 2
    RING = 4
    streams = sorted({int(t >= TC) for t in tiles})
    with ExitStack() as ctx:
        gate = k.sb(ctx, "gate", [P, 2, D])
        picked = k.sb(ctx, "picked", [P, RING, HALF, D])
        acc = k.sb(ctx, "acc", [P, D])
        gate_in, added = k.sem("gate_in"), k.sem("added")
        picked_in = [k.sem(f"picked_in{r}") for r in range(RING)]
        block = ctx.enter_context(nc.Block())
        y_rows = y_dram[0:book.picks].rearrange("(t p s j) d -> t s p j d", p=P, s=2, j=HALF)
        STEPS = TOPK + 2
        out_done = k.sem("out_done")

        @block.sync
        def _(sp):
            for t in range(n):
                if t == 1:
                    for s in streams:
                        sp.dma_start(gate[:, s], mod_dram[s, layer][5 * D:6 * D].partition_broadcast(P)).then_inc(gate_in, 16)
                for s in range(2):
                    m = 2 * t + s
                    if m >= RING:
                        sp.wait_ge(added, STEPS * ((m - RING) // 2) + HALF * (s + 1))
                    sp.dma_start(picked[:, m % RING], y_rows[t, s]).then_inc(picked_in[m % RING], 16)

        if out is not None:
            @block.scalar
            def _(act):
                for i, t in enumerate(tiles):
                    act.wait_ge(added, STEPS * (i + 1))
                    act.dma_start(out[0, i * P:(i + 1) * P, :], x_sb[:, t]).then_inc(out_done, 16)
                act.wait_ge(out_done, 16 * n)

        @block.vector
        def _(dve):
            count = [0]

            def then(ins):
                count[0] += 1
                ins.then_inc(added, 1)
                dve.wait_ge(added, count[0])

            for i, t in enumerate(tiles):
                for j in range(TOPK):
                    m = 2 * i + j // HALF
                    if j % HALF == 0:
                        dve.wait_ge(picked_in[m % RING], 16 * (m // RING + 1))
                    pick, weight = picked[:, m % RING, j % HALF], book.weight[:, i, j:j + 1]
                    if j == 0:
                        then(dve.tensor_scalar(acc[:], pick, weight, None, ALU.mult))
                    else:
                        then(dve.scalar_tensor_tensor(acc[:], pick, weight, acc[:], ALU.mult, ALU.add))
                if i == 0:
                    dve.wait_ge(gate_in, 16 * len(streams))
                then(dve.tensor_tensor(acc[:], acc[:], gate[:, int(t >= TC)], ALU.mult))
                then(dve.tensor_tensor(x_sb[:, t], x_sb[:, t], acc[:], ALU.add))


class Book:

    def __init__(self, k, ctx, name, n):
        self.picks = n * P * TOPK
        self.blocks = self.picks // P + E
        nc = k.nc
        self.slot = k.sb(ctx, "slot", [P, n, TOPK], U32)
        self.weight = k.sb(ctx, "weight", [P, n, TOPK])
        self.last_pair = k.sb(ctx, "last_pair", [P, 2], I32)
        self.table_dram = nc.dram_tensor(f"table_{name}", [self.blocks * P, 2], U32).ap()
        self.expert_dram = nc.dram_tensor(f"expert_{name}", [P, 1], I32).ap()


def expert_layer(k, ident, layer, x_sb, tiles, mod_dram, y_dram, out=None):
    nc = k.nc
    n = len(tiles)
    with ExitStack() as ctx:
        book = Book(k, ctx, str(layer), n)
        h_dram = nc.dram_tensor(f"h_{layer}", [n * P, D], F32).ap()
        with ExitStack() as normed:
            hT = k.sb(normed, "hT", [P, KD, n * P])
            rw = k.sb(normed, "router_w", [P, KD, E])
            bias = k.sb(normed, "router_bias", [P, E])
            lower = k.sb(normed, "lower", [P, NG, NG])
            loads = ((rw[:], k.a["router_w"][layer].rearrange("(k p) e -> p k e", p=P)),
                     (bias[:], k.a["router_bias"][layer].partition_broadcast(P)),
                     (lower[:], k.c["lower"].rearrange("p (g f) -> p g f", g=NG)))
            norm_modulate(k, ident, layer, 3, k.a["norm_ffn"][layer], mod_dram, tiles, x_sb=x_sb, hT=hT, h_dram=h_dram, prefetch=loads)
            route(k, ident, layer, hT, x_sb, tiles, book, mod_dram, rw, bias, lower)
        experts(k, ident, layer, book, h_dram, y_dram)
        combine(k, layer, x_sb, tiles, book, y_dram, mod_dram, out)


def rotate(eng, then, dst, src, cos, sin, tmp):
    then(eng.tensor_tensor(tmp, src, cos, ALU.mult))
    for b in range(2):
        then(eng.tensor_tensor(dst[:, :, :, b], src[:, :, :, 1 - b], sin[:, :, :, b], ALU.mult))
    then(eng.tensor_tensor(dst, dst, tmp, ALU.add))


def latent_down(k, ident, hT, qaT, kvaT, krT):
    nc, a, c = k.nc, k.a, k.c
    MLA_IN = QR + KVR + ROPE
    with ExitStack() as ctx:
        w = k.sb(ctx, "w_in", [P, KD, MLA_IN])
        gq = k.sb(ctx, "gq", [P, QR])
        gkv = k.sb(ctx, "gkv", [P, KVR])
        gkr = k.sb(ctx, "gkr", [P, ROPE])
        cos = k.sb(ctx, "cos", [P, TL, 2, 2, ROPE // 4])
        sin = k.sb(ctx, "sin", [P, TL, 2, 2, ROPE // 4])
        low = k.sb(ctx, "low", [P, T, MLA_IN])
        kr = k.sb(ctx, "kr", [P, T, ROPE])
        krt = k.sb(ctx, "krt", [P, TL, ROPE])
        krr = k.sb(ctx, "krr", [P, TL, ROPE])
        square = k.sb(ctx, "square", [P, QR])
        S = TL + 2 * T
        ms, mse, root, rinv = (k.sb(ctx, x, [P, S]) for x in ("ms", "mse", "root", "rinv"))
        bank = k.ps(ctx, "bank", [P, 8, NC])
        turn_ps = [bank[:, 4:6].rearrange("p b n -> p (b n)"), bank[:, 6:8].rearrange("p b n -> p (b n)")]
        w_in, rows_in = k.sem("w_in"), k.sem("rows_in")
        product, copied, squared = k.sem("product"), k.sem("copied"), k.sem("squared")
        ms_ready, root_ready, step, tile_ready, tile_turned, tile_out = (
            k.sem(x) for x in ("ms_ready", "root_ready", "step", "tile_ready", "tile_turned", "tile_out"))
        items = []
        for t in range(T):
            items.append((t, t % 2, slice(QR, MLA_IN)))
            if t >= TC:
                items.append((t, 2 + t % 2, slice(0, QR)))
        last_user = {}
        block = ctx.enter_context(nc.Block())

        @block.sync
        def _(sp):
            for half in range(2):
                ks = slice(half * KD // 2, (half + 1) * KD // 2)
                sp.dma_start(w[:, ks], a["mla_w_in"][0].rearrange("(k p) n -> p k n", p=P)[:, ks]).then_inc(w_in, 16)
            sp.dma_start(gq[:], a["mla_q_a_norm"][0].partition_broadcast(P)).then_inc(rows_in, 16)
            sp.dma_start(gkv[:], a["mla_kv_a_norm"][0].partition_broadcast(P)).then_inc(rows_in, 16)
            sp.dma_start(gkr[:], a["mla_k_norm"][0, NOPE:QK].partition_broadcast(P)).then_inc(rows_in, 16)
            sp.dma_start(cos[:], c["mla_cos"].rearrange("p (t a b n) -> p t a b n", t=TL, a=2, b=2)).then_inc(rows_in, 16)
            sp.dma_start(sin[:], c["mla_sin"].rearrange("p (t a b n) -> p t a b n", t=TL, a=2, b=2)).then_inc(rows_in, 16)

        @block.tensor
        def _(pe):
            pe.wait_ge(w_in, 32)
            for m, (t, b, cols) in enumerate(items):
                if b in last_user:
                    pe.wait_ge(copied, last_user[b] + 1)
                last_user[b] = m
                for kk in range(KD):
                    mm = pe.matmul(bank[:, b, 0:cols.stop - cols.start], hT[:, kk, t * P:(t + 1) * P], w[:, kk, cols],
                                   start=(kk == 0), stop=(kk == KD - 1))
                mm.then_inc(product, 1)
            for t in range(T):
                pe.wait_ge(tile_ready, t + 1)
                if t >= 2:
                    pe.wait_ge(tile_out, t - 1)
                for j in range(0 if t >= TC else 3, 5):
                    pe.transpose(turn_ps[t % 2][:, j * P:(j + 1) * P], low[:, t, j * P:(j + 1) * P], ident[:])
                pe.transpose(turn_ps[t % 2][0:ROPE, 5 * P:6 * P], kr[:, t], ident[:]).then_inc(tile_turned, 1)

        @block.scalar
        def _(act):
            for m, (t, b, cols) in enumerate(items):
                act.wait_ge(copied, m + 1)
                if m:
                    act.wait_ge(squared, m)
                parts = [(0, QR, t - TC)] if b >= 2 else [(0, KVR, TL + t), (KVR, KVR + ROPE, TL + T + t)]
                for n, (lo, hi, col) in enumerate(parts):
                    ins = act.activation(square[:, 0:hi - lo] if not n else square[:, KVR:KVR + ROPE], low[:, t, cols.start + lo:cols.start + hi], ACT.Square,
                                         accum_out=ms[:, col:col + 1])
                ins.then_inc(squared, 1)
            act.wait_ge(ms_ready, 1)
            act.activation(root[:], mse[:], ACT.Sqrt).then_inc(root_ready, 1)
            for t in range(T):
                at = slice(t * P, (t + 1) * P)
                act.wait_ge(tile_turned, t + 1)
                ps = turn_ps[t % 2]
                if t >= TC:
                    act.activation(qaT[:, :, (t - TC) * P:(t - TC + 1) * P], ps[:, 0:3 * P].rearrange("p (k m) -> p k m", k=3), ACT.Copy)
                act.activation(kvaT[:, :, at], ps[:, 3 * P:5 * P].rearrange("p (k m) -> p k m", k=2), ACT.Copy)
                act.activation(krT[0:ROPE, at], ps[0:ROPE, 5 * P:6 * P], ACT.Copy).then_inc(tile_out, 1)

        @block.vector
        def _(dve):
            count = [0]

            def then(ins):
                count[0] += 1
                ins.then_inc(step, 1)
                dve.wait_ge(step, count[0])

            for m, (t, b, cols) in enumerate(items):
                dve.wait_ge(product, m + 1)
                dve.tensor_copy(low[:, t, cols], bank[:, b, 0:cols.stop - cols.start]).then_inc(copied, 1)
            dve.wait_ge(squared, len(items))
            dve.wait_ge(copied, len(items))
            for lo, hi, width in ((0, TL, QR), (TL, TL + T, KVR), (TL + T, S, ROPE)):
                then(dve.tensor_scalar(mse[:, lo:hi], ms[:, lo:hi], 1.0 / width, EPS, ALU.mult, ALU.add))
            dve.sem_inc(ms_ready, 1)
            dve.wait_ge(root_ready, 1)
            then(dve.reciprocal(rinv[:], root[:]))
            dve.wait_ge(rows_in, 80)
            for t in range(T):
                col = TL + T + t
                then(dve.scalar_tensor_tensor(kr[:, t], low[:, t, QR + KVR:MLA_IN], rinv[:, col:col + 1], gkr[:], ALU.mult, ALU.mult))
            split = "p t (a b n) -> p t a b n"
            rotate(dve, then, krr[:].rearrange(split, a=2, b=2), kr[:, TC:T].rearrange(split, a=2, b=2), cos[:], sin[:],
                   krt[:].rearrange(split, a=2, b=2))
            then(dve.tensor_copy(kr[:, TC:T], krr[:]))
            for t in range(T):
                if t >= TC:
                    dve.scalar_tensor_tensor(low[:, t, 0:QR], low[:, t, 0:QR], rinv[:, t - TC:t - TC + 1], gq[:], ALU.mult, ALU.mult)
                col = TL + t
                dve.scalar_tensor_tensor(low[:, t, QR:QR + KVR], low[:, t, QR:QR + KVR], rinv[:, col:col + 1], gkv[:],
                                         ALU.mult, ALU.mult).then_inc(tile_ready, 1)


def latent_up(k, qaT, kvaT, q_sb, kv_sb, rq, rk):
    nc, a = k.nc, k.a
    KQ, KK = QR // P, KVR // P
    with ExitStack() as ctx:
        wq = k.sb(ctx, "wq", [P, KQ, MH * QK])
        wkv = k.sb(ctx, "wkv", [P, KK, MH * (NOPE + MV)])
        square = k.sb(ctx, "square", [P, 2, MH * QK])
        msq, rootq = k.sb(ctx, "msq", [P, TL, MH, 2]), k.sb(ctx, "rootq", [P, TL, MH, 2])
        msk, rootk = k.sb(ctx, "msk", [P, T, MH]), k.sb(ctx, "rootk", [P, T, MH])
        bank = k.ps(ctx, "bank", [P, 2, 4 * NC])
        wq_in, wkv_in = k.sem("wq_in"), k.sem("wkv_in")
        product, copied, squared, reduced = k.sem("product"), k.sem("copied"), k.sem("squared"), k.sem("reduced")
        mean_ready, root_ready, step = k.sem("mean_ready"), k.sem("root_ready"), k.sem("step")
        items = [("q", t) for t in range(TL)] + [("kv", t) for t in range(T)]
        block = ctx.enter_context(nc.Block())

        @block.sync
        def _(sp):
            sp.dma_start(wq[:], a["mla_w_q_b"][0].rearrange("(k p) n -> p k n", p=P)).then_inc(wq_in, 16)
            sp.dma_start(wkv[:], a["mla_w_kv_b"][0].rearrange("(k p) n -> p k n", p=P)).then_inc(wkv_in, 16)

        @block.tensor
        def _(pe):
            for m, (what, t) in enumerate(items):
                if m == 0:
                    pe.wait_ge(wq_in, 16)
                if m == TL:
                    pe.wait_ge(wkv_in, 16)
                if m >= 2:
                    pe.wait_ge(copied, m - 1)
                x, w, kt = (qaT, wq, KQ) if what == "q" else (kvaT, wkv, KK)
                for n in range(w.shape[2] // NC):
                    for kk in range(kt):
                        mm = pe.matmul(bank[:, m % 2, n * NC:(n + 1) * NC], x[:, kk, t * P:(t + 1) * P], w[:, kk, n * NC:(n + 1) * NC],
                                       start=(kk == 0), stop=(kk == kt - 1))
                mm.then_inc(product, 1)

        @block.scalar
        def _(act):
            for m, (what, t) in enumerate(items):
                act.wait_ge(copied, m + 1)
                if m >= 2:
                    act.wait_ge(reduced, m - 1)
                if what == "q":
                    ins = act.activation(square[:, m % 2], q_sb[:, t], ACT.Square)
                else:
                    ins = act.activation(square[:, m % 2, 0:MH * NOPE].rearrange("p (h n) -> p h n", h=MH),
                                         kv_sb[:, t].rearrange("p (h n) -> p h n", h=MH)[:, :, 0:NOPE], ACT.Square)
                ins.then_inc(squared, 1)
            act.wait_ge(mean_ready, 1)
            act.activation(rootq[:], msq[:], ACT.Sqrt).then_inc(root_ready, 1)
            act.activation(rootk[:], msk[:], ACT.Sqrt).then_inc(root_ready, 1)

        @block.vector
        def _(dve):
            count = [0]

            def then(ins):
                count[0] += 1
                ins.then_inc(step, 1)
                dve.wait_ge(step, count[0])

            for m, (what, t) in enumerate(items):
                dve.wait_ge(product, m + 1)
                if what == "q":
                    dve.tensor_copy(q_sb[:, t], bank[:, m % 2, 0:MH * QK]).then_inc(copied, 1)
                    dve.wait_ge(squared, m + 1)
                    sq = square[:, m % 2].rearrange("p (h n) -> p h n", h=MH)
                    dve.tensor_reduce(msq[:, t, :, 0], sq[:, :, 0:NOPE], AX_X, ALU.add)
                    dve.tensor_reduce(msq[:, t, :, 1], sq[:, :, NOPE:QK], AX_X, ALU.add).then_inc(reduced, 1)
                else:
                    dve.tensor_copy(kv_sb[:, t], bank[:, m % 2]).then_inc(copied, 1)
                    dve.wait_ge(squared, m + 1)
                    dve.tensor_reduce(msk[:, t], square[:, m % 2, 0:MH * NOPE].rearrange("p (h n) -> p h n", h=MH), AX_X,
                                      ALU.add).then_inc(reduced, 1)
            dve.wait_ge(reduced, len(items))
            then(dve.tensor_scalar(msq[:, :, :, 0], msq[:, :, :, 0], 1.0 / NOPE, EPS, ALU.mult, ALU.add))
            then(dve.tensor_scalar(msq[:, :, :, 1], msq[:, :, :, 1], 1.0 / ROPE, EPS, ALU.mult, ALU.add))
            then(dve.tensor_scalar(msk[:], msk[:], 1.0 / NOPE, EPS, ALU.mult, ALU.add))
            dve.sem_inc(mean_ready, 1)
            dve.wait_ge(root_ready, 2)
            dve.reciprocal(rq[:], rootq[:])
            dve.reciprocal(rk[:], rootk[:])


def attention(k, ident, q_sb, kv_sb, rq, rk, krT, oT):
    nc, a, c = k.nc, k.a, k.c
    NK = T * P
    with ExitStack() as ctx:
        gqn, gqr, gkn = k.sb(ctx, "gqn", [P, NOPE]), k.sb(ctx, "gqr", [P, ROPE]), k.sb(ctx, "gkn", [P, NOPE])
        cos = k.sb(ctx, "cos", [P, TL, 2, 2, ROPE // 4])
        sin = k.sb(ctx, "sin", [P, TL, 2, 2, ROPE // 4])
        qn, qr = k.sb(ctx, "qn", [P, 2, TL, NOPE]), k.sb(ctx, "qr", [P, 2, TL, ROPE])
        qx, qt = k.sb(ctx, "qx", [P, TL, ROPE]), k.sb(ctx, "qt", [P, TL, ROPE])
        kn, vh = k.sb(ctx, "kn", [P, 2, T, NOPE]), k.sb(ctx, "vh", [P, 2, T, MV])
        qnT, qrT = k.sb(ctx, "qnT", [P, 2, SEQ]), k.sb(ctx, "qrT", [ROPE, 2, SEQ])
        knT = k.sb(ctx, "knT", [P, 2, NK])
        top, ntop = k.sb(ctx, "top", [P, 2]), k.sb(ctx, "ntop", [P, 2])
        total, inv = k.sb(ctx, "total", [P, 2]), k.sb(ctx, "inv", [P, 2])
        probs = k.sb(ctx, "probs", [P, 2, NK])
        probsT = k.sb(ctx, "probsT", [P, 2, T, SEQ])
        bank = k.ps(ctx, "bank", [P, 8, NC])
        score_ps = [bank[:, 0:2].rearrange("p b n -> p (b n)")[:, 0:NK], bank[:, 2:4].rearrange("p b n -> p (b n)")[:, 0:NK]]
        probT_ps = bank[:, 4:6].rearrange("p b n -> p (b n)")[:, 0:NK]
        out_ps = bank[:, 6]
        head_ps = bank[:, 7]
        rows_in = k.sem("rows_in")
        passed = k.sem("passed")
        step, staged, head_turned, head_out = k.sem("step"), k.sem("staged"), k.sem("head_turned"), k.sem("head_out")
        values_staged, first_staged, first_step = k.sem("values_staged"), k.sem("first_staged"), k.sem("first_step")
        scored, top_ready, exp_ready, probs_ready, probs_turned, probsT_ready = (
            k.sem(x) for x in ("scored", "top_ready", "exp_ready", "probs_ready", "probs_turned", "probsT_ready"))
        top_step, inv_step, attended, oT_ready = k.sem("top_step"), k.sem("inv_step"), k.sem("attended"), k.sem("oT_ready")
        block = ctx.enter_context(nc.Block())
        OPEN, R = 2, 4

        def heads(h):
            return h + 1 + OPEN

        def units(h, i):
            return TL * (h + OPEN) + i + 1

        @block.sync
        def _(sp):
            sp.dma_start(gqn[:], a["mla_q_norm"][0, 0:NOPE].partition_broadcast(P)).then_inc(rows_in, 16)
            sp.dma_start(gqr[:], a["mla_q_norm"][0, NOPE:QK].partition_broadcast(P)).then_inc(rows_in, 16)
            sp.dma_start(gkn[:], a["mla_k_norm"][0, 0:NOPE].partition_broadcast(P)).then_inc(rows_in, 16)
            sp.dma_start(cos[:], c["mla_cos"].rearrange("p (t a b n) -> p t a b n", t=TL, a=2, b=2)).then_inc(rows_in, 16)
            sp.dma_start(sin[:], c["mla_sin"].rearrange("p (t a b n) -> p t a b n", t=TL, a=2, b=2)).then_inc(rows_in, 16)

        q_h = q_sb[:].rearrange("p t (h n) -> p t h n", h=MH)
        kv_h = kv_sb[:].rearrange("p t (h n) -> p t h n", h=MH)

        def head(x, h, lo, hi):
            return x[:, :, bass.ds(h, 1), lo:hi].rearrange("p t o n -> p t (o n)")

        def stage(eng, then, h, j, scratch_free=None):
            then(eng.tensor_tensor(kn[:, j], head(kv_h, h, 0, NOPE), rk[:, :, bass.ds(h, 1)].broadcast_to([P, T, NOPE]), ALU.mult))
            then(eng.tensor_tensor(kn[:, j], kn[:, j], bc(gkn[:], [P, T, NOPE], [1]), ALU.mult))
            then(eng.tensor_tensor(qn[:, j], head(q_h, h, 0, NOPE), rq[:, :, bass.ds(h, 1), 0].broadcast_to([P, TL, NOPE]), ALU.mult))
            then(eng.tensor_tensor(qn[:, j], qn[:, j], bc(gqn[:], [P, TL, NOPE], [1]), ALU.mult))
            if scratch_free is not None:
                eng.wait_ge(scratch_free, 1)
            then(eng.tensor_tensor(qx[:], head(q_h, h, NOPE, QK), rq[:, :, bass.ds(h, 1), 1].broadcast_to([P, TL, ROPE]), ALU.mult))
            then(eng.tensor_tensor(qx[:], qx[:], bc(gqr[:], [P, TL, ROPE], [1]), ALU.mult))
            split = "p t (a b n) -> p t a b n"
            x5, d5 = qx[:].rearrange(split, a=2, b=2), qr[:, j].rearrange(split, a=2, b=2)
            eng.tensor_tensor(qt[:], qx[:], cos[:].rearrange("p t a b n -> p t (a b n)"), ALU.mult)
            eng.tensor_tensor(d5[:, :, :, 0], x5[:, :, :, 1], sin[:, :, :, 0], ALU.mult)
            then(eng.tensor_tensor(d5[:, :, :, 1], x5[:, :, :, 0], sin[:, :, :, 1], ALU.mult))
            then(eng.tensor_tensor(qr[:, j], qr[:, j], qt[:], ALU.add))

        @block.gpsimd
        def _(pool):
            pool.sem_inc(staged, OPEN + 1)
            STEPS = 9

            def stage_head(i, j, scratch_free=None):
                h = 2 * i + j
                made = [0]

                def then(ins):
                    made[0] += 1
                    ins.then_inc(step, 1)
                    pool.wait_ge(step, STEPS * (h - 1) + 1 + made[0])

                pool.wait_ge(head_turned, R * (h + 1))
                stage(pool, then, h, j, scratch_free)
                pool.sem_inc(staged, 1)
                pool.wait_ge(attended, h + 1)
                then(pool.tensor_copy(vh[:, j], head(kv_h, h, NOPE, NOPE + MV)))
                pool.sem_inc(values_staged, 1)

            pool.tensor_copy(vh[:, 0], head(kv_h, 0, NOPE, NOPE + MV)).then_inc(step, 1)
            pool.wait_ge(step, 1)
            pool.sem_inc(values_staged, 1)
            pool.wait_ge(rows_in, 80)
            stage_head(0, 1, scratch_free=first_staged)
            with pool.Fori(1, MH // 2) as i:
                stage_head(i, 0)
                stage_head(i, 1)

        @block.tensor
        def _(pe):
            pe.sem_inc(head_turned, R * OPEN)
            pe.sem_inc(attended, OPEN)
            pe.sem_inc(probs_turned, TL * OPEN)
            pe.sem_inc(scored, TL * OPEN)

            def turn_head(i, j, r, first=False):
                h = 2 * i + j
                if r == 0:
                    pe.wait_ge(*((first_staged, 1) if first else (staged, heads(h))))
                pe.wait_ge(head_out, R * (h + OPEN) + r)
                if r == 3:
                    pe.sem_inc(passed, 1)
                if r in (0, 3):
                    src, w = (qn, P) if r == 0 else (qr, ROPE)
                    for t in range(TL):
                        mm = pe.transpose(head_ps[0:w, t * P:(t + 1) * P], src[:, j, t], ident[:])
                else:
                    for n, t in enumerate(range(4) if r == 1 else range(4, T)):
                        mm = pe.transpose(head_ps[:, n * P:(n + 1) * P], kn[:, j, t], ident[:])
                mm.then_inc(head_turned, 1)

            def scores(i, j, t):
                h = 2 * i + j
                if t == 0:
                    pe.wait_ge(head_out, R * heads(h))
                pe.wait_ge(exp_ready, units(h, t) - 2)
                for lo, hi in ((0, NC), (NC, NK)):
                    pe.matmul(score_ps[t % 2][:, lo:hi], qnT[:, j, t * P:(t + 1) * P], knT[:, j, lo:hi], start=True, stop=False)
                    mm = pe.matmul(score_ps[t % 2][:, lo:hi], qrT[:, j, t * P:(t + 1) * P], krT[0:ROPE, lo:hi], start=False, stop=True)
                mm.then_inc(scored, 1)

            def turn_probs(i, j, t):
                h = 2 * i + j
                pe.wait_ge(probs_ready, units(h, t))
                pe.wait_ge(probsT_ready, units(h, t) - 1)
                for n in range(T):
                    mm = pe.transpose(probT_ps[:, n * P:(n + 1) * P], probs[:, t % 2, n * P:(n + 1) * P], ident[:])
                mm.then_inc(probs_turned, 1)

            def values(i, j):
                h = 2 * i + j
                pe.wait_ge(probsT_ready, units(h, TL - 1))
                pe.wait_ge(values_staged, h + 1)
                pe.wait_ge(oT_ready, heads(h) - 1)
                for n in range(T):
                    mm = pe.matmul(out_ps, vh[:, j, n], probsT[:, j, n], start=(n == 0), stop=(n == T - 1))
                mm.then_inc(attended, 1)

            def attend(i, j, nxt):
                if nxt:
                    turn_head(*nxt, 0)
                scores(i, j, 1)
                if nxt:
                    turn_head(*nxt, 1)
                turn_probs(i, j, 0)
                scores(i, j, 2)
                if nxt:
                    turn_head(*nxt, 2)
                turn_probs(i, j, 1)
                scores(i, j, 3)
                if nxt:
                    turn_head(*nxt, 3)
                turn_probs(i, j, 2)
                if nxt:
                    scores(*nxt, 0)
                turn_probs(i, j, 3)
                values(i, j)

            for r in range(R):
                turn_head(0, 0, r, first=True)
            scores(0, 0, 0)
            last = MH // 2 - 1
            with pe.Fori(0, last) as i:
                attend(i, 0, (i, 1))
                attend(i, 1, (i + 1, 0))
            attend(last, 0, (last, 1))
            attend(last, 1, None)

        @block.scalar
        def _(act):
            act.sem_inc(head_out, R * OPEN)
            act.sem_inc(exp_ready, TL * OPEN)
            act.sem_inc(probsT_ready, TL * OPEN)
            act.sem_inc(oT_ready, OPEN)

            def copy_head(i, j, r):
                h = 2 * i + j
                act.wait_ge(head_turned, R * (h + OPEN) + r + 1)
                if r == 0:
                    act.wait_ge(scored, units(h, TL - 1) - 2 * TL)
                    act.activation(qnT[:, j], head_ps, ACT.Copy, scale=float(QK) ** -0.5).then_inc(head_out, 1)
                elif r == 1:
                    act.activation(knT[:, j, 0:NC], head_ps, ACT.Copy).then_inc(head_out, 1)
                elif r == 2:
                    act.activation(knT[:, j, NC:NK], head_ps[:, 0:NK - NC], ACT.Copy).then_inc(head_out, 1)
                else:
                    act.activation(qrT[:, j], head_ps[0:ROPE], ACT.Copy, scale=float(QK) ** -0.5).then_inc(head_out, 1)

            def exps(i, j, t):
                h = 2 * i + j
                act.wait_ge(top_ready, units(h, t))
                act.wait_ge(probs_turned, units(h, t) - 2)
                act.activation(probs[:, t % 2], score_ps[t % 2], ACT.Exp, bias=ntop[:, t % 2:t % 2 + 1],
                               accum_out=total[:, t % 2:t % 2 + 1]).then_inc(exp_ready, 1)

            def copy_probs(i, j, t):
                h = 2 * i + j
                act.wait_ge(probs_turned, units(h, t))
                if t == 0:
                    act.wait_ge(attended, heads(h) - 2)
                act.activation(probsT[:, j, :, t * P:(t + 1) * P], probT_ps.rearrange("p (n m) -> p n m", n=T),
                               ACT.Copy).then_inc(probsT_ready, 1)

            def copy_out(i, j):
                h = 2 * i + j
                act.wait_ge(attended, heads(h))
                act.activation(oT[:, bass.ds(h, 1)].rearrange("p o n -> p (o n)"), out_ps, ACT.Copy).then_inc(oT_ready, 1)

            def attend(i, j, nxt):
                if nxt:
                    copy_head(*nxt, 0)
                exps(i, j, 1)
                if nxt:
                    copy_head(*nxt, 1)
                copy_probs(i, j, 0)
                exps(i, j, 2)
                if nxt:
                    copy_head(*nxt, 2)
                copy_probs(i, j, 1)
                exps(i, j, 3)
                if nxt:
                    copy_head(*nxt, 3)
                copy_probs(i, j, 2)
                if nxt:
                    exps(*nxt, 0)
                copy_probs(i, j, 3)
                copy_out(i, j)

            for r in range(R):
                copy_head(0, 0, r)
            exps(0, 0, 0)
            last = MH // 2 - 1
            with act.Fori(0, last) as i:
                attend(i, 0, (i, 1))
                attend(i, 1, (i + 1, 0))
            attend(last, 0, (last, 1))
            attend(last, 1, None)

        @block.vector
        def _(dve):
            dve.sem_inc(top_ready, TL * OPEN)
            dve.sem_inc(probs_ready, TL * OPEN)

            def maximum(h, t):
                n = TL * h + t
                dve.wait_ge(scored, units(h, t))
                dve.tensor_reduce(top[:, t % 2:t % 2 + 1], score_ps[t % 2], AX_X, ALU.max).then_inc(top_step, 1)
                dve.wait_ge(top_step, n + 1)
                dve.tensor_scalar(ntop[:, t % 2:t % 2 + 1], top[:, t % 2:t % 2 + 1], -1.0, None, ALU.mult).then_inc(top_ready, 1)

            def normalise(h, t):
                n = TL * h + t
                dve.wait_ge(exp_ready, units(h, t))
                dve.reciprocal(inv[:, t % 2:t % 2 + 1], total[:, t % 2:t % 2 + 1]).then_inc(inv_step, 1)
                dve.wait_ge(inv_step, n + 1)
                dve.tensor_scalar(probs[:, t % 2], probs[:, t % 2], inv[:, t % 2:t % 2 + 1], None, ALU.mult).then_inc(probs_ready, 1)

            made = [0]

            def then(ins):
                made[0] += 1
                ins.then_inc(first_step, 1)
                dve.wait_ge(first_step, made[0])

            dve.wait_ge(rows_in, 80)
            stage(dve, then, 0, 0)
            dve.sem_inc(first_staged, 1)
            with dve.Fori(0, MH) as h:
                for t in range(TL):
                    maximum(h, t)
                    normalise(h, t)


def latent_attention(k, ident, x_sb, mod_dram):
    with ExitStack() as ctx:
        oT = k.sb(ctx, "oT", [P, MH, SEQ])
        with ExitStack() as heads:
            krT = k.sb(heads, "krT", [ROPE, T * P])
            q_sb = k.sb(heads, "q", [P, TL, MH * QK])
            kv_sb = k.sb(heads, "kv", [P, T, MH * (NOPE + MV)])
            rq, rk = k.sb(heads, "rq", [P, TL, MH, 2]), k.sb(heads, "rk", [P, T, MH])
            with ExitStack() as low:
                qaT = k.sb(low, "qaT", [P, QR // P, SEQ])
                kvaT = k.sb(low, "kvaT", [P, KVR // P, T * P])
                with ExitStack() as h:
                    hT = k.sb(h, "hT", [P, KD, T * P])
                    norm_modulate(k, ident, 1, 0, k.a["norm_mix"][1], mod_dram, list(range(T)), x_sb=x_sb, hT=hT)
                    latent_down(k, ident, hT, qaT, kvaT, krT)
                latent_up(k, qaT, kvaT, q_sb, kv_sb, rq, rk)
            attention(k, ident, q_sb, kv_sb, rq, rk, krT, oT)
        project_out(k, MH, k.a["mla_w_o"][0], (1, 2), mod_dram, x_sb, list(range(TC, T)), oT=oT)



def shape_constants():
    out = {"ident": np.eye(P, dtype=np.float32)}

    def angles(rot_dim):
        axis = rot_dim // 2
        inv = (10000.0 ** (-np.arange(0, axis, 2, dtype=np.float32) / axis)).astype(np.float32)
        rows = SEQ // GRID_W
        row = np.repeat(np.arange(rows, dtype=np.float32), GRID_W)
        col = np.tile(np.arange(GRID_W, dtype=np.float32), rows)
        return row[:, None] * inv, col[:, None] * inv

    def rope(rot_dim):
        ang = np.stack(angles(rot_dim), 1).astype(np.float32)
        cos = np.repeat(np.cos(ang)[:, :, None, :], 2, axis=2)
        sin = np.sin(ang)[:, :, None, :] * np.array([-1, 1], np.float32)[None, None, :, None]

        def lay(x):
            return np.ascontiguousarray(x.reshape(TL, P, -1).transpose(1, 0, 2).reshape(P, -1).astype(np.float32))
        return lay(cos), lay(sin)

    out["ret_cos"], out["ret_sin"] = rope(DK)
    out["mla_cos"], out["mla_sin"] = rope(ROPE)
    p, x = np.arange(P)[:, None], np.arange(P)[None, :]
    fwd = np.concatenate([np.maximum(d * P + x - p, 0) for d in reversed(range(T))], 1)
    bwd = np.concatenate([np.maximum(e * P + p - x, 0) for e in range(T)], 1)
    out["ret_rel"] = np.concatenate([fwd, bwd], 1).astype(np.float32)
    out["ret_tri"] = np.concatenate([x >= p, p >= x], 1).astype(np.float32)
    g = np.arange(NG)
    out["lower"] = np.broadcast_to((g[None, :] < g[:, None]).astype(np.float32).reshape(1, -1), (P, NG * NG)).copy()
    return out


def build(nc, a, consts, out, dbg=None):
    k = Kit(nc, a, consts)
    mod_dram = nc.dram_tensor("mod", [2, 2, 6 * D], F32).ap()
    y_dram = nc.dram_tensor("y", [T * TOPK * P, D], F32).ap()
    with ExitStack() as ctx:
        ident = k.sb(ctx, "ident", [P, P])
        ident_in = k.sem("ident_in")
        with nc.Block() as block:
            @block.sync
            def _(sp):
                sp.dma_start(ident[:], consts["ident"]).then_inc(ident_in, 16)
                sp.wait_ge(ident_in, 16)
        conditioning(k, mod_dram)
        x_sb = k.sb(ctx, "x", [P, T, D])
        oT_dram = nc.dram_tensor("oT", [H, P, 4, T * P], F32).ap()
        with ExitStack() as mixer:
            hT, hT_lo = k.sb(mixer, "hT_hi", [P, KD, T * P], F32R), k.sb(mixer, "hT_lo", [P, KD, T * P], F32R)
            raw = k.sb(mixer, "w", [P, 2, KD, DK])
            ret_consts, loads = retention_constants(k, mixer)
            loads += [(raw[:, piece], retention_piece(a["ret_w_in"][0], 0, piece)) for piece in range(2)]
            norm_modulate(k, ident, 0, 0, a["norm_mix"][0], mod_dram, list(range(T)), x_sb, hT, hT_lo, x_dram=(a["ctx"], a["x"]),
                          prefetch=loads)
            retention(k, ident, hT, hT_lo, oT_dram, x_sb, raw, ret_consts)
        project_out(k, VW // P, a["ret_w_o"][0], (0, 2), mod_dram, x_sb, list(range(T)), oT_dram=oT_dram, x_dram=(a["ctx"], a["x"]))
        expert_layer(k, ident, 0, x_sb, list(range(T)), mod_dram, y_dram)
        k.recycle_semaphores()
        latent_attention(k, ident, x_sb, mod_dram)
        expert_layer(k, ident, 1, x_sb, list(range(TC, T)), mod_dram, y_dram, out)


_INS = ['x', 'c', 'ctx', 'c_ctx', 'ada_w', 'ada_b', 'norm_mix', 'norm_ffn', 'ret_w_in', 'ret_decay_f', 'ret_decay_b',
        'ret_w_o', 'mla_w_in', 'mla_q_a_norm', 'mla_w_q_b', 'mla_kv_a_norm', 'mla_w_kv_b', 'mla_q_norm', 'mla_k_norm',
        'mla_w_o', 'router_w', 'router_bias', 'exp_w_gu', 'exp_w_down', 'sh_w_gu', 'sh_w_down']


def kernel(**inputs):
    import numpy as _np
    import concourse.bacc as _bacc
    from concourse import mybir as _mybir
    from concourse.bass_utils import run_bass_kernel_spmd as _run

    nc = _bacc.Bacc("TRN2", target_bir_lowering=False, num_devices=1)
    arrays, args, consts = {}, {}, {}
    for name in _INS:
        arr = _np.ascontiguousarray(inputs[name])
        arrays[f"in_{name}"] = arr
        args[name] = nc.dram_tensor(f"in_{name}", arr.shape, _mybir.dt.from_np(arr.dtype), kind="ExternalInput").ap()
    for name, arr in shape_constants().items():
        arrays[f"const_{name}"] = arr
        consts[name] = nc.dram_tensor(f"const_{name}", arr.shape, _mybir.dt.from_np(arr.dtype), kind="ExternalInput").ap()
    out = nc.dram_tensor("out", (1, SEQ, D), _mybir.dt.float32, kind="ExternalOutput").ap()
    build(nc, args, consts, out)
    r = _run(nc, [arrays], core_ids=[0])
    return r.results[0]["out"]
```
